# Optimizing a Trainium2 kernel written in Bass

```python
import jax, jax.numpy as jnp
from jax import lax
import numpy as np
import math
import jax
import jax.numpy as jnp

D_MODEL = 1024
BATCH = 1
SEQ = 1024
DEPTH = 1

HEAD_A = 64
N_HEADS_A = 8
C_A = N_HEADS_A * HEAD_A
R_DECAY = 64
R_ICLR = 64
R_VRES = 32
GN_EPS = HEAD_A * 1e-5
C_B = 512
CONV_W = 3
C_C = 512
POOL_WINDOWS = (2, 4, 8, 16)
N_POOL_GROUPS = 4
G_C = C_C // N_POOL_GROUPS
N_BRANCH = 3
BRANCH_W = 512
NORM_EPS = 1e-6

N_RWKV_IN = 4 * C_A + R_DECAY + R_ICLR
N_CONV_IN = 4 * C_B
N_POOL_IN = 2 * C_C
N_GATE_IN = N_BRANCH * D_MODEL
N_IN = N_RWKV_IN + N_CONV_IN + N_POOL_IN + N_GATE_IN


def rms_norm(x, g):
    xf = x.astype(jnp.float32)
    y = xf * lax.rsqrt(jnp.mean(xf * xf, axis=-1, keepdims=True) + NORM_EPS)
    return (y * g.astype(jnp.float32)).astype(x.dtype)

def token_shift(p, mu):
    p_prev = jnp.pad(p, ((0, 0), (1, 0), (0, 0)))[:, :-1]
    return p + (p_prev - p) * mu

def _rwkv7_step(state, inp):
    r_t, w_t, k_t, v_t, a_t, b_t = inp
    sa = jnp.einsum('bhvk,bhk->bhv', state, a_t)
    state = (state * w_t[:, :, None, :] + sa[..., None] * b_t[:, :, None, :]
             + v_t[..., None] * k_t[:, :, None, :])
    y_t = jnp.einsum('bhvk,bhk->bhv', state, r_t)
    return state, y_t

def rwkv7_branch(p_rwkv, w0, w_up, a0, a_up, k_k, k_a, r_k, gn_w, gn_b, v_first, vres):
    bsz, slen, _ = p_rwkv.shape
    dt = p_rwkv.dtype
    f32 = jnp.float32
    r, k, v, z, wd, ad = jnp.split(
        p_rwkv, [C_A, 2 * C_A, 3 * C_A, 4 * C_A, 4 * C_A + R_DECAY], axis=-1)
    w = -jax.nn.softplus(-(w0 + jnp.tanh(wd) @ w_up).astype(f32)) - 0.5
    v_layer = v
    if vres is not None:
        vd, v0, v_up = vres
        v = v + (v_first - v) * jax.nn.sigmoid(v0 + vd @ v_up)
    a = jax.nn.sigmoid(a0 + ad @ a_up)
    heads = lambda t: t.reshape(bsz, slen, N_HEADS_A, HEAD_A).astype(f32)
    kk = heads(k * k_k)
    kk = kk / jnp.maximum(jnp.sqrt(jnp.sum(kk * kk, axis=-1, keepdims=True)), 1e-12)
    k = k * (1 + (a - 1) * k_a)
    rh, kh, vh, ah = heads(r), heads(k), heads(v), heads(a)
    decay = heads(jnp.exp(-jnp.exp(w)))
    seq_major = lambda t: jnp.transpose(t, (1, 0, 2, 3))
    state0 = jnp.zeros((bsz, N_HEADS_A, HEAD_A, HEAD_A), f32)
    _, y = lax.scan(_rwkv7_step, state0,
                    (seq_major(rh), seq_major(decay), seq_major(kh), seq_major(vh),
                     seq_major(-kk), seq_major(kk * ah)))
    y = jnp.transpose(y, (1, 0, 2, 3))
    mean = jnp.mean(y, axis=-1, keepdims=True)
    var = jnp.mean(jnp.square(y - mean), axis=-1, keepdims=True)
    y = ((y - mean) * lax.rsqrt(var + GN_EPS)).reshape(bsz, slen, C_A)
    y = y * gn_w.astype(f32) + gn_b.astype(f32)
    bonus = jnp.sum(rh * kh * r_k.astype(f32), axis=-1, keepdims=True) * vh
    y = y + bonus.reshape(bsz, slen, C_A)
    out = y.astype(dt) * jax.nn.silu(z)
    return out, v_layer

def short_conv_branch(p_conv, conv_w):
    b, c, u, z = jnp.split(p_conv, 4, axis=-1)
    cu = c * u
    y = lax.conv_general_dilated(
        cu, conv_w[:, None, :], window_strides=(1,), padding=[(CONV_W - 1, 0)],
        dimension_numbers=('NWC', 'WIO', 'NWC'), feature_group_count=C_B)
    return b * y * jax.nn.silu(z)

def pool_branch(p_pool, pool_w, pool_scale):
    u, z = jnp.split(p_pool, 2, axis=-1)
    bsz, slen, _ = u.shape
    f32 = jnp.float32
    ug = u.reshape(bsz, slen, N_POOL_GROUPS, G_C).astype(f32)
    csum = jnp.cumsum(ug, axis=1)
    t = jnp.arange(1, slen + 1, dtype=f32)
    outs = []
    for gi, win in enumerate(POOL_WINDOWS):
        cg = csum[:, :, gi]
        prev = jnp.pad(cg, ((0, 0), (win, 0), (0, 0)))[:, :slen]
        cnt = jnp.minimum(t, float(win))[None, :, None]
        outs.append((cg - prev) / cnt - ug[:, :, gi])
    pooled = jnp.stack(outs, axis=2)
    mixed = jnp.einsum('bsgc,gcd->bsgd', pooled, pool_w.astype(f32)).reshape(bsz, slen, C_C)
    return (mixed * pool_scale.astype(f32)).astype(u.dtype) * jax.nn.silu(z)

def first_inputs(seed: int = 0) -> dict:
    key = jax.random.key(seed)
    ks = iter(jax.random.split(key, 32))
    nrm = lambda shape, scale: scale * jax.random.normal(next(ks), shape, jnp.float32)
    uni = lambda shape, lo, hi: jax.random.uniform(next(ks), shape, jnp.float32, lo, hi)
    L = DEPTH
    Lv = DEPTH - 1
    return {
        'x': nrm((BATCH, SEQ, D_MODEL), 1.0),
        'pre_norm_w': 1.0 + nrm((L, D_MODEL), 0.1),
        'post_norm_w': 1.0 + nrm((L, D_MODEL), 0.1),
        'w_in': nrm((L, D_MODEL, N_IN), D_MODEL ** -0.5),
        'mu_shift': uni((L, N_RWKV_IN), 0.0, 1.0),
        'rwkv_w0': uni((L, C_A), -6.0, -1.0),
        'rwkv_w_up': nrm((L, R_DECAY, C_A), 0.1 * R_DECAY ** -0.5),
        'rwkv_a0': nrm((L, C_A), 0.1),
        'rwkv_a_up': nrm((L, R_ICLR, C_A), R_ICLR ** -0.5),
        'rwkv_k_k': 0.85 + nrm((L, C_A), 0.05),
        'rwkv_k_a': 1.0 + nrm((L, C_A), 0.05),
        'rwkv_r_k': nrm((L, N_HEADS_A, HEAD_A), 0.1),
        'rwkv_gn_w': 1.0 + nrm((L, C_A), 0.1),
        'rwkv_gn_b': nrm((L, C_A), 0.02),
        'vres_down': nrm((Lv, D_MODEL, R_VRES), D_MODEL ** -0.5),
        'vres_mu': uni((Lv, R_VRES), 0.0, 1.0),
        'vres_v0': nrm((Lv, C_A), 0.1),
        'vres_up': nrm((Lv, R_VRES, C_A), R_VRES ** -0.5),
        'conv_w': nrm((L, CONV_W, C_B), CONV_W ** -0.5),
        'pool_w': nrm((L, N_POOL_GROUPS, G_C, G_C), G_C ** -0.5),
        'pool_scale': 1.0 + nrm((L, C_C), 0.1),
        'w_branch': nrm((L, N_BRANCH, BRANCH_W, D_MODEL), BRANCH_W ** -0.5),
        'w_out': nrm((L, D_MODEL, D_MODEL), D_MODEL ** -0.5),
    }

def first_block(x, pre_norm_w, post_norm_w, w_in, mu_shift, rwkv_w0, rwkv_w_up, rwkv_a0,
              rwkv_a_up, rwkv_k_k, rwkv_k_a, rwkv_r_k, rwkv_gn_w, rwkv_gn_b, vres_down,
              vres_mu, vres_v0, vres_up, conv_w, pool_w, pool_scale, w_branch, w_out):
    bsz, slen, _ = x.shape
    v_first = None
    for l in range(DEPTH):
        h = rms_norm(x, pre_norm_w[l])
        if l == 0:
            w_cat = w_in[l]
        else:
            w_cat = jnp.concatenate([w_in[l], vres_down[l - 1]], axis=1)
        p = h @ w_cat
        p_rwkv, p_conv, p_pool, p_gate = jnp.split(
            p[..., :N_IN],
            [N_RWKV_IN, N_RWKV_IN + N_CONV_IN, N_RWKV_IN + N_CONV_IN + N_POOL_IN], axis=-1)
        p_rwkv = token_shift(p_rwkv, mu_shift[l])
        if l == 0:
            vres = None
        else:
            vres = (token_shift(p[..., N_IN:], vres_mu[l - 1]), vres_v0[l - 1], vres_up[l - 1])
        y_a, v_layer = rwkv7_branch(p_rwkv, rwkv_w0[l], rwkv_w_up[l], rwkv_a0[l], rwkv_a_up[l],
                                    rwkv_k_k[l], rwkv_k_a[l], rwkv_r_k[l], rwkv_gn_w[l],
                                    rwkv_gn_b[l], v_first, vres)
        if l == 0:
            v_first = v_layer
        y_b = short_conv_branch(p_conv, conv_w[l])
        y_c = pool_branch(p_pool, pool_w[l], pool_scale[l])
        ys = jnp.stack([y_a, y_b, y_c], axis=0)
        proj = jnp.einsum('nbsc,ncd->nbsd', ys, w_branch[l])
        gates = jax.nn.sigmoid(p_gate.reshape(bsz, slen, N_BRANCH, D_MODEL))
        merged = jnp.einsum('bsnd,nbsd->bsd', gates, proj)
        out = merged @ w_out[l]
        x = x + rms_norm(out, post_norm_w[l])
    return x


N_META = 16
CHUNK = 64
META_PAD = (-N_META) % CHUNK
N_FGROUPS = 4
FGROUP_DIM = 128
F_WIDTH = N_FGROUPS * FGROUP_DIM
N_HEADS = 8
HEAD_DK = 128
HEAD_DV = 128
QK_WIDTH = N_HEADS * HEAD_DK
V_WIDTH = N_HEADS * HEAD_DV
QKV_WIDTH = 2 * QK_WIDTH + V_WIDTH
CONV_K = 5
SPLIT_SIZES = (F_WIDTH, QKV_WIDTH, V_WIDTH, 4 * N_HEADS, D_MODEL, D_MODEL)
IN_WIDTH = sum(SPLIT_SIZES)
N_GROUPS = 8
EXPERTS_PER_GROUP = 8
N_EXPERTS = N_GROUPS * EXPERTS_PER_GROUP
TOP_K = 2
D_EXPERT = 256
EXPERT_BLOCK = 128


def rms_norm_2(x, gain):
    xf = x.astype(jnp.float32)
    y = xf * lax.rsqrt(jnp.mean(xf * xf, axis=-1, keepdims=True) + NORM_EPS)
    return (y * gain.astype(jnp.float32)).astype(x.dtype)

def l2_normalize(x):
    return x * lax.rsqrt(jnp.sum(x * x, axis=-1, keepdims=True) + NORM_EPS)

def depthwise_conv_centred(x, w):
    k = w.shape[0]
    return lax.conv_general_dilated(
        x, w[:, None, :].astype(x.dtype), window_strides=(1,),
        padding=[((k - 1) // 2, k // 2)],
        dimension_numbers=("NWC", "WIO", "NWC"),
        feature_group_count=x.shape[-1])

def gated_delta_chunked(q, k, v, g, beta):
    b, h, lp, dk = k.shape
    dv = v.shape[-1]
    nc = lp // CHUNK
    q = q.reshape(b, h, nc, CHUNK, dk)
    k = k.reshape(b, h, nc, CHUNK, dk)
    v = v.reshape(b, h, nc, CHUNK, dv)
    beta = beta.reshape(b, h, nc, CHUNK)
    g = jnp.cumsum(g.reshape(b, h, nc, CHUNK), axis=-1)
    lower = jnp.tril(jnp.ones((CHUNK, CHUNK), dtype=bool))
    strict = jnp.tril(jnp.ones((CHUNK, CHUNK), dtype=bool), -1)
    diff = g[..., :, None] - g[..., None, :]
    decay = jnp.where(lower, jnp.exp(jnp.where(lower, diff, 0.0)), 0.0)
    k_beta = k * beta[..., None]
    a_mat = jnp.where(strict, jnp.einsum("bhncd,bhnsd->bhncs", k_beta, k) * decay, 0.0)
    eye = jnp.eye(CHUNK, dtype=a_mat.dtype)
    t_mat = lax.linalg.triangular_solve(
        eye + a_mat, jnp.broadcast_to(eye, a_mat.shape),
        left_side=True, lower=True, unit_diagonal=True)
    u = jnp.einsum("bhncs,bhnsv->bhncv", t_mat, v * beta[..., None])
    w = jnp.einsum("bhncs,bhnsd->bhncd", t_mat, k_beta * jnp.exp(g)[..., None])
    qk = jnp.where(lower, jnp.einsum("bhncd,bhnsd->bhncs", q, k) * decay, 0.0)
    q_dec = q * jnp.exp(g)[..., None]
    k_dec = k * jnp.exp(g[..., -1:] - g)[..., None]
    chunk_decay = jnp.exp(g[..., -1])

    def step(state, inp):
        q_c, k_c, u_c, w_c, qk_c, dec_c = inp
        v_new = u_c - jnp.einsum("bhcd,bhdv->bhcv", w_c, state)
        o_c = (jnp.einsum("bhcd,bhdv->bhcv", q_c, state)
               + jnp.einsum("bhcs,bhsv->bhcv", qk_c, v_new))
        state = state * dec_c[..., None, None] + jnp.einsum("bhcd,bhcv->bhdv", k_c, v_new)
        return state, o_c

    xs = tuple(jnp.moveaxis(t, 2, 0) for t in (q_dec, k_dec, u, w, qk, chunk_decay))
    state0 = jnp.zeros((b, h, dk, dv), jnp.float32)
    _, o = lax.scan(step, state0, xs)
    return jnp.moveaxis(o, 0, 2).reshape(b, h, lp, dv)

def pad_to_chunks(t):
    t = jnp.pad(t, [(0, 0), (META_PAD, 0)] + [(0, 0)] * (t.ndim - 2))
    return jnp.moveaxis(t, 1, 2)

def hybrid_mixer(h, norm_g, w_in, conv_w, a_log_f, dt_bias_f, a_log_b, dt_bias_b,
                 out_norm_g, w_fourier, w_delta, w_out):
    bsz, seq_len, _ = h.shape
    hn = rms_norm_2(h, norm_g)
    proj = hn @ w_in
    points = np.cumsum(SPLIT_SIZES)[:-1].tolist()
    f_in, qkv, z, ab, gate_f, gate_d = jnp.split(proj, points, axis=-1)

    fg = f_in.reshape(bsz, seq_len, N_FGROUPS, FGROUP_DIM).astype(jnp.float32)
    f_mix = jnp.real(jnp.fft.fft2(fg, axes=(1, 3), norm="ortho")).astype(h.dtype)
    y_f = f_mix.reshape(bsz, seq_len, F_WIDTH) @ w_fourier

    qkv = jax.nn.silu(depthwise_conv_centred(qkv, conv_w))
    q, k, v = jnp.split(qkv, [QK_WIDTH, 2 * QK_WIDTH], axis=-1)
    q = l2_normalize(q.reshape(bsz, seq_len, N_HEADS, HEAD_DK).astype(jnp.float32)) * (HEAD_DK ** -0.5)
    k = l2_normalize(k.reshape(bsz, seq_len, N_HEADS, HEAD_DK).astype(jnp.float32))
    v = v.reshape(bsz, seq_len, N_HEADS, HEAD_DV).astype(jnp.float32)
    a_f, b_f, a_b, b_b = jnp.split(ab.astype(jnp.float32), 4, axis=-1)
    g_f = -jnp.exp(a_log_f.astype(jnp.float32)) * jax.nn.softplus(a_f + dt_bias_f.astype(jnp.float32))
    g_b = -jnp.exp(a_log_b.astype(jnp.float32)) * jax.nn.softplus(a_b + dt_bias_b.astype(jnp.float32))
    beta_f = jax.nn.sigmoid(b_f)
    beta_b = jax.nn.sigmoid(b_b)

    qp, kp, vp = pad_to_chunks(q), pad_to_chunks(k), pad_to_chunks(v)
    o_fwd = gated_delta_chunked(qp, kp, vp, pad_to_chunks(g_f), pad_to_chunks(beta_f))
    flip = lambda t: jnp.flip(t, axis=2)
    o_bwd = flip(gated_delta_chunked(flip(qp), flip(kp), flip(vp),
                                     flip(pad_to_chunks(g_b)), flip(pad_to_chunks(beta_b))))
    o = jnp.moveaxis(o_fwd + o_bwd, 1, 2)[:, META_PAD:]
    zf = z.reshape(bsz, seq_len, N_HEADS, HEAD_DV).astype(jnp.float32)
    o = rms_norm_2(o, out_norm_g) * jax.nn.silu(zf)
    y_d = o.reshape(bsz, seq_len, V_WIDTH).astype(h.dtype) @ w_delta

    merged = jax.nn.sigmoid(gate_f) * y_f + jax.nn.sigmoid(gate_d) * y_d
    return merged @ w_out

def hierarchical_moe(h, norm_g, w_rg, b_rg, w_re, b_re, w_gate, w_up, w_down):
    bsz, seq_len, d = h.shape
    hn = rms_norm_2(h, norm_g).reshape(-1, d)
    n_tok = hn.shape[0]
    gl = (hn @ w_rg).astype(jnp.float32) + b_rg.astype(jnp.float32)
    gp = jax.nn.softmax(gl, axis=-1)
    p_group, g_idx = lax.top_k(gp, 1)
    el = (hn @ w_re).astype(jnp.float32) + b_re.astype(jnp.float32)
    el = el.reshape(n_tok, N_GROUPS, EXPERTS_PER_GROUP)
    el_g = jnp.take_along_axis(el, g_idx[:, :, None], axis=1)[:, 0]
    ep = jax.nn.softmax(el_g, axis=-1)
    top_w, top_i = lax.top_k(ep, TOP_K)
    top_w = top_w / jnp.sum(top_w, axis=-1, keepdims=True)
    weights = p_group * top_w
    expert_idx = g_idx * EXPERTS_PER_GROUP + top_i

    n_assign = n_tok * TOP_K
    n_blocks = -(-n_assign // EXPERT_BLOCK) + N_EXPERTS
    n_slots = n_blocks * EXPERT_BLOCK
    flat_e = expert_idx.reshape(-1).astype(jnp.int32)
    flat_tok = jnp.repeat(jnp.arange(n_tok, dtype=jnp.int32), TOP_K)
    flat_w = weights.reshape(-1)
    order = jnp.argsort(flat_e, stable=True)
    e_sorted = flat_e[order]
    counts = jnp.bincount(flat_e, length=N_EXPERTS)
    padded_counts = (counts + EXPERT_BLOCK - 1) // EXPERT_BLOCK * EXPERT_BLOCK
    padded_ends = jnp.cumsum(padded_counts)
    padded_start = padded_ends - padded_counts
    start = jnp.cumsum(counts) - counts
    rank = jnp.arange(n_assign, dtype=jnp.int32) - start[e_sorted]
    dest = padded_start[e_sorted] + rank
    slot_tok = jnp.zeros((n_slots,), jnp.int32).at[dest].set(flat_tok[order])
    slot_w = jnp.zeros((n_slots,), hn.dtype).at[dest].set(flat_w[order].astype(hn.dtype))
    block_start = jnp.arange(n_blocks, dtype=jnp.int32) * EXPERT_BLOCK
    block_expert = jnp.minimum(jnp.searchsorted(padded_ends, block_start, side="right"),
                               N_EXPERTS - 1).astype(jnp.int32)
    xb = hn[slot_tok].reshape(n_blocks, EXPERT_BLOCK, d)

    def expert_block(args):
        x_blk, e = args
        return (jax.nn.silu(x_blk @ w_gate[e]) * (x_blk @ w_up[e])) @ w_down[e]

    yb = lax.map(expert_block, (xb, block_expert)).reshape(n_slots, d)
    out = jnp.zeros((n_tok, d), hn.dtype).at[slot_tok].add(yb * slot_w[:, None])
    return out.reshape(bsz, seq_len, d)

def second_inputs(seed: int = 0) -> dict:
    key = jax.random.key(seed)
    ks = jax.random.split(key, 24)
    nrm = lambda k, shape, scale: jax.random.normal(k, shape, jnp.float32) * scale
    gain = lambda k, shape: 1.0 + 0.05 * jax.random.normal(k, shape, jnp.float32)

    def a_log(k):
        return jnp.log(jax.random.uniform(k, (DEPTH, N_HEADS), jnp.float32, minval=1.0, maxval=16.0))

    def dt_bias(k):
        dt = jnp.exp(jax.random.uniform(k, (DEPTH, N_HEADS), jnp.float32,
                                        minval=math.log(1e-3), maxval=math.log(1e-1)))
        return dt + jnp.log(-jnp.expm1(-dt))

    return {
        "x": nrm(ks[0], (BATCH, SEQ, D_MODEL), 1.0),
        "meta_tokens": nrm(ks[1], (N_META, D_MODEL), 1.0),
        "norm1_g": gain(ks[2], (DEPTH, D_MODEL)),
        "w_in": nrm(ks[3], (DEPTH, D_MODEL, IN_WIDTH), D_MODEL ** -0.5),
        "conv_w": nrm(ks[4], (DEPTH, CONV_K, QKV_WIDTH), CONV_K ** -0.5),
        "a_log_fwd": a_log(ks[5]),
        "dt_bias_fwd": dt_bias(ks[6]),
        "a_log_bwd": a_log(ks[7]),
        "dt_bias_bwd": dt_bias(ks[8]),
        "out_norm_g": gain(ks[9], (DEPTH, HEAD_DV)),
        "w_fourier": nrm(ks[10], (DEPTH, F_WIDTH, D_MODEL), F_WIDTH ** -0.5),
        "w_delta": nrm(ks[11], (DEPTH, V_WIDTH, D_MODEL), V_WIDTH ** -0.5),
        "w_out": nrm(ks[12], (DEPTH, D_MODEL, D_MODEL), D_MODEL ** -0.5),
        "norm2_g": gain(ks[13], (DEPTH, D_MODEL)),
        "w_router_group": nrm(ks[14], (DEPTH, D_MODEL, N_GROUPS), D_MODEL ** -0.5),
        "b_router_group": nrm(ks[15], (DEPTH, N_GROUPS), 0.01),
        "w_router_expert": nrm(ks[16], (DEPTH, D_MODEL, N_EXPERTS), D_MODEL ** -0.5),
        "b_router_expert": nrm(ks[17], (DEPTH, N_EXPERTS), 0.01),
        "w_gate_e": nrm(ks[18], (DEPTH, N_EXPERTS, D_MODEL, D_EXPERT), D_MODEL ** -0.5),
        "w_up_e": nrm(ks[19], (DEPTH, N_EXPERTS, D_MODEL, D_EXPERT), D_MODEL ** -0.5),
        "w_down_e": nrm(ks[20], (DEPTH, N_EXPERTS, D_EXPERT, D_MODEL), D_EXPERT ** -0.5),
        "final_norm_g": gain(ks[21], (D_MODEL,)),
    }

def second_block(x, meta_tokens, norm1_g, w_in, conv_w, a_log_fwd, dt_bias_fwd, a_log_bwd,
              dt_bias_bwd, out_norm_g, w_fourier, w_delta, w_out, norm2_g, w_router_group,
              b_router_group, w_router_expert, b_router_expert, w_gate_e, w_up_e, w_down_e,
              final_norm_g):
    bsz = x.shape[0]
    meta = jnp.broadcast_to(meta_tokens[None].astype(x.dtype), (bsz, N_META, D_MODEL))
    h = jnp.concatenate([meta, x], axis=1)
    for layer in range(DEPTH):
        h = h + hybrid_mixer(h, norm1_g[layer], w_in[layer], conv_w[layer],
                             a_log_fwd[layer], dt_bias_fwd[layer], a_log_bwd[layer],
                             dt_bias_bwd[layer], out_norm_g[layer], w_fourier[layer],
                             w_delta[layer], w_out[layer])
        h = h + hierarchical_moe(h, norm2_g[layer], w_router_group[layer], b_router_group[layer],
                                 w_router_expert[layer], b_router_expert[layer],
                                 w_gate_e[layer], w_up_e[layer], w_down_e[layer])
    return rms_norm_2(h, final_norm_g)[:, N_META:]


def setup_inputs(seed=0):
    out = dict(first_inputs(seed))
    for name, value in second_inputs(seed + 1).items():
        if name != "x":
            out[name + "_2"] = value
    return out


def reference(
    x, pre_norm_w, post_norm_w, w_in, mu_shift, rwkv_w0, rwkv_w_up, rwkv_a0, rwkv_a_up,
    rwkv_k_k, rwkv_k_a, rwkv_r_k, rwkv_gn_w, rwkv_gn_b, vres_down, vres_mu, vres_v0, vres_up,
    conv_w, pool_w, pool_scale, w_branch, w_out, meta_tokens_2, norm1_g_2, w_in_2, conv_w_2,
    a_log_fwd_2, dt_bias_fwd_2, a_log_bwd_2, dt_bias_bwd_2, out_norm_g_2, w_fourier_2,
    w_delta_2, w_out_2, norm2_g_2, w_router_group_2, b_router_group_2, w_router_expert_2,
    b_router_expert_2, w_gate_e_2, w_up_e_2, w_down_e_2, final_norm_g_2,
):
    x = first_block(
        x, pre_norm_w, post_norm_w, w_in, mu_shift, rwkv_w0, rwkv_w_up, rwkv_a0, rwkv_a_up,
        rwkv_k_k, rwkv_k_a, rwkv_r_k, rwkv_gn_w, rwkv_gn_b, vres_down, vres_mu, vres_v0,
        vres_up, conv_w, pool_w, pool_scale, w_branch, w_out,
    )
    return second_block(
        x, meta_tokens_2, norm1_g_2, w_in_2, conv_w_2, a_log_fwd_2, dt_bias_fwd_2, a_log_bwd_2,
        dt_bias_bwd_2, out_norm_g_2, w_fourier_2, w_delta_2, w_out_2, norm2_g_2,
        w_router_group_2, b_router_group_2, w_router_expert_2, b_router_expert_2, w_gate_e_2,
        w_up_e_2, w_down_e_2, final_norm_g_2,
    )


_drawn_inputs = setup_inputs


def setup_inputs(seed=0):
    import zlib

    import numpy as np

    out = dict(_drawn_inputs(seed))
    spreads = {}
    factors = {'rwkv_w_up': 8.0,
     'rwkv_a0': 3.107,
     'rwkv_gn_b': 4.422,
     'a_log_bwd_2': 2.744,
     'out_norm_g_2': 3.628,
     'b_router_group_2': 17.89,
     'b_router_expert_2': 23.167}
    for name, (base, spread) in spreads.items():
        noise = np.random.default_rng([zlib.crc32(name.encode()), seed]).standard_normal(out[name].shape)
        drawn = base * np.exp(spread * noise) if base else spread * noise
        out[name] = jnp.asarray(drawn.astype(out[name].dtype))
    for name, factor in factors.items():
        out[name] = (out[name] * factor).astype(out[name].dtype)
    return out
```

```python
from contextlib import ExitStack

import numpy as np

import concourse.bass as bass
from concourse import mybir

F32 = mybir.dt.float32
I32 = mybir.dt.int32
U32 = mybir.dt.uint32
ALU = mybir.AluOpType
ACT = mybir.ActivationFunctionType
AX = mybir.AxisListType
ds = bass.ds

P = 128
D = 1024
KT = D // P
EPS = 1e-6

SEQ = 1024
N_META = 16
LEN = SEQ + N_META

C_BR = 512
CT = C_BR // P
N_RWKV_IN = 4 * C_BR + 128
N_CONV_IN = 4 * C_BR
N_POOL_IN = 2 * C_BR
N_IN = N_RWKV_IN + N_CONV_IN + N_POOL_IN + 3 * D
CONV_AT = N_RWKV_IN
POOL_AT = CONV_AT + N_CONV_IN
GATE_AT = POOL_AT + N_POOL_IN
RC = 64
RCH = SEQ // RC
DECAY = float(np.exp(-0.5))
GN_EPS = 64 * 1e-5
POOL_WINDOWS = (2, 4, 8, 16)

HEADS = 8
DK = 128
F_W = 512
QKV_AT = F_W
Z_AT = QKV_AT + 3 * HEADS * DK
AB_AT = Z_AT + HEADS * DK
GF_AT = AB_AT + 4 * HEADS
IN2 = GF_AT + 2 * D
ROWS = 104
NCH = LEN // ROWS
HD = 2 * HEADS
GROUPS = ((0, 4), (4, 4), (8, 2))

N_GRP = 8
N_EXP = 64
D_EXP = 256
BT = 64
N_BLK = (2 * LEN + N_EXP * (BT - 1)) // BT
N_BLK += N_BLK % 2
N_SLOT = N_BLK * BT
MAX_BLK = -(-LEN // BT)
N_LOG = N_GRP + N_EXP


def pieces(n):
    if n <= 512:
        return [(0, n)]
    k = -(-n // 512)
    w = -(-n // (8 * k)) * 8
    return [(a, min(w, n - a)) for a in range(0, n, w)]


class Steps:

    def __init__(self, eng, sem, base=0):
        self.eng, self.sem, self.base, self.n = eng, sem, base, 0

    def then(self, instruction):
        instruction.then_inc(self.sem, 1)
        self.n += 1
        self.eng.wait_ge(self.sem, self.base + self.n)


class Stage:

    def __init__(self, nc, ctx, name):
        self.nc, self.ctx, self.name, self.taken = nc, ctx, name, []
        ctx.callback(self.give_back)

    def give_back(self):
        self.nc.clear_and_free_semaphores(self.taken)
        self.nc.all_engine_barrier()

    def sb(self, name, shape, dt=F32):
        return self.ctx.enter_context(self.nc.sbuf_tensor(f"{self.name}_{name}_sb", shape, dt))

    def ps(self, name, shape, dt=F32):
        return self.ctx.enter_context(self.nc.psum_tensor(f"{self.name}_{name}_ps", shape, dt))

    def sem(self, name):
        self.taken.append(self.nc.alloc_semaphore(name=f"{self.name}_{name}"))
        return self.taken[-1]

    def sems(self, name, n=2):
        return [self.sem(f"{name}{k}") for k in range(n)]


def norm_project(nc, name, src, n_tok, rows, gain, w, first_pairs, peeled, second, dst, ident_d, neghalf_d):
    n_tiles = n_tok // rows
    pcs = pieces(n_tok)
    w_v = w.rearrange("(k p) n -> p k n", p=P)
    pc, pw = peeled
    sc, sp_ = second
    mid = 2 * first_pairs
    with ExitStack() as ctx:
        st = Stage(nc, ctx, name)
        hT = st.sb("hT", [P, KT, n_tok])
        ident = st.sb("ident", [P, P])
        neghalf = st.sb("neghalf", [P, 1])
        gain_sb = st.sb("gain", [P, KT])
        x_in = st.sb("x_in", [P, 2, D])
        junk = st.sb("junk", [P, D])
        ssq = st.sb("ssq", [P, 2])
        ms = st.sb("ms", [P, 2])
        rstd = st.sb("rstd", [P, 2])
        xn = st.sb("xn", [P, 2, D])
        w_sb = st.sb("w", [P, 2, KT, P])
        o_sb = st.sb("o", [P, 2, n_tok])
        bank = st.ps("bank", [P, 8, 512])

        consts = st.sem("consts_loaded")
        x_ld = st.sems("x_loaded")
        ssq_rdy = st.sem("ssq_ready")
        ms_rdy = st.sem("ms_ready")
        rstd_rdy = st.sem("rstd_ready")
        xn_rdy = st.sem("xn_ready")
        tr_done = st.sem("transposed")
        hT_rdy = st.sem("hT_ready")
        w_ld = st.sems("w_loaded")
        mm_done = st.sem("product_done")
        ev_dve = st.sem("evacuated_by_dve")
        ev_act = st.sem("evacuated_by_act")
        stored = st.sems("tile_stored")
        block = ctx.enter_context(nc.Block())

        @block.sync
        def _(sp):
            sp.dma_start(ident[:, :], ident_d).then_inc(consts, 16)
            sp.dma_start(neghalf[:, :], neghalf_d).then_inc(consts, 16)
            sp.dma_start(gain_sb[:, :], gain).then_inc(consts, 16)
            with sp.Fori(0, n_tiles // 2) as i:
                for s in range(2):
                    sp.wait_ge(xn_rdy, 2 * i + s + 1)
                    sp.dma_start(x_in[:rows, s, :], src[ds(i * (2 * rows) + s * rows, rows), :]).then_inc(x_ld[s], 16)

            def load_w(i, c, col, width):
                sp.wait_ge(mm_done, 2 * i + c + 1)
                sp.dma_start(w_sb[:, c % 2, :, 0:width], w_v[:, :, ds(col, width)]).then_inc(w_ld[c % 2], 16)

            with sp.Fori(0, first_pairs) as i:
                for s in range(2):
                    load_w(i, s, i * (2 * P) + s * P, P)
            load_w(0, mid, pc, pw)
            with sp.Fori(0, sp_) as i:
                for s in range(2):
                    load_w(i, mid + 1 + s, i * (2 * P) + (sc + s * P), P)

        @block.scalar
        def _(act):
            act.sem_inc(xn_rdy, 2)
            act.sem_inc(ev_act, 2)
            for q in stored:
                act.sem_inc(q, 16)
            act.wait_ge(consts, 48)
            with act.Fori(0, n_tiles // 2) as i:
                for s in range(2):
                    act.wait_ge(x_ld[s], i * 16 + 16)
                    act.activation(junk[:rows, :], x_in[:rows, s, :], ACT.Square,
                                   accum_out=ssq[:rows, s:s + 1]).then_inc(ssq_rdy, 1)
                    act.wait_ge(rstd_rdy, 2 * i + s + 1)
                    act.wait_ge(tr_done, 2 * i + s + 1)
                    act.activation(xn[:rows, s, :], x_in[:rows, s, :], ACT.Copy,
                                   scale=rstd[:rows, s:s + 1]).then_inc(xn_rdy, 1)

            def evacuate(i, c, row, width):
                s = c % 2
                act.wait_ge(mm_done, 2 * i + c + 3)
                act.wait_ge(stored[s], i * 16 + (c // 2 + 1) * 16)
                for n, (a, m) in enumerate(pcs):
                    if n:
                        last = act.activation(o_sb[:width, s, a:a + m], bank[:width, 4 * s + n, 0:m], ACT.Copy)
                last.then_inc(ev_act, 1)
                act.wait_ge(ev_act, 2 * i + c + 3)
                act.wait_ge(ev_dve, 2 * i + c + 3)
                act.dma_start(dst[ds(row, width), :], o_sb[:width, s, :]).then_inc(stored[s], 16)

            with act.Fori(0, first_pairs) as i:
                for s in range(2):
                    evacuate(i, s, i * (2 * P) + s * P, P)
            evacuate(0, mid, pc, pw)
            with act.Fori(0, sp_) as i:
                for s in range(2):
                    evacuate(i, mid + 1 + s, i * (2 * P) + (sc + s * P), P)
            total = mid + 1 + 2 * sp_
            act.wait_ge(stored[0], 16 * ((total + 1) // 2 + 1))
            act.wait_ge(stored[1], 16 * (total // 2 + 1))

        @block.vector
        def _(dve):
            dve.sem_inc(hT_rdy, 2)
            dve.sem_inc(ev_dve, 2)
            dve.wait_ge(consts, 48)
            with dve.Fori(0, n_tiles // 2) as i:
                for s in range(2):
                    dve.wait_ge(ssq_rdy, 2 * i + s + 1)
                    dve.tensor_scalar(ms[:rows, s:s + 1], ssq[:rows, s:s + 1], 1.0 / D, EPS,
                                      ALU.mult, ALU.add).then_inc(ms_rdy, 1)
                    dve.wait_ge(tr_done, 2 * i + s + 3)
                    for h in range(2):
                        last = dve.tensor_tensor(
                            hT[:, 4 * h:4 * h + 4, ds(i * (2 * rows) + s * rows, rows)],
                            bank[:, 2 * s + h, 0:4 * rows].rearrange("p (k r) -> p k r", k=4),
                            gain_sb[:, 4 * h:4 * h + 4].unsqueeze(2).broadcast_to([P, 4, rows]), ALU.mult)
                    last.then_inc(hT_rdy, 1)

            def evacuate(i, c, width):
                s = c % 2
                dve.wait_ge(mm_done, 2 * i + c + 3)
                dve.wait_ge(stored[s], i * 16 + (c // 2 + 1) * 16)
                a, m = pcs[0]
                dve.tensor_copy(o_sb[:width, s, a:a + m], bank[:width, 4 * s, 0:m]).then_inc(ev_dve, 1)

            with dve.Fori(0, first_pairs) as i:
                for s in range(2):
                    evacuate(i, s, P)
            evacuate(0, mid, pw)
            with dve.Fori(0, sp_) as i:
                for s in range(2):
                    evacuate(i, mid + 1 + s, P)

        @block.gpsimd
        def _(pool):
            pool.wait_ge(consts, 48)
            with pool.Fori(0, n_tiles // 2) as i:
                for s in range(2):
                    pool.wait_ge(ms_rdy, 2 * i + s + 1)
                    pool.tensor_tensor(rstd[:rows, s:s + 1], ms[:rows, s:s + 1], neghalf[:rows, :],
                                       ALU.pow).then_inc(rstd_rdy, 1)

        @block.tensor
        def _(pe):
            pe.sem_inc(tr_done, 2)
            pe.sem_inc(mm_done, 2)
            pe.wait_ge(consts, 48)
            with pe.Fori(0, n_tiles // 2) as i:
                for s in range(2):
                    pe.wait_ge(xn_rdy, 2 * i + s + 3)
                    pe.wait_ge(hT_rdy, 2 * i + s + 1)
                    for k in range(KT):
                        last = pe.transpose(bank[:, 2 * s + k // 4, (k % 4) * rows:(k % 4 + 1) * rows],
                                            xn[:rows, s, k * P:(k + 1) * P], ident[:rows, :rows])
                    last.then_inc(tr_done, 1)
            pe.wait_ge(hT_rdy, n_tiles + 2)

            def product(i, c, width):
                s = c % 2
                pe.wait_ge(w_ld[s], i * 16 + (c // 2 + 1) * 16)
                pe.wait_ge(ev_dve, 2 * i + c + 1)
                pe.wait_ge(ev_act, 2 * i + c + 1)
                for n, (a, m) in enumerate(pcs):
                    for k in range(KT):
                        last = pe.matmul(bank[:width, 4 * s + n, 0:m], w_sb[:, s, k, 0:width], hT[:, k, a:a + m],
                                         start=(k == 0), stop=(k == KT - 1))
                last.then_inc(mm_done, 1)

            with pe.Fori(0, first_pairs) as i:
                for s in range(2):
                    product(i, s, P)
            product(0, mid, pw)
            with pe.Fori(0, sp_) as i:
                for s in range(2):
                    product(i, mid + 1 + s, P)


def conv_branch(nc, pT, conv_w, ybT):
    with ExitStack() as ctx:
        st = Stage(nc, ctx, "conv")
        W = conv_w.shape[1]
        pad = W - 1
        inp = st.sb("bcuz", [P, 4, SEQ])
        taps_j = st.sb("taps_j", [P, W])
        cu = st.sb("cu", [P, pad + SEQ])
        y = st.sb("y", [P, 2, SEQ])
        sz = st.sb("silu_z", [P, SEQ])
        o = st.sb("o", [P, SEQ])
        ld = st.sem("loaded")
        tp = st.sem("taps_loaded")
        silu = st.sem("silu_ready")
        step = st.sem("dve_step")
        out_rdy = st.sem("out_ready")
        stored = st.sem("stored")
        block = ctx.enter_context(nc.Block())
        src = pT[CONV_AT:CONV_AT + N_CONV_IN, :].rearrange("(q r) t -> r q t", q=4)

        @block.sync
        def _(sp):
            with sp.Fori(0, CT) as j:
                sp.wait_ge(out_rdy, j + 1)
                sp.dma_start(inp[:, :, :], src[ds(j * P, P), :, :]).then_inc(ld, 16)
                sp.dma_start(taps_j[:, :], conv_w[ds(j * P, P), :]).then_inc(tp, 16)

        @block.scalar
        def _(act):
            act.sem_inc(stored, 16)
            with act.Fori(0, CT) as j:
                act.wait_ge(ld, j * 16 + 16)
                act.wait_ge(out_rdy, j + 1)
                act.activation(sz[:, :], inp[:, 3, :], ACT.Silu).then_inc(silu, 1)
                act.wait_ge(out_rdy, j + 2)
                act.dma_start(ybT[ds(j * P, P), :], o[:, :]).then_inc(stored, 16)
            act.wait_ge(stored, 16 * (CT + 1))

        @block.vector
        def _(dve):
            dve.sem_inc(out_rdy, 1)
            dve.memset(cu[:, 0:pad], 0.0).then_inc(step, 1)
            dve.wait_ge(step, 1)
            with dve.Fori(0, CT) as j:
                dve.wait_ge(ld, j * 16 + 16)
                dve.wait_ge(tp, j * 16 + 16)
                c = Steps(dve, step, j * 5 + 1)
                c.then(dve.tensor_tensor(cu[:, pad:pad + SEQ], inp[:, 1, :], inp[:, 2, :], ALU.mult))
                c.then(dve.tensor_scalar(y[:, 0, :], cu[:, 0:SEQ], taps_j[:, 0:1], None, ALU.mult))
                for k in range(1, W):
                    c.then(dve.scalar_tensor_tensor(y[:, k % 2, :], cu[:, k:k + SEQ], taps_j[:, k:k + 1],
                                                    y[:, (k - 1) % 2, :], ALU.mult, ALU.add))
                c.then(dve.tensor_tensor(y[:, W % 2, :], y[:, (W - 1) % 2, :], inp[:, 0, :], ALU.mult))
                assert c.n == 5
                dve.wait_ge(silu, j + 1)
                dve.wait_ge(stored, j * 16 + 16)
                dve.tensor_tensor(o[:, :], y[:, W % 2, :], sz[:, :], ALU.mult).then_inc(out_rdy, 1)


def pool_branch(nc, pT, pool_w, pool_scale, inv_cnt_d, ycT):
    with ExitStack() as ctx:
        st = Stage(nc, ctx, "pool")
        G = len(POOL_WINDOWS)
        pad = max(POOL_WINDOWS)
        u = st.sb("u", [P, G, pad + SEQ])
        z = st.sb("z", [P, G, SEQ])
        w = st.sb("w", [P, G, P])
        scale = st.sb("scale", [P, G])
        inv = st.sb("inv_cnt", [P, G, SEQ])
        sums = st.sb("sums", [P, 2, pad + SEQ])
        pooled = st.sb("pooled", [P, G, SEQ])
        sz = st.sb("silu_z", [P, G, SEQ])
        o = st.sb("o", [P, G, SEQ])
        ps = st.ps("mixed", [P, G, 2, 512])
        ld = st.sem("loaded")
        step = st.sem("dve_step")
        pooled_rdy = st.sem("pooled_ready")
        silu = st.sem("silu_ready")
        mixed = st.sem("mixed")
        out_rdy = st.sem("out_ready")
        stored = st.sem("stored")
        block = ctx.enter_context(nc.Block())
        n_ld = 4 + G

        @block.sync
        def _(sp):
            up = pT[POOL_AT:POOL_AT + C_BR, :].rearrange("(g p) t -> p g t", p=P)
            zp = pT[POOL_AT + C_BR:POOL_AT + 2 * C_BR, :].rearrange("(g p) t -> p g t", p=P)
            sp.dma_start(u[:, :, pad:], up).then_inc(ld, 16)
            sp.dma_start(z[:, :, :], zp).then_inc(ld, 16)
            sp.dma_start(w[:, :, :], pool_w.rearrange("g c d -> c g d")).then_inc(ld, 16)
            sp.dma_start(scale[:, :], pool_scale).then_inc(ld, 16)
            for g in range(G):
                sp.dma_start(inv[:, g, :], inv_cnt_d[g:g + 1, :].broadcast_to([P, SEQ])).then_inc(ld, 16)
            for g in range(G):
                sp.wait_ge(out_rdy, g + 1)
                sp.dma_start(ycT[g * P:(g + 1) * P, :], o[:, g, :]).then_inc(stored, 16)
            sp.wait_ge(stored, 16 * G)

        @block.scalar
        def _(act):
            act.wait_ge(ld, 16 * n_ld)
            for g in range(G):
                act.activation(sz[:, g, :], z[:, g, :], ACT.Silu).then_inc(silu, 1)

        @block.vector
        def _(dve):
            c = Steps(dve, step)
            c.then(dve.memset(u[:, :, 0:pad], 0.0))
            c.then(dve.memset(sums[:, :, 0:pad], 0.0))
            dve.wait_ge(ld, 16 * n_ld)
            for g, win in enumerate(POOL_WINDOWS):
                src, k, n = u[:, g, :], 1, 0
                while k < win:
                    c.then(dve.tensor_tensor(sums[:, n, pad:], src[:, pad:], src[:, pad - k:pad + SEQ - k], ALU.add))
                    src, k, n = sums[:, n, :], 2 * k, 1 - n
                c.then(dve.tensor_tensor(sums[:, n, pad:], src[:, pad:], inv[:, g, :], ALU.mult))
                dve.tensor_tensor(pooled[:, g, :], sums[:, n, pad:], u[:, g, pad:], ALU.subtract).then_inc(pooled_rdy, 1)
                dve.wait_ge(pooled_rdy, g + 1)
            dve.wait_ge(silu, G)
            for g in range(G):
                dve.wait_ge(mixed, g + 1)
                for h in range(2):
                    last = dve.scalar_tensor_tensor(o[:, g, h * 512:(h + 1) * 512], ps[:, g, h, :], scale[:, g:g + 1],
                                                    sz[:, g, h * 512:(h + 1) * 512], ALU.mult, ALU.mult)
                last.then_inc(out_rdy, 1)

        @block.tensor
        def _(pe):
            pe.wait_ge(ld, 16 * n_ld)
            for g in range(G):
                pe.wait_ge(pooled_rdy, g + 1)
                for h in range(2):
                    last = pe.matmul(ps[:, g, h, :], w[:, g, :], pooled[:, g, h * 512:(h + 1) * 512], start=True, stop=True)
                last.then_inc(mixed, 1)


def rwkv_prepare(nc, pT, prm, blockones_d, chunk_mask_d, ar_d, bk_d, v_d, wc_d, bonus_d, sz_d):
    columns, mu_lora, w_up, a_up = prm
    with ExitStack() as ctx:
        st = Stage(nc, ctx, "prep")
        N = SEQ
        lora = st.sb("lora", [P, 1 + N])
        lora_s = st.sb("lora_shifted", [P, N])
        lora_t = st.sb("lora_tanh", [64, N])
        mu_l = st.sb("mu_lora", [P, 1])
        raw = st.sb("rkvz", [P, 4, 1 + N])
        par = st.sb("params", [P, 9])
        W0, A0, KK_, KA_, RK_, MU = 0, 1, 2, 3, 4, 5
        up = st.sb("lora_up", [P, P])
        blk = st.sb("blockones", [P, P])
        cmask = st.sb("chunk_mask", [P, N])
        sh = st.sb("shifted", [P, 4, N])
        diff = st.sb("diff", [P, N])
        sgw = st.sb("sgw", [P, N])
        a = st.sb("a", [P, N])
        cs = st.sb("cs", [P, N])
        w_t = st.sb("w_t", [P, N])
        w_p = st.sb("w_prev", [P, N])
        w_i = st.sb("w_inv", [P, N])
        kk = st.sb("kk", [P, N])
        sq = st.sb("sq", [P, N])
        rn = st.sb("rn", [P, N])
        k2 = st.sb("k2", [P, N])
        tmp = st.sb("tmp", [P, N])
        ar = st.sb("ar", [P, RCH, 2, RC])
        bk = st.sb("bk", [P, RCH, 2, RC])
        bon = st.sb("bonus", [P, N])
        sz = st.sb("silu_z", [P, N])
        wc = st.sb("chunk_decay", [P, RCH])
        pre = st.ps("pre", [P, 2, 2, 512])
        sums = st.ps("sums", [P, 2, 2, 512])

        cst = st.sem("consts_loaded")
        ld = st.sem("inputs_loaded")
        step = st.sem("dve_step")
        free = st.sem("turn_done")
        shifted = st.sem("lora_shifted")
        tanhed = st.sem("lora_tanhed")
        pre_done = st.sem("lora_product_done")
        sig = st.sem("sigmoids_ready")
        cum = st.sem("cumsum_ready")
        exps = st.sem("exps_ready")
        sq_rdy = st.sem("square_ready")
        sum_done = st.sem("head_sum_done")
        ss_rdy = st.sem("clamped_ready")
        root = st.sem("root_ready")
        act_step = st.sem("act_step")
        z_sh = st.sem("z_shifted")
        z_rdy = st.sem("silu_ready")
        stored = st.sem("stored")
        block = ctx.enter_context(nc.Block())
        src = pT[0:4 * C_BR, :].rearrange("(q r) t -> r q t", q=4)
        n_par = 4

        @block.sync
        def _(sp):
            sp.dma_start(blk[:, :], blockones_d).then_inc(cst, 16)
            sp.dma_start(cmask[:, :], chunk_mask_d.broadcast_to([P, N])).then_inc(cst, 16)
            sp.dma_start(lora[:, 1:], pT[4 * C_BR:N_RWKV_IN, :]).then_inc(cst, 16)
            sp.dma_start(mu_l[:, :], mu_lora).then_inc(cst, 16)
            with sp.Fori(0, CT) as j:
                sp.wait_ge(free, j + 1)
                sp.wait_ge(stored, j * 96 + 96)
                sp.dma_start(raw[:, :, 1:], src[ds(j * P, P), :, :]).then_inc(ld, 16)
                sp.dma_start(par[:, :], columns[ds(j * P, P), :]).then_inc(ld, 16)
                sp.dma_start(up[0:64, :], w_up[:, ds(j * P, P)]).then_inc(ld, 16)
                sp.dma_start(up[64:128, :], a_up[:, ds(j * P, P)]).then_inc(ld, 16)
                sp.wait_ge(free, j + 2)
                sp.dma_start(ar_d[ds(j * P, P), :, :], ar[:, :, :, :].rearrange("p c w t -> p c (w t)")).then_inc(stored, 16)
                sp.dma_start(bk_d[ds(j * P, P), :, :], bk[:, :, :, :].rearrange("p c w t -> p c (w t)")).then_inc(stored, 16)
                sp.dma_start(v_d[ds(j * P, P), :], sh[:, 2, :]).then_inc(stored, 16)
                sp.dma_start(wc_d[ds(j * P, P), :], wc[:, :]).then_inc(stored, 16)
                sp.dma_start(bonus_d[ds(j * P, P), :], bon[:, :]).then_inc(stored, 16)
                sp.dma_start(sz_d[ds(j * P, P), :], sz[:, :]).then_inc(stored, 16)
            sp.wait_ge(stored, 96 * (CT + 1))

        @block.scalar
        def _(act):
            act.sem_inc(stored, 96)
            act.wait_ge(shifted, 1)
            act.activation(lora_t[:, :], lora_s[0:64, :], ACT.Tanh).then_inc(tanhed, 1)
            with act.Fori(0, CT) as j:
                act.wait_ge(ld, j * (16 * n_par) + 16 * n_par)
                act.wait_ge(pre_done, 2 * j + 2)
                act.wait_ge(free, j + 1)
                for h in range(2):
                    act.activation(sgw[:, h * 512:(h + 1) * 512], pre[:, 0, h, :], ACT.Sigmoid, bias=par[:, W0:W0 + 1])
                for h in range(2):
                    last = act.activation(a[:, h * 512:(h + 1) * 512], pre[:, 1, h, :], ACT.Sigmoid, bias=par[:, A0:A0 + 1])
                last.then_inc(sig, 1)
                act.wait_ge(z_sh, j + 1)
                act.activation(sz[:, :], sh[:, 3, :], ACT.Silu).then_inc(z_rdy, 1)
                act.wait_ge(cum, j + 1)
                act.activation(w_t[:, :], cs[:, :], ACT.Exp, scale=-DECAY)
                act.activation(w_i[:, :], cs[:, :], ACT.Exp, scale=DECAY)
                act.activation(w_p[:, :], diff[:, :], ACT.Exp, scale=-DECAY).then_inc(exps, 1)
                act.wait_ge(ss_rdy, j + 1)
                act.activation(rn[:, :], tmp[:, :], ACT.Sqrt).then_inc(root, 1)

        @block.tensor
        def _(pe):
            pe.wait_ge(cst, 64)
            pe.wait_ge(tanhed, 1)
            with pe.Fori(0, CT) as j:
                pe.wait_ge(ld, j * (16 * n_par) + 16 * n_par)
                pe.wait_ge(free, j + 1)
                for h in range(2):
                    last = pe.matmul(pre[:, 0, h, :], up[0:64, :], lora_t[:, h * 512:(h + 1) * 512], start=True, stop=True)
                last.then_inc(pre_done, 1)
                for h in range(2):
                    last = pe.matmul(pre[:, 1, h, :], up[64:128, :], lora_s[64:128, h * 512:(h + 1) * 512], start=True, stop=True)
                last.then_inc(pre_done, 1)
                for m in range(2):
                    pe.wait_ge(sq_rdy, 2 * j + m + 1)
                    for h in range(2):
                        last = pe.matmul(sums[:, m, h, :], blk[:, :], sq[:, h * 512:(h + 1) * 512], start=True, stop=True)
                    last.then_inc(sum_done, 1)

        @block.vector
        def _(dve):
            dve.sem_inc(free, 1)
            c = Steps(dve, step)
            c.then(dve.memset(lora[:, 0:1], 0.0))
            c.then(dve.memset(raw[:, :, 0:1], 0.0))
            dve.wait_ge(cst, 64)
            c.then(dve.tensor_tensor(diff[:, :], lora[:, 0:N], lora[:, 1:], ALU.subtract))
            dve.scalar_tensor_tensor(lora_s[:, :], diff[:, :], mu_l[:, 0:1], lora[:, 1:], ALU.mult, ALU.add).then_inc(shifted, 1)
            dve.wait_ge(shifted, 1)
            PER = 18
            with dve.Fori(0, CT) as j:
                c = Steps(dve, step, j * PER + 3)
                dve.wait_ge(ld, j * (16 * n_par) + 16 * n_par)
                for q in (3, 0, 1, 2):
                    c.then(dve.tensor_tensor(diff[:, :], raw[:, q, 0:N], raw[:, q, 1:], ALU.subtract))
                    ins = dve.scalar_tensor_tensor(sh[:, q, :], diff[:, :], par[:, MU + q:MU + q + 1], raw[:, q, 1:], ALU.mult, ALU.add)
                    if q == 3:
                        ins.then_inc(z_sh, 1)
                        dve.wait_ge(z_sh, j + 1)
                    else:
                        c.then(ins)
                r, k, v = sh[:, 0, :], sh[:, 1, :], sh[:, 2, :]
                dve.wait_ge(sig, j + 1)
                c.then(dve.tensor_tensor_scan(cs[:, :], cmask[:, :], sgw[:, :], 0.0, ALU.mult, ALU.add))
                dve.tensor_tensor(diff[:, :], cs[:, :], sgw[:, :], ALU.subtract).then_inc(cum, 1)
                c.then(dve.tensor_scalar(kk[:, :], k, par[:, KK_:KK_ + 1], None, ALU.mult))
                dve.tensor_tensor(sq[:, :], kk[:, :], kk[:, :], ALU.mult).then_inc(sq_rdy, 1)
                c.then(dve.tensor_scalar(k2[:, :], a[:, :], 1.0, par[:, KA_:KA_ + 1], ALU.subtract, ALU.mult))
                c.then(dve.scalar_tensor_tensor(k2[:, :], k2[:, :], 1.0, k, ALU.add, ALU.mult))
                dve.wait_ge(sum_done, 2 * j + 1)
                for h in range(2):
                    ins = dve.tensor_scalar(tmp[:, h * 512:(h + 1) * 512], sums[:, 0, h, :], 1e-24, None, ALU.max)
                ins.then_inc(ss_rdy, 1)
                dve.scalar_tensor_tensor(sq[:, :], r, par[:, RK_:RK_ + 1], k2[:, :], ALU.mult, ALU.mult).then_inc(sq_rdy, 1)
                dve.wait_ge(root, j + 1)
                c.then(dve.reciprocal(rn[:, :], rn[:, :]))
                c.then(dve.tensor_tensor(kk[:, :], kk[:, :], rn[:, :], ALU.mult))
                dve.wait_ge(exps, j + 1)
                dve.tensor_copy(wc[:, :], w_t[:, :].rearrange("p (c t) -> p c t", t=RC)[:, :, RC - 1])
                ch = lambda t: t[:, :].rearrange("p (c t) -> p c t", t=RC)
                c.then(dve.scalar_tensor_tensor(ar[:, :, 0, :], ch(kk), -1.0, ch(w_p), ALU.mult, ALU.mult))
                c.then(dve.tensor_tensor(ar[:, :, 1, :], sh[:, 0, :].rearrange("p (c t) -> p c t", t=RC), ch(w_t), ALU.mult))
                c.then(dve.tensor_tensor(rn[:, :], kk[:, :], a[:, :], ALU.mult))
                c.then(dve.tensor_tensor(bk[:, :, 0, :], ch(rn), ch(w_i), ALU.mult))
                c.then(dve.tensor_tensor(bk[:, :, 1, :], ch(k2), ch(w_i), ALU.mult))
                dve.wait_ge(sum_done, 2 * j + 2)
                dve.wait_ge(z_rdy, j + 1)
                for h in range(2):
                    last = dve.tensor_tensor(bon[:, h * 512:(h + 1) * 512], sums[:, 1, h, :], sh[:, 2, h * 512:(h + 1) * 512], ALU.mult)
                last.then_inc(free, 1)
                assert c.n == PER, c.n


def rwkv_scan(nc, ar_d, bk_d, v_d, wc_d, ident_d, masks_d, yT_d):
    NP = CT
    ROUNDS = 5
    with ExitStack() as ctx:
        st = Stage(nc, ctx, "scan")
        ident = st.sb("ident", [P, P])
        masks = st.sb("masks", [P, 4, P])
        lower = st.sb("lower", [P, P])
        ar = st.sb("ar", [P, 2, NP, 2, P])
        bk = st.sb("bk", [P, 2, NP, 2, P])
        vb = st.sb("v", [P, 2, NP, P])
        wc = st.sb("wc", [P, NP, RCH])
        S = st.sb("S", [P, NP, P])
        gb = st.sb("gb", [P, NP, 2, P])
        gk = st.sb("gk", [P, NP, 2, P])
        tok = st.sb("tok", [P, NP, 3, P])
        n_ = st.sb("n", [P, 2, NP, P])
        nt = st.sb("nt", [P, 2, NP, P])
        pp = st.sb("p", [P, NP, P])
        rhs = st.sb("rhs", [P, NP, P])
        U = st.sb("U", [P, NP, P])
        yo = st.sb("y", [P, 2, NP, RC])
        bank = st.ps("bank", [P, 8, 512])

        cst = st.sem("consts_loaded")
        ld = st.sems("chunk_loaded")
        zero = st.sem("zeroed")
        used = st.sem("chunk_used")
        pe = st.sem("pe_step")
        dv = st.sem("dve_step")
        ac = st.sem("act_step")
        y_rdy = st.sem("y_ready")
        stored = st.sems("y_stored")
        block = ctx.enter_context(nc.Block())
        N_LD = 2 * 5
        bv = lambda b, n=P: bank[:, b, :].rearrange("p (a t) -> p a t", t=n)

        @block.sync
        def _(sp):
            sp.dma_start(ident[:, :], ident_d).then_inc(cst, 16)
            sp.dma_start(masks[:, :, :], masks_d[:, 0:4 * P].rearrange("p (a t) -> p a t", a=4)).then_inc(cst, 16)
            sp.dma_start(wc[:, :, :], wc_d.rearrange("(p c) n -> c p n", c=P)).then_inc(cst, 16)
            sp.dma_start(lower[:, :], masks_d[:, 4 * P:5 * P]).then_inc(cst, 16)
            sp.wait_ge(zero, 1)
            ar_v = ar_d.rearrange("(p c) n (w t) -> c n p w t", c=P, w=2)
            bk_v = bk_d.rearrange("(p c) n (w t) -> c n p w t", c=P, w=2)
            v_v = v_d.rearrange("(p c) (n t) -> c n p t", c=P, t=RC)
            with sp.Fori(0, RCH // 2) as i:
                for s in range(2):
                    sp.wait_ge(used, 2 * i + s + 1)
                    for x in range(2):
                        h = slice(64 * x, 64 * x + 64)
                        for dst, src in ((ar, ar_v), (bk, bk_v)):
                            for w in range(2):
                                sp.dma_start(dst[h, s, :, w, h],
                                             src[h, ds(2 * i + s, 1), :, w, :].rearrange("c n p t -> c (n p) t")).then_inc(ld[s], 16)
                        sp.dma_start(vb[h, s, :, h], v_v[h, ds(2 * i + s, 1), :, :].rearrange("c n p t -> c (n p) t")).then_inc(ld[s], 16)

        PE_N = 4 + (3 * ROUNDS - 1) + 4
        DV_0 = 4
        DV_N = DV_0 + (2 * ROUNDS - 1) + 1 + 2
        AC_N = 1 + ROUNDS + 1 + 1

        @block.tensor
        def _(t):
            t.wait_ge(cst, 64)
            t.wait_ge(zero, 1)
            with t.Fori(0, RCH // 2) as i:
                for s in range(2):
                    D0 = (2 * i + s) * DV_N
                    A0 = (2 * i + s) * AC_N
                    t.wait_ge(ld[s], i * (16 * N_LD) + 16 * N_LD)
                    t.wait_ge(used, 2 * i + s + 2)
                    for b, src in ((0, 0), (2, 1)):
                        for p in range(NP):
                            last = t.matmul(bank[:, b + p // 2, (p % 2) * 256:(p % 2) * 256 + 256], bk[:, s, p, src, :],
                                            ar[:, s, p, :, :].rearrange("c w t -> c (w t)"), start=True, stop=True)
                        last.then_inc(pe, 1)
                    for p in range(NP):
                        last = t.matmul(bv(4)[:, p, :], ar[:, s, p, 0, :], bk[:, s, p, 0, :], start=True, stop=True)
                    last.then_inc(pe, 1)
                    for m in range(3):
                        for p in range(NP):
                            src = bk[:, s, p, m, :] if m < 2 else vb[:, s, p, :]
                            last = t.transpose(bv(5 + m)[:, p, :], src, ident[:, :])
                    last.then_inc(pe, 1)
                    for r in range(1, ROUNDS + 1):
                        o, w = (r + 1) % 2, r % 2
                        t.wait_ge(dv, D0 + DV_0 + 2 * (r - 1))
                        t.wait_ge(ac, A0 + 1 + (r - 1))
                        cur = (lambda p: gb[:, p, 0, :]) if r == 1 else (lambda p: n_[:, o, p, :])
                        if r < ROUNDS:
                            for p in range(NP):
                                last = t.matmul(bv(0)[:, p, :], nt[:, o, p, :], cur(p), start=True, stop=True)
                            last.then_inc(pe, 1)
                        for p in range(NP):
                            last = t.matmul(bv(1)[:, p, :], cur(p), nt[:, o, p, :], start=True, stop=True)
                        last.then_inc(pe, 1)
                        t.wait_ge(ac, A0 + 1 + r)
                        for p in range(NP):
                            last = t.matmul(bv(2)[:, p, :], nt[:, w, p, :], pp[:, p, :], start=True, stop=True)
                        last.then_inc(pe, 1)
                    for p in range(NP):
                        t.matmul(bv(3)[:, p, :], ar[:, s, p, 0, :], S[:, p, :], start=True, stop=False)
                        last = t.matmul(bv(3)[:, p, :], gk[:, p, 0, :], tok[:, p, 2, :], start=False, stop=True)
                    last.then_inc(pe, 1)
                    t.wait_ge(dv, D0 + DV_0 + 2 * ROUNDS)
                    for p in range(NP):
                        last = t.matmul(bv(4)[:, p, :], pp[:, p, :], rhs[:, p, :], start=True, stop=True)
                    last.then_inc(pe, 1)
                    t.wait_ge(ac, A0 + 1 + ROUNDS + 1)
                    for p in range(NP):
                        o = bv(6)[:, p, :]
                        t.matmul(o, S[:, p, :], ar[:, s, p, 1, :], start=True, stop=False)
                        t.matmul(o, U[:, p, :], gb[:, p, 1, :], start=False, stop=False)
                        last = t.matmul(o, tok[:, p, 2, :], gk[:, p, 1, :], start=False, stop=True)
                    last.then_inc(pe, 1)
                    for p in range(NP):
                        o = bv(7)[:, p, :]
                        t.matmul(o, tok[:, p, 0, :], U[:, p, :], start=True, stop=False)
                        last = t.matmul(o, tok[:, p, 1, :], tok[:, p, 2, :], start=False, stop=True)
                    last.then_inc(pe, 1)

        @block.vector
        def _(v):
            for b in (ar, bk):
                v.memset(b[:, :, :, :, :].rearrange("c s p w t -> c (s p w t)"), 0.0)
            v.memset(vb[:, :, :, :].rearrange("c s p t -> c (s p t)"), 0.0)
            v.memset(S[:, :, :], 0.0)
            v.drain().then_inc(zero, 1)
            v.sem_inc(used, 2)
            v.wait_ge(cst, 64)
            with v.Fori(0, RCH // 2) as i:
                for s in range(2):
                    P0 = (2 * i + s) * PE_N
                    D0 = (2 * i + s) * DV_N
                    A0 = (2 * i + s) * AC_N
                    for m, g in ((0, gb), (2, gk)):
                        v.wait_ge(pe, P0 + 1 + m // 2)
                        for h in range(2):
                            last = v.tensor_tensor(g[:, 2 * h:2 * h + 2, :, :].rearrange("c p w t -> c (p w) t"),
                                                   bv(m + h), masks[:, :, :], ALU.mult)
                        last.then_inc(dv, 1)
                    v.wait_ge(pe, P0 + 3)
                    v.tensor_tensor(nt[:, 0, :, :], bv(4), lower[:, :].unsqueeze(1).broadcast_to([P, NP, P]),
                                    ALU.mult).then_inc(dv, 1)
                    v.wait_ge(dv, D0 + 1)
                    v.tensor_tensor(pp[:, :, :], gb[:, :, 0, :], ident[:, :].unsqueeze(1).broadcast_to([P, NP, P]),
                                    ALU.add).then_inc(dv, 1)
                    for r in range(1, ROUNDS + 1):
                        k = P0 + 4 + 3 * (r - 1)
                        if r < ROUNDS:
                            v.wait_ge(pe, k + 1)
                            v.tensor_copy(n_[:, r % 2, :, :], bv(0)).then_inc(dv, 1)
                            k += 1
                        v.wait_ge(pe, k + 2)
                        v.wait_ge(dv, D0 + DV_0 + 2 * (r - 1))
                        v.tensor_tensor(pp[:, :, :], pp[:, :, :], bv(2), ALU.add).then_inc(dv, 1)
                    k = P0 + 4 + 3 * ROUNDS - 1
                    v.wait_ge(pe, k + 1)
                    v.tensor_copy(rhs[:, :, :], bv(3)).then_inc(dv, 1)
                    v.wait_ge(pe, k + 4)
                    v.tensor_tensor(S[:, :, :], S[:, :, :], bv(7), ALU.add).then_inc(dv, 1)
                    v.wait_ge(dv, D0 + DV_N - 1)
                    v.tensor_tensor(S[:, :, :], S[:, :, :], wc[:, :, ds(2 * i + s, 1)].broadcast_to([P, NP, P]),
                                    ALU.mult).then_inc(dv, 1)
                    v.wait_ge(ac, A0 + AC_N)
                    v.wait_ge(dv, D0 + DV_N)
                    v.sem_inc(used, 1)

        @block.scalar
        def _(a):
            for q in stored:
                a.sem_inc(q, 32)
            a.wait_ge(cst, 64)
            with a.Fori(0, RCH // 2) as i:
                for s in range(2):
                    P0 = (2 * i + s) * PE_N
                    A0 = (2 * i + s) * AC_N
                    a.wait_ge(pe, P0 + 4)
                    for m in range(3):
                        last = a.activation(tok[:, :, m, :], bv(5 + m), ACT.Copy)
                    last.then_inc(ac, 1)
                    for r in range(1, ROUNDS + 1):
                        a.wait_ge(pe, P0 + 4 + 3 * (r - 1) + (2 if r < ROUNDS else 1))
                        a.activation(nt[:, r % 2, :, :], bv(1), ACT.Copy).then_inc(ac, 1)
                    k = P0 + 4 + 3 * ROUNDS - 1
                    a.wait_ge(pe, k + 2)
                    a.activation(U[:, :, :], bv(4), ACT.Copy).then_inc(ac, 1)
                    a.wait_ge(pe, k + 3)
                    a.wait_ge(stored[s], i * 32 + 32)
                    for x in range(2):
                        h = slice(64 * x, 64 * x + 64)
                        last = a.activation(yo[h, s, :, :], bv(6)[h, :, h], ACT.Copy)
                    last.then_inc(ac, 1)
                    a.wait_ge(ac, A0 + AC_N)
                    y_v = yT_d.rearrange("(p c) (n t) -> c n p t", c=P, t=RC)
                    for x in range(2):
                        h = slice(64 * x, 64 * x + 64)
                        a.dma_start(y_v[h, ds(2 * i + s, 1), :, :].rearrange("c n p t -> c (n p) t"), yo[h, s, :, :]).then_inc(stored[s], 16)
            for q in stored:
                a.wait_ge(q, 32 * (RCH // 2 + 1))


def rwkv_finish(nc, yT_d, bonus_d, sz_d, gn_w, gn_b, blockmean_d, yaT):
    with ExitStack() as ctx:
        st = Stage(nc, ctx, "fin")
        N = SEQ
        blk = st.sb("blockmean", [P, P])
        y = st.sb("y", [P, 2, N])
        bon = st.sb("bonus", [P, 2, N])
        sz = st.sb("silu_z", [P, 2, N])
        par = st.sb("par", [P, 2, CT])
        d = st.sb("d", [P, 2, N])
        sq = st.sb("sq", [P, 2, N])
        rn = st.sb("rn", [P, 2, N])
        o = st.sb("o", [P, 2, N])
        mean = st.ps("mean", [P, 2, 2, 512])
        var = st.ps("var", [P, 2, 2, 512])
        cst = st.sem("consts_loaded")
        ld = st.sems("loaded")
        mean_rdy = st.sem("mean_ready")
        d_rdy = st.sem("deviation_ready")
        sq_rdy = st.sem("square_ready")
        var_rdy = st.sem("var_ready")
        ve_rdy = st.sem("var_eps_ready")
        root = st.sem("root_ready")
        step = st.sem("dve_step")
        out_rdy = st.sem("out_ready")
        stored = st.sems("stored")
        block = ctx.enter_context(nc.Block())

        @block.sync
        def _(sp):
            sp.dma_start(blk[:, :], blockmean_d).then_inc(cst, 16)
            sp.dma_start(par[:, 0, :], gn_w).then_inc(cst, 16)
            sp.dma_start(par[:, 1, :], gn_b).then_inc(cst, 16)
            for j in range(CT):
                s, rows = j % 2, slice(j * P, (j + 1) * P)
                if j >= 2:
                    sp.wait_ge(out_rdy, j - 1)
                for dst, src in ((y, yT_d), (bon, bonus_d), (sz, sz_d)):
                    sp.dma_start(dst[:, s, :], src[rows, :]).then_inc(ld[s], 16)

        @block.tensor
        def _(pe):
            pe.wait_ge(cst, 48)
            for j in range(CT):
                s = j % 2
                pe.wait_ge(ld[s], 48 * (j // 2 + 1))
                if j >= 2:
                    pe.wait_ge(out_rdy, j - 1)
                for h in range(2):
                    last = pe.matmul(mean[:, s, h, :], blk[:, :], y[:, s, h * 512:(h + 1) * 512], start=True, stop=True)
                last.then_inc(mean_rdy, 1)
                pe.wait_ge(sq_rdy, j + 1)
                for h in range(2):
                    last = pe.matmul(var[:, s, h, :], blk[:, :], sq[:, s, h * 512:(h + 1) * 512], start=True, stop=True)
                last.then_inc(var_rdy, 1)

        @block.scalar
        def _(act):
            for j in range(CT):
                s = j % 2
                act.wait_ge(d_rdy, j + 1)
                act.activation(sq[:, s, :], d[:, s, :], ACT.Square).then_inc(sq_rdy, 1)
                act.wait_ge(ve_rdy, j + 1)
                act.activation(rn[:, s, :], rn[:, s, :], ACT.Sqrt).then_inc(root, 1)
                act.wait_ge(out_rdy, j + 1)
                act.dma_start(yaT[j * P:(j + 1) * P, :], o[:, s, :]).then_inc(stored[s], 16)
            for q in stored:
                act.wait_ge(q, 16 * (CT // 2))

        @block.vector
        def _(dve):
            dve.wait_ge(cst, 48)
            c = Steps(dve, step)
            for j in range(CT):
                s = j % 2
                dve.wait_ge(mean_rdy, j + 1)
                for h in range(2):
                    last = dve.tensor_tensor(d[:, s, h * 512:(h + 1) * 512], y[:, s, h * 512:(h + 1) * 512], mean[:, s, h, :], ALU.subtract)
                last.then_inc(d_rdy, 1)
                dve.wait_ge(var_rdy, j + 1)
                for h in range(2):
                    last = dve.tensor_scalar(rn[:, s, h * 512:(h + 1) * 512], var[:, s, h, :], GN_EPS, None, ALU.add)
                last.then_inc(ve_rdy, 1)
                dve.wait_ge(root, j + 1)
                c.then(dve.reciprocal(rn[:, s, :], rn[:, s, :]))
                c.then(dve.tensor_tensor(d[:, s, :], d[:, s, :], rn[:, s, :], ALU.mult))
                c.then(dve.tensor_scalar(d[:, s, :], d[:, s, :], par[:, 0, j:j + 1], par[:, 1, j:j + 1], ALU.mult, ALU.add))
                c.then(dve.tensor_tensor(d[:, s, :], d[:, s, :], bon[:, s, :], ALU.add))
                if j >= 2:
                    dve.wait_ge(stored[s], 16 * (j // 2))
                dve.tensor_tensor(o[:, s, :], d[:, s, :], sz[:, s, :], ALU.mult).then_inc(out_rdy, 1)


def gate_merge_out(nc, name, n_tok, rows, branches, gates, w_out, post_gain, resid_in, resid_out, neghalf_d, copy=None):
    NB = len(branches)
    pcs = pieces(n_tok)
    NPC = len(pcs)
    n_tiles = n_tok // rows
    kts = [w.shape[0] // P for w, _ in branches]
    with ExitStack() as ctx:
        st = Stage(nc, ctx, name)
        ys = st.sb("ys", [P, sum(kts), n_tok])
        wb = st.sb("wb", [P, 2, max(kts), P])
        gate = st.sb("gate", [P, 2, n_tok])
        tmp = st.sb("tmp", [P, n_tok])
        acc = st.sb("acc", [P, n_tok])
        mT = st.sb("mT", [P, KT, n_tok])
        wo = st.sb("wo", [P, KT, D])
        gain = st.sb("gain", [P, D])
        neghalf = st.sb("neghalf", [P, 1])
        stg = st.sb("stg", [P, 2, KT, rows])
        res = st.sb("res", [P, 2, D])
        ssq = st.sb("ssq", [P, 2, 2])
        ms = st.sb("ms", [P, 2])
        rstd = st.sb("rstd", [P, 2])
        junk = st.sb("junk", [P, 2, 2, 512])
        bank = st.ps("bank", [P, 8, 512])

        y_ld = st.sem("y_loaded")
        wo_ld = st.sem("w_out_loaded")
        u_ld = st.sems("unit_loaded")
        sig = st.sem("sigmoid_ready")
        prod = st.sem("product_done")
        used = st.sem("unit_used")
        step = st.sem("sum_step")
        o_step = st.sem("out_step")
        merged = st.sem("merged_tile_ready")
        staged = st.sem("staged")
        o_done = st.sem("out_product_done")
        r_ld = st.sems("resid_loaded")
        ssq_rdy = st.sem("ssq_ready")
        ms_rdy = st.sem("ms_ready")
        rstd_rdy = st.sem("rstd_ready")
        o_rdy = st.sem("out_ready")
        stored = st.sems("out_stored")
        copied = st.sem("copied")
        block = ctx.enter_context(nc.Block())
        M = 2
        UPT = M * NB
        k0 = [sum(kts[:n]) for n in range(NB)]
        units = [(m, n) for m in range(M) for n in range(NB)]
        n_wo = 2 + (post_gain is not None)

        @block.sync
        def _(sp):
            if copy:
                sp.dma_start(*copy).then_inc(copied, 16)
            for (w, yT), k, at in zip(branches, kts, k0):
                sp.dma_start(ys[:, at:at + k, :], yT.rearrange("(k p) t -> p k t", p=P)).then_inc(y_ld, 16)
            with sp.Fori(0, KT // M) as i:
                for u, (m, n) in enumerate(units):
                    sp.wait_ge(used, i * UPT + u + 1)
                    f = i * (M * P) + m * P
                    sp.dma_start(wb[:, u % 2, 0:kts[n], :],
                                 branches[n][0].rearrange("(k p) d -> p k d", p=P)[:, :, ds(f, P)]).then_inc(u_ld[u % 2], 16)
                    sp.dma_start(gate[:, u % 2, :], gates[n][ds(f, P), :]).then_inc(u_ld[u % 2], 16)
            sp.dma_start(wo[:, :, :], w_out.rearrange("(k p) d -> p k d", p=P)).then_inc(wo_ld, 16)
            sp.dma_start(neghalf[:, :], neghalf_d).then_inc(wo_ld, 16)
            if post_gain is not None:
                sp.dma_start(gain[:, :], post_gain.rearrange("(a d) -> a d", a=1).broadcast_to([P, D])).then_inc(wo_ld, 16)
            with sp.Fori(0, n_tiles // 2) as i:
                for s in range(2):
                    sp.wait_ge(stored[s], i * 16 + 16)
                    sp.dma_start(res[:rows, s, :], resid_in[ds(i * (2 * rows) + s * rows, rows), :]).then_inc(r_ld[s], 16)
            if copy:
                sp.wait_ge(copied, 16)

        @block.tensor
        def _(pe):
            pe.wait_ge(y_ld, 16 * NB)
            with pe.Fori(0, KT // M) as i:
                for u, (m, n) in enumerate(units):
                    s = u % 2
                    pe.wait_ge(u_ld[s], i * (16 * UPT) + 32 * (u // 2 + 1))
                    pe.wait_ge(used, i * UPT + u + 1)
                    for c, (a, w) in enumerate(pcs):
                        for k in range(kts[n]):
                            last = pe.matmul(bank[:, 4 * s + c, 0:w], wb[:, s, k, :], ys[:, k0[n] + k, a:a + w],
                                             start=(k == 0), stop=(k == kts[n] - 1))
                    last.then_inc(prod, 1)
            pe.wait_ge(wo_ld, 16 * n_wo)
            pe.wait_ge(used, KT // M * UPT + 2)
            with pe.Fori(0, n_tiles // 2) as i:
                for s in range(2):
                    pe.wait_ge(staged, 2 * i + s + 3)
                    pe.wait_ge(o_rdy, 2 * i + s + 1)
                    for c in range(2):
                        for k in range(KT):
                            last = pe.matmul(bank[:rows, 4 * s + c, :], stg[:, s, k, :], wo[:, k, c * 512:(c + 1) * 512],
                                             start=(k == 0), stop=(k == KT - 1))
                    last.then_inc(o_done, 1)

        @block.scalar
        def _(act):
            for q in stored:
                act.sem_inc(q, 16)
            with act.Fori(0, KT // M) as i:
                for u, (m, n) in enumerate(units):
                    s = u % 2
                    act.wait_ge(u_ld[s], i * (16 * UPT) + 32 * (u // 2 + 1))
                    act.activation(gate[:, s, :], gate[:, s, :], ACT.Sigmoid).then_inc(sig, 1)
            with act.Fori(0, n_tiles // 2) as i:
                for s in range(2):
                    if post_gain is not None:
                        act.wait_ge(o_done, 2 * i + s + 1)
                        act.wait_ge(o_rdy, 2 * i + s + 1)
                        for c in range(2):
                            last = act.activation(junk[:rows, s, c, :], bank[:rows, 4 * s + c, :], ACT.Square,
                                                  accum_out=ssq[:rows, s, c:c + 1])
                        last.then_inc(ssq_rdy, 1)
                    act.wait_ge(o_rdy, 2 * i + s + 3)
                    act.dma_start(resid_out[ds(i * (2 * rows) + s * rows, rows), :], res[:rows, s, :]).then_inc(stored[s], 16)
            for q in stored:
                act.wait_ge(q, 16 * (n_tiles // 2 + 1))

        @block.gpsimd
        def _(pool):
            pool.sem_inc(staged, 2)
            pool.wait_ge(wo_ld, 16 * n_wo)
            with pool.Fori(0, n_tiles // 2) as i:
                for s in range(2):
                    pool.wait_ge(merged, KT)
                    pool.wait_ge(o_rdy, 2 * i + s + 1)
                    pool.tensor_copy(stg[:, s, :, :], mT[:, :, ds(i * (2 * rows) + s * rows, rows)]).then_inc(staged, 1)
                    if post_gain is not None:
                        pool.wait_ge(ms_rdy, 2 * i + s + 1)
                        pool.tensor_tensor(rstd[:rows, s:s + 1], ms[:rows, s:s + 1], neghalf[:rows, :], ALU.pow).then_inc(rstd_rdy, 1)

        @block.vector
        def _(dve):
            dve.sem_inc(used, 2)
            dve.sem_inc(o_rdy, 2)
            PER = M * (NB - 2)
            with dve.Fori(0, KT // M) as i:
                c = Steps(dve, step, i * PER)
                for u, (m, n) in enumerate(units):
                    s = u % 2
                    dve.wait_ge(prod, i * UPT + u + 1)
                    dve.wait_ge(sig, i * UPT + u + 1)
                    dst = acc if n == 0 else tmp
                    for q, (a, w) in enumerate(pcs):
                        ins = dve.tensor_tensor(dst[:, a:a + w], gate[:, s, a:a + w], bank[:, 4 * s + q, 0:w], ALU.mult)
                    ins.then_inc(used, 1)
                    dve.wait_ge(used, i * UPT + u + 3)
                    if n == NB - 1:
                        dve.tensor_tensor(mT[:, ds(i * M + m, 1), :].rearrange("p a t -> p (a t)"), acc[:, :], tmp[:, :],
                                          ALU.add).then_inc(merged, 1)
                        dve.wait_ge(merged, i * M + m + 1)
                    elif n:
                        c.then(dve.tensor_tensor(acc[:, :], acc[:, :], tmp[:, :], ALU.add))
                assert c.n == PER, c.n
            dve.wait_ge(wo_ld, 16 * n_wo)
            with dve.Fori(0, n_tiles // 2) as i:
                c = Steps(dve, o_step, 4 * i)
                for s in range(2):
                    dve.wait_ge(r_ld[s], i * 16 + 16)
                    b = lambda c_: bank[:rows, 4 * s + c_, :]
                    rs = lambda c_: res[:rows, s, c_ * 512:(c_ + 1) * 512]
                    if post_gain is None:
                        dve.wait_ge(o_done, 2 * i + s + 1)
                        for c_ in range(2):
                            last = dve.tensor_tensor(rs(c_), rs(c_), b(c_), ALU.add)
                    else:
                        dve.wait_ge(ssq_rdy, 2 * i + s + 1)
                        c.then(dve.tensor_tensor(ms[:rows, s:s + 1], ssq[:rows, s, 0:1], ssq[:rows, s, 1:2], ALU.add))
                        dve.tensor_scalar(ms[:rows, s:s + 1], ms[:rows, s:s + 1], 1.0 / D, EPS, ALU.mult, ALU.add).then_inc(ms_rdy, 1)
                        dve.wait_ge(rstd_rdy, 2 * i + s + 1)
                        for c_ in range(2):
                            last = dve.scalar_tensor_tensor(tmp[:rows, c_ * 512:(c_ + 1) * 512], b(c_), rstd[:rows, s:s + 1],
                                                            gain[:rows, c_ * 512:(c_ + 1) * 512], ALU.mult, ALU.mult)
                        c.then(last)
                        last = dve.tensor_tensor(res[:rows, s, :], res[:rows, s, :], tmp[:rows, 0:D], ALU.add)
                    last.then_inc(o_rdy, 1)


class Plan:

    def __init__(self, sem, keys):
        self.sem, self.keys, self.n = sem, keys, len(keys)
        self.value = {k: i + 2 for i, k in enumerate(keys)}
        assert len(self.value) == self.n
        self.done = 0

    def begin(self, eng):
        eng.sem_inc(self.sem, 1)

    def wait_turn(self, eng, turn):
        eng.wait_ge(self.sem, turn * self.n + 1)

    def step(self, instruction, *key):
        assert self.keys[self.done % self.n] == key, (self.keys[self.done % self.n], key)
        self.done += 1
        instruction.then_inc(self.sem, 1)

    def wait(self, eng, turn, *key):
        eng.wait_ge(self.sem, turn * self.n + self.value[key])

    def wait_all(self, eng, turn, *keys):
        self.wait(eng, turn, *max(keys, key=self.value.get))


def qkv_conv(nc, p2T, taps_d, ones_d, qT_d, kT_d, vT_d):
    with ExitStack() as ctx:
        st = Stage(nc, ctx, "qkv")
        N, W = LEN, taps_d.shape[1]
        pad = W // 2
        pcs = pieces(N)
        ones = st.sb("ones", [P, P])
        x = st.sb("x", [P, 3, N + 2 * pad])
        taps = st.sb("taps", [P, 3, W])
        y = st.sb("y", [P, 3, 2, N])
        s = st.sb("s", [P, 3, N])
        sq = st.sb("sq", [P, 2, N])
        rn = st.sb("rn", [P, 2, N])
        o = st.sb("o", [P, 2, N])
        ss = st.ps("ss", [P, 2, 4, 512])
        cst = st.sem("consts_loaded")
        ld = st.sem("loaded")
        act_s = st.sem("act_done")
        dve_s = st.sem("dve_done")
        pe_s = st.sem("sums_done")
        zero = st.sem("padding_zeroed")
        stored = st.sem("stored")
        conv = [("conv", q, k) for q in range(3) for k in range(W)]
        dv = Plan(dve_s, conv + [(n, q) for q in range(2) for n in ("eps",)] +
                  [(n, q) for q in range(2) for n in ("inv", "out")])
        ac = Plan(act_s, [("silu", 0), ("square", 0), ("silu", 1), ("square", 1), ("silu", 2), ("root", 0), ("root", 1)])
        pp = Plan(pe_s, [("sum", 0), ("sum", 1)])
        block = ctx.enter_context(nc.Block())
        src = p2T[QKV_AT:Z_AT, :].rearrange("(q r) t -> r q t", q=3)
        tp = taps_d.rearrange("(q r) w -> r q w", q=3)

        @block.sync
        def _(sp):
            sp.dma_start(ones[:, :], ones_d).then_inc(cst, 16)
            with sp.Fori(0, HEADS) as h:
                dv.wait_turn(sp, h)
                sp.dma_start(x[:, :, pad:pad + N], src[ds(h * P, P), :, :]).then_inc(ld, 16)
                sp.dma_start(taps[:, :, :], tp[ds(h * P, P), :, :]).then_inc(ld, 16)

        @block.vector
        def _(v):
            dv.begin(v)
            v.memset(x[:, :, 0:pad], 0.0)
            v.memset(x[:, :, pad + N:], 0.0).then_inc(zero, 1)
            v.wait_ge(zero, 1)
            with v.Fori(0, HEADS) as h:
                v.wait_ge(ld, h * 32 + 32)
                for q in range(3):
                    for k in range(W):
                        if k:
                            dv.wait(v, h, "conv", q, k - 1)
                            dv.step(v.scalar_tensor_tensor(y[:, q, k % 2, :], x[:, q, k:k + N], taps[:, q, k:k + 1],
                                                           y[:, q, (k - 1) % 2, :], ALU.mult, ALU.add), "conv", q, k)
                        else:
                            dv.step(v.tensor_scalar(y[:, q, 0, :], x[:, q, 0:N], taps[:, q, 0:1], None, ALU.mult), "conv", q, k)
                for q in range(2):
                    pp.wait(v, h, "sum", q)
                    for c, (a, w) in enumerate(pcs):
                        last = v.tensor_scalar(rn[:, q, a:a + w], ss[:, q, c, 0:w], EPS, None, ALU.add)
                    dv.step(last, "eps", q)
                for q in range(2):
                    ac.wait(v, h, "root", q)
                    dv.step(v.reciprocal(rn[:, q, :], rn[:, q, :]), "inv", q)
                    dv.wait(v, h, "inv", q)
                    v.wait_ge(stored, h * 48 + 48)
                    dv.step(v.scalar_tensor_tensor(o[:, q, :], s[:, q, :], float(DK) ** -0.5 if q == 0 else 1.0, rn[:, q, :],
                                                   ALU.mult, ALU.mult), "out", q)

        @block.scalar
        def _(a):
            ac.begin(a)
            a.sem_inc(stored, 48)
            with a.Fori(0, HEADS) as h:
                for q in range(3):
                    dv.wait(a, h, "conv", q, W - 1)
                    if q == 2:
                        a.wait_ge(stored, h * 48 + 48)
                    ac.step(a.activation(s[:, q, :], y[:, q, (W - 1) % 2, :], ACT.Silu), "silu", q)
                    if q < 2:
                        ac.wait(a, h, "silu", q)
                        ac.step(a.activation(sq[:, q, :], s[:, q, :], ACT.Square), "square", q)
                for q in range(2):
                    dv.wait(a, h, "eps", q)
                    ac.step(a.activation(rn[:, q, :], rn[:, q, :], ACT.Sqrt), "root", q)
                ac.wait(a, h, "silu", 2)
                a.dma_start(vT_d[ds(h * P, P), :], s[:, 2, :]).then_inc(stored, 16)
                for q, dst in ((0, qT_d), (1, kT_d)):
                    dv.wait(a, h, "out", q)
                    a.dma_start(dst[ds(h * P, P), :], o[:, q, :]).then_inc(stored, 16)
            a.wait_ge(stored, HEADS * 48 + 48)

        @block.tensor
        def _(t):
            pp.begin(t)
            t.wait_ge(cst, 16)
            with t.Fori(0, HEADS) as h:
                for q in range(2):
                    ac.wait(t, h, "square", q)
                    for c, (a, w) in enumerate(pcs):
                        last = t.matmul(ss[:, q, c, 0:w], ones[:, :], sq[:, q, a:a + w], start=True, stop=True)
                    pp.step(last, "sum", q)


def delta_decays(nc, p2T, alog_d, dtb_d, dirs_d, chunk_mask_d, ident_d, gc_d, egc_d, tot_d, etot_d, sc_d):
    with ExitStack() as ctx:
        st = Stage(nc, ctx, "dec")
        N = LEN
        par = st.sb("par", [HD, 2])
        dirs = st.sb("dirs", [HD, 2])
        cmask = st.sb("cmask", [HD, N])
        ident = st.sb("ident", [P, P])
        a = st.sb("a", [HD, N])
        b = st.sb("b", [HD, N])
        x = st.sb("x", [HD, N])
        ab = st.sb("ab", [HD, N])
        ea = st.sb("ea", [HD, 1])
        g = st.sb("g", [HD, N])
        pre = st.sb("pre", [HD, N])
        suf = st.sb("suf", [HD, N])
        gc = st.sb("gc", [HD, N])
        egc = st.sb("egc", [HD, N])
        tot = st.sb("tot", [HD, NCH])
        totb = st.sb("totb", [P, HD, NCH])
        etot = st.sb("etot", [P, HD, NCH])
        tok = st.sb("tok", [ROWS, HD, 5, NCH])
        tmp = st.sb("tmp", [ROWS, HD, 2, NCH])
        ps = st.ps("tr", [ROWS, 2, 512])
        ld = st.sem("loaded")
        dv = st.sem("dve_step")
        ac = st.sem("act_step")
        pe = st.sem("transposed")
        gc_half = st.sem("half_ready")
        tt = st.sem("tot_stored")
        tb = st.sem("tot_loaded")
        stored = st.sem("stored")
        block = ctx.enter_context(nc.Block())
        rows = p2T[AB_AT:GF_AT, :].rearrange("(d w h) t -> w d h t", d=2, w=2)
        by_chunk = lambda z: z[:, :].rearrange("p (c t) -> p c t", t=ROWS)

        @block.sync
        def _(sp):
            for d in range(2):
                sp.dma_start(a[8 * d:8 * d + 8, :], rows[0, d]).then_inc(ld, 16)
                sp.dma_start(b[8 * d:8 * d + 8, :], rows[1, d]).then_inc(ld, 16)
            sp.dma_start(par[:, 0:1], alog_d).then_inc(ld, 16)
            sp.dma_start(par[:, 1:2], dtb_d).then_inc(ld, 16)
            sp.dma_start(dirs[:, :], dirs_d).then_inc(ld, 16)
            sp.dma_start(cmask[:, :], chunk_mask_d.broadcast_to([HD, N])).then_inc(ld, 16)
            sp.dma_start(ident[:, :], ident_d).then_inc(ld, 16)
            sp.wait_ge(dv, 9)
            sp.dma_start(tot_d, tot[:, :]).then_inc(tt, 16)
            sp.dma_start(gc_d, gc[:, :]).then_inc(stored, 16)
            sp.wait_ge(tt, 16)
            sp.dma_start(totb[:, :, :].rearrange("p h c -> p (h c)"),
                         tot_d.rearrange("(a h) c -> a (h c)", a=1).broadcast_to([P, HD * NCH])).then_inc(tb, 16)
            sp.wait_ge(ac, 5)
            sp.dma_start(egc_d, egc[:, :]).then_inc(stored, 16)
            sp.wait_ge(ac, 8)
            sp.dma_start(etot_d.rearrange("(a h) c -> a (h c)", a=1), etot[0:1, :, :].rearrange("p h c -> p (h c)")).then_inc(stored, 16)
            sp.wait_ge(dv, 14)
            sp.dma_start(sc_d.rearrange("h t k -> t h k"), tok[:, :, :, :].rearrange("t h k c -> t h (k c)")).then_inc(stored, 16)
            sp.wait_ge(stored, 64)

        @block.vector
        def _(v):
            c = Steps(v, dv)
            v.wait_ge(ld, 16 * 9)
            c.then(v.tensor_scalar(x[:, :], a[:, :], par[:, 1:2], None, ALU.add))
            c.then(v.scalar_tensor_tensor(ab[:, :], x[:, :], -1.0, x[:, :], ALU.mult, ALU.max))
            v.wait_ge(ac, 4)
            c.then(v.scalar_tensor_tensor(x[:, :], x[:, :], 0.0, ab[:, :], ALU.max, ALU.add))
            c.then(v.tensor_scalar(g[:, :], x[:, :], ea[:, 0:1], -1.0, ALU.mult, ALU.mult))
            c.then(v.tensor_tensor_scan(pre[:, :], cmask[:, :], g[:, :], 0.0, ALU.mult, ALU.add))
            c.then(v.tensor_copy(tot[:, :], by_chunk(pre)[:, :, ROWS - 1]))
            c.then(v.tensor_tensor(suf[:, :], g[:, :], pre[:, :], ALU.subtract))
            c.then(v.tensor_tensor(by_chunk(suf), by_chunk(suf), tot[:, :].unsqueeze(2).broadcast_to([HD, NCH, ROWS]), ALU.add))
            v.tensor_scalar(gc[:, :], pre[:, :], dirs[:, 0:1], None, ALU.mult).then_inc(gc_half, 1)
            v.wait_ge(gc_half, 1)
            c.then(v.scalar_tensor_tensor(gc[:, :], suf[:, :], dirs[:, 1:2], gc[:, :], ALU.mult, ALU.add))
            v.wait_ge(pe, 2)
            tr = lambda n: ps[:, n, 0:NCH * HD].rearrange("t (c h) -> t h c", h=HD)
            c.then(v.tensor_copy(tok[:, :, 0, :], tr(0)))
            c.then(v.tensor_copy(tok[:, :, 1, :], tr(1)))
            v.wait_ge(tb, 16)
            c.then(v.tensor_tensor(tmp[:, :, 1, :], totb[0:ROWS, :, :], tok[:, :, 0, :], ALU.subtract))
            v.tensor_scalar(tok[:, :, 2, :], tok[:, :, 1, :], -1.0, None, ALU.mult).then_inc(gc_half, 1)
            v.wait_ge(gc_half, 2)
            v.wait_ge(ac, 7)
            c.then(v.tensor_tensor(tok[:, :, 3, :], tok[:, :, 2, :], tmp[:, :, 0, :], ALU.mult))
            c.then(v.tensor_copy(tok[:, :, 4, :], tmp[:, :, 1, :]))
            assert c.n == 14

        @block.scalar
        def _(s):
            c = Steps(s, ac)
            s.wait_ge(ld, 16 * 9)
            c.then(s.activation(b[:, :], b[:, :], ACT.Sigmoid))
            c.then(s.activation(ea[:, :], par[:, 0:1], ACT.Exp))
            s.wait_ge(dv, 2)
            c.then(s.activation(ab[:, :], ab[:, :], ACT.Exp, scale=-1.0))
            c.then(s.activation(ab[:, :], ab[:, :], ACT.Ln, bias=1.0))
            s.wait_ge(dv, 9)
            c.then(s.activation(egc[:, :], gc[:, :], ACT.Exp))
            s.wait_ge(dv, 12)
            c.then(s.activation(tmp[:, :, 0, :], tok[:, :, 0, :], ACT.Exp))
            c.then(s.activation(tmp[:, :, 1, :], tmp[:, :, 1, :], ACT.Exp))
            c.then(s.activation(etot[:, :, :], totb[:, :, :], ACT.Exp))

        @block.tensor
        def _(t):
            t.wait_ge(ld, 16 * 9)
            for n, (src, q) in enumerate(((gc, (dv, 9)), (b, (ac, 1)))):
                t.wait_ge(*q)
                for c in range(NCH):
                    last = t.transpose(ps[:, n, c * HD:(c + 1) * HD], src[:, c * ROWS:(c + 1) * ROWS], ident[:HD, :HD])
                last.then_inc(pe, 1)


def delta_scan(nc, p2T, qT_d, kT_d, vT_d, gc_d, egc_d, etot_d, sc_d, dmask_d, strict_d, ident_d, ones_d, gout_d, ydT):
    ROUNDS = 6
    R = ROWS
    with ExitStack() as ctx:
        st = Stage(nc, ctx, "dlt")
        N = LEN
        pcs = pieces(N)
        NG = len(GROUPS)
        ident = st.sb("ident", [P, P])
        ones = st.sb("ones", [P, P])
        dmask = st.sb("dmask", [R, 2, R])
        strict = st.sb("strict", [R, R])
        gout = st.sb("gout", [P, 1])
        qT = st.sb("qT", [P, N])
        kT = st.sb("kT", [P, N])
        vT = st.sb("vT", [P, N])
        zT = st.sb("zT", [P, N])
        gcr = st.sb("gcr", [R, 2, N])
        qd = st.sb("qdec", [P, 2, N])
        sc = st.sb("sc", [R, 2, 5, NCH])
        GCT, BETA, NBETA, NBEG, KDEC = range(5)
        et = st.sb("etot", [P, 2, NCH])
        ktok = st.sb("ktok", [R, NCH, P])
        vtok = st.sb("vtok", [R, NCH, P])
        bv = st.sb("bv", [R, 2, NCH, P])
        kd = st.sb("kd", [R, 2, NCH, P])
        dd = st.sb("dd", [R, 2, NCH, R])
        nb = st.sb("nb", [R, 2, NCH, R])
        qk = st.sb("qk", [R, 2, NCH, R])
        qkT = st.sb("qkT", [R, 2, NCH, R])
        n_ = st.sb("n", [R, 2, 2, NCH, R])
        nt = st.sb("nt", [R, 2, 2, NCH, R])
        pp = st.sb("p", [R, 2, NCH, R])
        S = st.sb("S", [P, 2, 2, P])
        U = st.sb("U", [R, 2, 2, P])
        rh = st.sb("rh", [R, 2, P])
        oT = st.sb("oT", [P, 2, N])
        sq = st.sb("sq", [P, N])
        rn = st.sb("rn", [P, N])
        yo = st.sb("yo", [P, N])
        bank = st.ps("bank", [P, 8, 512])

        cst = st.sem("consts_loaded")
        ld = st.sem("head_loaded")
        stored = st.sem("y_stored")
        units = [(d, g) for g in range(NG) for d in range(2)]
        dirs = range(2)
        chunk = lambda k, d: k if d == 0 else NCH - 1 - k

        pe = Plan(st.sem("pe_step"), [(x, g) for x in ("ktok", "vtok") for g in range(NG)]
                  + [(x, g) for g in range(NG) for x in ("kk", "qk")]
                  + [(x, *u) for u in units for x in ("n", "qkT")]
                  + [k for r in range(1, ROUNDS + 1) for k in
                     [(x, r, *u) for u in units for x in (("N", "T") if r < ROUNDS else ("T",))] + [("P", r, *u) for u in units]]
                  + [(x, k, d) for k in range(NCH) for x in ("KS", "U", "dS", "O") for d in dirs
                     if not (x == "KS" and k == 0) and not (x == "dS" and k == NCH - 1)]
                  + [("sum",)])
        dv = Plan(st.sem("dve_step"), [("qdec",)] + [(x, d) for d in dirs for x in ("diff", "clamp")]
                  + [(x, *u) for g in range(NG) for x in ("nt", "qk") for u in ((0, g), (1, g))]
                  + [("p0", *u) for u in units]
                  + [k for r in range(1, ROUNDS + 1) for k in
                     ([("N", r, *u) for u in units] if r < ROUNDS else []) + [("P", r, *u) for u in units]]
                  + [(x, k, d) for k in range(NCH) for x in ("rhs", "S") for d in dirs
                     if not (x == "rhs" and k == 0) and not (x == "S" and k == NCH - 1)]
                  + [("osum",), ("ms",), ("inv",), ("onorm",), ("y",)])
        ac = Plan(st.sem("act_step"), [(x, g) for x in ("ktok", "vtok") for g in range(NG)]
                  + [("exp", d) for d in dirs]
                  + [(x, *u) for u in units for x in ("n", "qkT")]
                  + [("T", r, *u) for r in range(1, ROUNDS + 1) for u in units]
                  + [(x, k, d) for k in range(NCH) for x in ("U", "O") for d in dirs]
                  + [("square",), ("root",), ("silu",)])
        po = Plan(st.sem("pool_step"), [(x, d) for d in dirs for x in ("nbeta", "strict")]
                  + [(x, d) for d in dirs for x in ("kd", "bv")])
        block = ctx.enter_context(nc.Block())
        N_LD = 4 + 2 * 4

        def slot(b, g, w):
            return bank[:, b, 0:GROUPS[g][1] * w].rearrange("p (c w) -> p c w", w=w)

        def cs(g):
            return slice(GROUPS[g][0], GROUPS[g][0] + GROUPS[g][1])

        def tk(c):
            return slice(c * R, (c + 1) * R)

        @block.sync
        def _(sp):
            sp.sem_inc(stored, 16)
            for dst, src in ((ident[:, :], ident_d), (ones[:, :], ones_d), (dmask[:, :, :], dmask_d),
                             (strict[:, :], strict_d), (gout[:, :], gout_d)):
                sp.dma_start(dst, src).then_inc(cst, 16)
            with sp.Fori(0, HEADS) as h:
                dv.wait_turn(sp, h)
                for dst, src in ((kT, kT_d), (vT, vT_d), (qT, qT_d)):
                    sp.dma_start(dst[:, :], src[ds(h * P, P), :]).then_inc(ld, 16)
                for d in dirs:
                    hd = h + d * HEADS
                    sp.dma_start(gcr[:, d, :], gc_d[ds(hd, 1), :].broadcast_to([R, N])).then_inc(ld, 16)
                    sp.dma_start(sc[:, d, :, :].rearrange("t k c -> t (k c)"),
                                 sc_d[ds(hd, 1), :, :].rearrange("a t k -> (a t) k")).then_inc(ld, 16)
                    sp.dma_start(qd[:, d, :], egc_d[ds(hd, 1), :].broadcast_to([P, N])).then_inc(ld, 16)
                    sp.dma_start(et[:, d, :], etot_d[ds(hd, 1), :].broadcast_to([P, NCH])).then_inc(ld, 16)
                sp.dma_start(zT[:, :], p2T[ds(h * P + Z_AT, P), :]).then_inc(ld, 16)
                dv.wait(sp, h, "y")
                sp.dma_start(ydT[ds(h * P, P), :], yo[:, :]).then_inc(stored, 16)
            sp.wait_ge(stored, 16 * HEADS + 16)

        @block.tensor
        def _(t):
            pe.begin(t)
            t.wait_ge(cst, 80)
            with t.Fori(0, HEADS) as h:
                dv.wait_turn(t, h)
                ac.wait_turn(t, h)
                t.wait_ge(ld, h * (16 * N_LD) + 16 * N_LD)
                for m, (x, src) in enumerate((("ktok", kT), ("vtok", vT))):
                    for g in range(NG):
                        for j, c in enumerate(range(*GROUPS[g][:1], GROUPS[g][0] + GROUPS[g][1])):
                            last = t.transpose(bank[:R, 3 * m + g, j * P:(j + 1) * P], src[:, tk(c)], ident[:, :])
                        pe.step(last, x, g)
                kb = [6, 0, 2]
                for g in range(NG):
                    if g:
                        ac.wait(t, h, "ktok", NG - 1)
                        ac.wait(t, h, "vtok", 0)
                    for x, src, b in (("kk", kT, kb[g]), ("qk", qT, kb[g] + 1)):
                        for j, c in enumerate(range(GROUPS[g][0], GROUPS[g][0] + GROUPS[g][1])):
                            last = t.matmul(bank[:R, b, j * R:(j + 1) * R], src[:, tk(c)], kT[:, tk(c)], start=True, stop=True)
                        pe.step(last, x, g)
                for i, (d, g) in enumerate(units):
                    b = (4, 6)[i % 2]
                    if i < 2:
                        ac.wait(t, h, "vtok", NG - 1)
                        dv.wait_all(t, h, ("qk", 1, 0), ("qk", d, g))
                    else:
                        dv.wait_all(t, h, ("p0", *units[i - 2]), ("qk", d, g))
                        ac.wait_all(t, h, ("n", *units[i - 2]), ("qkT", *units[i - 2]))
                    for x, src, bb in (("n", nt[:, 0], b), ("qkT", qk, b + 1)):
                        for j, c in enumerate(range(GROUPS[g][0], GROUPS[g][0] + GROUPS[g][1])):
                            last = t.transpose(bank[:R, bb, j * R:(j + 1) * R], src[:, d, c, :], ident[:R, :R])
                        pe.step(last, x, d, g)
                for r in range(1, ROUNDS + 1):
                    o, w = (r - 1) % 2, r % 2
                    for i, u in enumerate(units):
                        d, g = u
                        b = 2 * (i % 3)
                        prev = (r, *units[i - 3]) if i >= 3 else (r - 1, *units[i + 3])
                        own = (r - 1, *u)
                        if r > 1:
                            dv.wait_all(t, h, *((("N",) + k) for k in (prev, own) if k[0] < ROUNDS))
                            ac.wait_all(t, h, ("T", *prev), ("T", *own))
                        elif i >= 3:
                            dv.wait(t, h, "N", *prev)
                            ac.wait(t, h, "T", *prev)
                        elif i == 0:
                            dv.wait(t, h, "p0", *units[-1])
                            ac.wait(t, h, "qkT", *units[-1])
                        cc = range(GROUPS[g][0], GROUPS[g][0] + GROUPS[g][1])
                        if r < ROUNDS:
                            for j, c in enumerate(cc):
                                last = t.matmul(bank[:R, b, j * R:(j + 1) * R], nt[:, o, d, c, :], n_[:, o, d, c, :], start=True, stop=True)
                            pe.step(last, "N", r, *u)
                        for j, c in enumerate(cc):
                            last = t.matmul(bank[:R, b + 1, j * R:(j + 1) * R], n_[:, o, d, c, :], nt[:, o, d, c, :], start=True, stop=True)
                        pe.step(last, "T", r, *u)
                    for i, u in enumerate(units):
                        d, g = u
                        b = 6 + i % 2
                        prev = (r, *units[i - 2]) if i >= 2 else (r - 1, *units[i + 4])
                        if r > 1:
                            dv.wait_all(t, h, ("P", *prev), ("P", r - 1, *u))
                        elif i >= 2:
                            dv.wait(t, h, "P", *prev)
                        ac.wait(t, h, "T", r, *u)
                        for j, c in enumerate(range(GROUPS[g][0], GROUPS[g][0] + GROUPS[g][1])):
                            last = t.matmul(bank[:R, b, j * R:(j + 1) * R], nt[:, w, d, c, :], pp[:, d, c, :], start=True, stop=True)
                        pe.step(last, "P", r, *u)
                dv.wait(t, h, "P", ROUNDS, *units[-1])
                po.wait(t, h, "bv", 1)
                for k in range(NCH):
                    for d in dirs:
                        c = chunk(k, d)
                        if k:
                            dv.wait(t, h, "S", k - 1, d)
                            pe.step(t.matmul(bank[:R, d, 0:P], kT[:, tk(c)], S[:, (k - 1) % 2, d, :], start=True, stop=True), "KS", k, d)
                    for d in dirs:
                        c = chunk(k, d)
                        if k:
                            dv.wait(t, h, "rhs", k, d)
                        pe.step(t.matmul(bank[:R, d, P:2 * P], pp[:, d, c, :], rh[:, d, :] if k else bv[:, d, c, :],
                                         start=True, stop=True), "U", k, d)
                    if k < NCH - 1:
                        for d in dirs:
                            ac.wait(t, h, "U", k, d)
                            pe.step(t.matmul(bank[:, 2 + d, 0:P], kd[:, d, chunk(k, d), :], U[:, k % 2, d, :], start=True, stop=True), "dS", k, d)
                    for d in dirs:
                        c = chunk(k, d)
                        ac.wait(t, h, "U", k, d)
                        if k:
                            t.matmul(bank[:, 4 + d, 0:R], S[:, (k - 1) % 2, d, :], qd[:, d, tk(c)], start=True, stop=False)
                        pe.step(t.matmul(bank[:, 4 + d, 0:R], U[:, k % 2, d, :], qkT[:, d, c, :], start=(k == 0), stop=True), "O", k, d)
                ac.wait(t, h, "square")
                for i, (a, w) in enumerate(pcs):
                    last = t.matmul(bank[:, 5 + i, 0:w], ones[:, :], sq[:, a:a + w], start=True, stop=True)
                pe.step(last, "sum")

        @block.vector
        def _(v):
            dv.begin(v)
            v.wait_ge(cst, 80)
            with v.Fori(0, HEADS) as h:
                v.wait_ge(ld, h * (16 * N_LD) + 16 * N_LD)
                for d in dirs:
                    last = v.tensor_tensor(qd[:, d, :], qd[:, d, :], qT[:, :], ALU.mult)
                dv.step(last, "qdec")
                for d in dirs:
                    dv.step(v.tensor_tensor(dd[:, d, :, :], sc[:, d, GCT, :].unsqueeze(2).broadcast_to([R, NCH, R]),
                                            gcr[:, d, :].rearrange("t (c s) -> t c s", s=R), ALU.subtract), "diff", d)
                    dv.wait(v, h, "diff", d)
                    dv.step(v.tensor_tensor(dd[:, d, :, :], dd[:, d, :, :], dmask[:, d, :].unsqueeze(1).broadcast_to([R, NCH, R]),
                                            ALU.min), "clamp", d)
                for g in range(NG):
                    pe.wait(v, h, "kk", g)
                    for d in dirs:
                        po.wait(v, h, "strict", d)
                        dv.step(v.tensor_tensor(nt[:, 0, d, cs(g), :], nb[:, d, cs(g), :], slot((6, 0, 2)[g], g, R)[:R], ALU.mult), "nt", d, g)
                    pe.wait(v, h, "qk", g)
                    for d in dirs:
                        ac.wait(v, h, "exp", d)
                        dv.step(v.tensor_tensor(qk[:, d, cs(g), :], dd[:, d, cs(g), :], slot((6, 0, 2)[g] + 1, g, R)[:R], ALU.mult), "qk", d, g)
                for i, (d, g) in enumerate(units):
                    pe.wait(v, h, "n", d, g)
                    ac.wait(v, h, "n", d, g)
                    dv.step(v.tensor_tensor(pp[:, d, cs(g), :], slot((4, 6)[i % 2], g, R)[:R],
                                            ident[:R, :R].unsqueeze(1).broadcast_to([R, GROUPS[g][1], R]), ALU.add), "p0", d, g)
                for r in range(1, ROUNDS + 1):
                    if r < ROUNDS:
                        for i, (d, g) in enumerate(units):
                            pe.wait(v, h, "N", r, d, g)
                            dv.step(v.tensor_copy(n_[:, r % 2, d, cs(g), :], slot(2 * (i % 3), g, R)[:R]), "N", r, d, g)
                    for i, (d, g) in enumerate(units):
                        pe.wait(v, h, "P", r, d, g)
                        dv.step(v.tensor_tensor(pp[:, d, cs(g), :], pp[:, d, cs(g), :], slot(6 + i % 2, g, R)[:R], ALU.add), "P", r, d, g)
                for k in range(NCH):
                    for d in dirs:
                        c = chunk(k, d)
                        if k:
                            pe.wait(v, h, "KS", k, d)
                            dv.step(v.scalar_tensor_tensor(rh[:, d, :], bank[:R, d, 0:P], sc[:, d, NBEG, c:c + 1], bv[:, d, c, :],
                                                           ALU.mult, ALU.add), "rhs", k, d)
                    if k < NCH - 1:
                        for d in dirs:
                            c = chunk(k, d)
                            pe.wait(v, h, "dS", k, d)
                            if k:
                                dv.step(v.scalar_tensor_tensor(S[:, k % 2, d, :], S[:, (k - 1) % 2, d, :], et[:, d, c:c + 1],
                                                               bank[:, 2 + d, 0:P], ALU.mult, ALU.add), "S", k, d)
                            else:
                                dv.step(v.tensor_copy(S[:, 0, d, :], bank[:, 2 + d, 0:P]), "S", k, d)
                for d in dirs:
                    ac.wait(v, h, "O", NCH - 1, d)
                dv.step(v.tensor_tensor(oT[:, 0, :], oT[:, 0, :], oT[:, 1, :], ALU.add), "osum")
                pe.wait(v, h, "sum")
                for i, (a, w) in enumerate(pcs):
                    last = v.tensor_scalar(rn[:, a:a + w], bank[:, 5 + i, 0:w], 1.0 / DK, EPS, ALU.mult, ALU.add)
                dv.step(last, "ms")
                ac.wait(v, h, "root")
                dv.step(v.reciprocal(rn[:, :], rn[:, :]), "inv")
                dv.wait(v, h, "inv")
                dv.step(v.tensor_tensor(rn[:, :], rn[:, :], oT[:, 0, :], ALU.mult), "onorm")
                dv.wait(v, h, "onorm")
                ac.wait(v, h, "silu")
                v.wait_ge(stored, h * 16 + 16)
                dv.step(v.scalar_tensor_tensor(yo[:, :], rn[:, :], gout[:, 0:1], zT[:, :], ALU.mult, ALU.mult), "y")

        @block.scalar
        def _(a):
            ac.begin(a)
            with a.Fori(0, HEADS) as h:
                for m, (x, dst) in enumerate((("ktok", ktok), ("vtok", vtok))):
                    for g in range(NG):
                        pe.wait(a, h, x, g)
                        ac.step(a.activation(dst[:, cs(g), :], slot(3 * m + g, g, P)[:R], ACT.Copy), x, g)
                for d in dirs:
                    dv.wait(a, h, "clamp", d)
                    ac.step(a.activation(dd[:, d, :, :], dd[:, d, :, :], ACT.Exp), "exp", d)
                for i, (d, g) in enumerate(units):
                    pe.wait(a, h, "n", d, g)
                    ac.step(a.activation(n_[:, 0, d, cs(g), :], slot((4, 6)[i % 2], g, R)[:R], ACT.Copy), "n", d, g)
                    pe.wait(a, h, "qkT", d, g)
                    ac.step(a.activation(qkT[:, d, cs(g), :], slot((5, 7)[i % 2], g, R)[:R], ACT.Copy), "qkT", d, g)
                for r in range(1, ROUNDS + 1):
                    for i, (d, g) in enumerate(units):
                        pe.wait(a, h, "T", r, d, g)
                        ac.step(a.activation(nt[:, r % 2, d, cs(g), :], slot(2 * (i % 3) + 1, g, R)[:R], ACT.Copy), "T", r, d, g)
                for k in range(NCH):
                    for d in dirs:
                        pe.wait(a, h, "U", k, d)
                        ac.step(a.activation(U[:, k % 2, d, :], bank[:R, d, P:2 * P], ACT.Copy), "U", k, d)
                    for d in dirs:
                        pe.wait(a, h, "O", k, d)
                        ac.step(a.activation(oT[:, d, tk(chunk(k, d))], bank[:, 4 + d, 0:R], ACT.Copy), "O", k, d)
                dv.wait(a, h, "osum")
                ac.step(a.activation(sq[:, :], oT[:, 0, :], ACT.Square), "square")
                dv.wait(a, h, "ms")
                ac.step(a.activation(rn[:, :], rn[:, :], ACT.Sqrt), "root")
                ac.step(a.activation(zT[:, :], zT[:, :], ACT.Silu), "silu")

        @block.gpsimd
        def _(g_):
            po.begin(g_)
            g_.wait_ge(cst, 80)
            with g_.Fori(0, HEADS) as h:
                for d in dirs:
                    ac.wait(g_, h, "exp", d)
                    po.step(g_.tensor_tensor(nb[:, d, :, :], dd[:, d, :, :], sc[:, d, NBETA, :].unsqueeze(2).broadcast_to([R, NCH, R]),
                                             ALU.mult), "nbeta", d)
                    po.wait(g_, h, "nbeta", d)
                    po.step(g_.tensor_tensor(nb[:, d, :, :], nb[:, d, :, :], strict[:, :].unsqueeze(1).broadcast_to([R, NCH, R]),
                                             ALU.mult), "strict", d)
                for d in dirs:
                    po.step(g_.tensor_tensor(kd[:, d, :, :], ktok[:, :, :], sc[:, d, KDEC, :].unsqueeze(2).broadcast_to([R, NCH, P]),
                                             ALU.mult), "kd", d)
                    po.step(g_.tensor_tensor(bv[:, d, :, :], vtok[:, :, :], sc[:, d, BETA, :].unsqueeze(2).broadcast_to([R, NCH, P]),
                                             ALU.mult), "bv", d)


def fourier(nc, p2T, chan_d, seq_d, yfT):
    with ExitStack() as ctx:
        st = Stage(nc, ctx, "dft")
        N, R = LEN, ROWS
        pcs = pieces(N)
        G = F_W // P
        chan = st.sb("chan", [P, 2 * P])
        seq = st.sb("seq", [R, 2, NCH, N])
        f = st.sb("f", [P, N])
        z = st.sb("z", [R, NCH, 2, P])
        o = st.sb("o", [P, N])
        bank = st.ps("bank", [P, 8, 512])
        cst = st.sem("consts_loaded")
        ld = st.sem("loaded")
        stored = st.sem("stored")
        pe = Plan(st.sem("pe_step"), [("z", k) for k in range(NCH // 2)] + [("y",)])
        ac = Plan(st.sem("act_step"), [("z", k) for k in range(NCH // 2)] + [("y",)])
        block = ctx.enter_context(nc.Block())

        @block.sync
        def _(sp):
            sp.sem_inc(stored, 16)
            sp.dma_start(chan[:, :], chan_d).then_inc(cst, 16)
            for m in range(2):
                sp.dma_start(seq[:, m, :, :], seq_d[m].rearrange("(c t) u -> t c u", t=R)).then_inc(cst, 16)
            with sp.Fori(0, G) as g:
                pe.wait_turn(sp, g)
                sp.dma_start(f[:, :], p2T[ds(g * P, P), :]).then_inc(ld, 16)
                ac.wait(sp, g, "y")
                sp.dma_start(yfT[ds(g * P, P), :], o[:, :]).then_inc(stored, 16)
            sp.wait_ge(stored, 16 * G + 16)

        @block.tensor
        def _(t):
            pe.begin(t)
            t.wait_ge(cst, 48)
            with t.Fori(0, G) as g:
                t.wait_ge(ld, g * 16 + 16)
                for k in range(NCH // 2):
                    for j in range(2):
                        c = 2 * k + j
                        last = t.matmul(bank[:R, k, j * 256:(j + 1) * 256], f[:, c * R:(c + 1) * R], chan[:, :], start=True, stop=True)
                    pe.step(last, "z", k)
                ac.wait_turn(t, g)
                ac.wait(t, g, "z", NCH // 2 - 1)
                for i, (a, w) in enumerate(pcs):
                    for c in range(NCH):
                        for m in range(2):
                            last = t.matmul(bank[:, 5 + i, 0:w], z[:, c, m, :], seq[:, m, c, a:a + w],
                                            start=(c == 0 and m == 0), stop=(c == NCH - 1 and m == 1))
                pe.step(last, "y")

        @block.scalar
        def _(a_):
            ac.begin(a_)
            with a_.Fori(0, G) as g:
                for k in range(NCH // 2):
                    pe.wait(a_, g, "z", k)
                    ac.step(a_.activation(z[:, 2 * k:2 * k + 2, :, :].rearrange("t c m w -> t (c m w)"), bank[:R, k, :], ACT.Copy), "z", k)
                pe.wait(a_, g, "y")
                a_.wait_ge(stored, g * 16 + 16)
                for i, (a, w) in enumerate(pcs):
                    last = a_.activation(o[:, a:a + w], bank[:, 5 + i, 0:w], ACT.Copy)
                ac.step(last, "y")


def route(nc, resid2, gain_d, w_rg, b_rg, w_re, b_re, cst_d, hn_d, slot_tok, slot_d, weight_d, table_d):
    with ExitStack() as ctx:
        st = Stage(nc, ctx, "rt")
        R, NT = ROWS, NCH
        half = NT // 2
        ident = st.sb("ident", [P, P])
        neghalf = st.sb("neghalf", [P, 1])
        gain = st.sb("gain", [P, D])
        wr = st.sb("w_router", [P, KT, N_LOG])
        bias = st.sb("bias", [P, N_LOG])
        iota = st.sb("iota", [P, N_BLK])
        steps = st.sb("block_steps", [P, MAX_BLK])
        before = st.sb("before", [P, P])
        ones = st.sb("ones", [P, P])
        tok_id = st.sb("tok_id", [R, NT])
        x_in = st.sb("x_in", [P, 2, D])
        junk = st.sb("junk", [P, D])
        ssq = st.sb("ssq", [P, 2])
        ms = st.sb("ms", [P, 2])
        rstd = st.sb("rstd", [P, 2])
        hn = st.sb("hn", [P, 2, D])
        hnT = st.sb("hnT", [P, 2, KT, R])
        gl = st.sb("gl", [R, NT, N_GRP])
        el = st.sb("el", [R, NT, N_EXP])
        g1 = st.sb("g1", [R, NT, N_GRP])
        g2 = st.sb("g2", [R, NT, N_GRP])
        gsel = st.sb("gsel", [R, NT, N_GRP])
        col = st.sb("col", [R, 8, NT])
        elm = st.sb("elm", [R, NT, N_EXP])
        e1 = st.sb("e1", [R, NT, N_EXP])
        pick = st.sb("pick", [R, 2, NT, N_EXP])
        both = st.sb("both", [R, NT, N_EXP])
        base = st.sb("base", [R, NT + 1, N_EXP])
        more = st.sb("more", [R, N_EXP, MAX_BLK])
        nblk = st.sb("nblk", [R, N_EXP])
        ends = st.sb("ends", [R, N_EXP])
        first = st.sb("first", [R, N_EXP])
        wt = st.sb("wt", [R, NT, 2])
        slot_f = st.sb("slot_f", [R, NT, 2])
        slot_i = st.sb("slot_i", [R, NT, 2], I32)
        done = st.sb("done", [1, N_BLK, N_EXP])
        tab_f = st.sb("tab_f", [1, N_BLK + 1])
        tab_i = st.sb("tab_i", [1, N_BLK + 1], I32)
        zero = st.sb("zero", [P, N_SLOT // P])
        bank = st.ps("bank", [P, 8, 512])

        cst = st.sem("consts_loaded")
        x_ld = st.sems("x_loaded")
        ssq_rdy = st.sem("ssq_ready")
        ms_rdy = st.sem("ms_ready")
        rstd_rdy = st.sem("rstd_ready")
        hn_rdy = st.sem("hn_ready")
        hn_st = st.sems("hn_stored")
        tr_done = st.sem("transposed")
        hnT_rdy = st.sem("hnT_ready")
        lg_done = st.sem("logits_done")
        lg_rdy = st.sem("logits_ready")
        zero_rdy = st.sem("zero_ready")
        zeroed = st.sem("slots_zeroed")
        dv = st.sem("dve_step")
        ac = st.sem("act_step")
        pre_done = st.sem("prefix_done")
        slots_rdy = st.sem("slots_ready")
        tab_rdy = st.sem("table_ready")
        wt_rdy = st.sem("weights_ready")
        scat = st.sem("scattered")
        stored = st.sem("stored")
        block = ctx.enter_context(nc.Block())
        row = lambda v: v.rearrange("(a d) -> a d", a=1).broadcast_to([P, v.shape[0]])
        loads = [(ident[:, :], cst_d["ident"]), (neghalf[:, :], cst_d["neghalf"]), (gain[:, :], row(gain_d)),
                 (wr[:, :, 0:N_GRP], w_rg.rearrange("(k p) n -> p k n", p=P)),
                 (wr[:, :, N_GRP:], w_re.rearrange("(k p) n -> p k n", p=P)),
                 (bias[:, 0:N_GRP], row(b_rg)), (bias[:, N_GRP:], row(b_re)),
                 (iota[:, :], cst_d["iota"].broadcast_to([P, N_BLK])), (steps[:, :], cst_d["block_steps"].broadcast_to([P, MAX_BLK])),
                 (before[:, :], cst_d["masks"][:, 0:P]), (ones[:, :], cst_d["ones"]), (tok_id[:, :], cst_d["tok_id"])]
        n_cst = 16 * len(loads)

        at = {}

        @block.sync
        def _(sp):
            for dst, src in loads:
                sp.dma_start(dst, src).then_inc(cst, 16)
            with sp.Fori(0, half) as i:
                for s in range(2):
                    sp.wait_ge(hn_rdy, 2 * i + s + 1)
                    sp.dma_start(x_in[:R, s, :], resid2[ds(i * (2 * R) + s * R, R), :]).then_inc(x_ld[s], 16)
            sp.wait_ge(zero_rdy, 1)
            sp.dma_start(slot_tok.rearrange("(p c) a -> p (c a)", p=P), zero[:, :]).then_inc(zeroed, 16)
            sp.wait_ge(slots_rdy, 1)
            sp.dma_start(slot_d.rearrange("(t r) j -> r t j", r=R), slot_i[:, :, :]).then_inc(stored, 16)
            sp.wait_ge(tab_rdy, 1)
            sp.dma_start(table_d, tab_i[:, :]).then_inc(stored, 16)
            sp.wait_ge(wt_rdy, 1)
            sp.dma_start(weight_d.rearrange("(t r) j -> r t j", r=R), wt[:, :, :]).then_inc(stored, 16)
            sp.wait_ge(stored, 48)

        @block.vector
        def _(v):
            v.sem_inc(hn_rdy, 2)
            v.sem_inc(lg_rdy, 2)
            v.memset(zero[:, :], 0.0).then_inc(zero_rdy, 1)
            v.wait_ge(cst, n_cst)
            with v.Fori(0, half) as i:
                for s in range(2):
                    v.wait_ge(ssq_rdy, 2 * i + s + 1)
                    v.tensor_scalar(ms[:R, s:s + 1], ssq[:R, s:s + 1], 1.0 / D, EPS, ALU.mult, ALU.add).then_inc(ms_rdy, 1)
                    v.wait_ge(rstd_rdy, 2 * i + s + 1)
                    v.wait_ge(hn_st[s], i * 16 + 16)
                    v.wait_ge(tr_done, 2 * i + s + 1)
                    v.scalar_tensor_tensor(hn[:R, s, :], x_in[:R, s, :], rstd[:R, s:s + 1], gain[:R, :], ALU.mult, ALU.mult).then_inc(hn_rdy, 1)
                    v.wait_ge(lg_done, 2 * i + s + 1)
                    tile = lambda z: z[:, ds(2 * i + s, 1), :].rearrange("r a e -> r (a e)")
                    v.tensor_tensor(tile(gl), bank[:R, 4 + s, 0:N_GRP], bias[:R, 0:N_GRP], ALU.add)
                    v.tensor_tensor(tile(el), bank[:R, 4 + s, N_GRP:N_LOG], bias[:R, N_GRP:], ALU.add).then_inc(lg_rdy, 1)
            v.wait_ge(lg_rdy, NT + 2)
            c = Steps(v, dv)
            over = lambda x, n: x.unsqueeze(2).broadcast_to([R, NT, n])
            ids = lambda n: iota[:R, 0:n].unsqueeze(1).broadcast_to([R, NT, n])
            reduce = lambda dst, src, op: v.tensor_reduce(dst, src, AX.X, op)
            GMAX, GSUM, M1, M2, IDX, EX, DEN, PG = range(8)
            c.then(reduce(col[:, GMAX, :], gl[:, :, :], ALU.max))
            c.then(v.tensor_tensor(g2[:, :, :], gl[:, :, :], over(col[:, GMAX, :], N_GRP), ALU.is_ge))
            c.then(v.scalar_tensor_tensor(g2[:, :, :], g2[:, :, :], -256.0, ids(N_GRP), ALU.mult, ALU.add))
            c.then(reduce(col[:, IDX, :], g2[:, :, :], ALU.min))
            c.then(v.tensor_tensor(gsel[:, :, :], g2[:, :, :], over(col[:, IDX, :], N_GRP), ALU.is_equal))
            c.then(v.tensor_tensor(g1[:, :, :], gl[:, :, :], over(col[:, GMAX, :], N_GRP), ALU.subtract))
            c.then(v.tensor_scalar(g2[:, :, :], gsel[:, :, :], -1.0, 1e30, ALU.add, ALU.mult))
            by_group = lambda z: z[:, :, :].rearrange("r t (g e) -> r (t g) e", g=N_GRP)
            spread = lambda z: z[:, :, :].rearrange("r t g -> r (t g)").unsqueeze(2).broadcast_to([R, NT * N_GRP, N_EXP // N_GRP])
            c.then(v.tensor_tensor(by_group(elm), by_group(el), spread(gsel), ALU.mult))
            c.then(v.tensor_tensor(by_group(elm), by_group(elm), spread(g2), ALU.add))
            at["shifted"] = 6
            for j, m in enumerate((M1, M2)):
                c.then(reduce(col[:, m, :], elm[:, :, :], ALU.max))
                c.then(v.tensor_tensor(e1[:, :, :], elm[:, :, :], over(col[:, m, :], N_EXP), ALU.is_ge))
                c.then(v.scalar_tensor_tensor(e1[:, :, :], e1[:, :, :], -256.0, ids(N_EXP), ALU.mult, ALU.add))
                c.then(reduce(col[:, IDX, :], e1[:, :, :], ALU.min))
                c.then(v.tensor_tensor(pick[:, j, :, :], e1[:, :, :], over(col[:, IDX, :], N_EXP), ALU.is_equal))
                if j == 0:
                    c.then(v.scalar_tensor_tensor(elm[:, :, :], pick[:, 0, :, :], -3e30, elm[:, :, :], ALU.mult, ALU.add))
            c.then(v.tensor_tensor(both[:, :, :], pick[:, 0, :, :], pick[:, 1, :, :], ALU.add))
            at["picked"] = c.n
            c.then(v.tensor_tensor(col[:, EX, :], col[:, M2, :], col[:, M1, :], ALU.subtract))
            at["gap"] = c.n
            c.then(v.memset(base[:, 0, :], 0.0))
            v.wait_ge(pre_done, 1)
            for t in range(NT):
                c.then(v.tensor_tensor(base[:, t + 1, :], base[:, t, :], bank[:R, 2 + t // half, (t % half) * N_EXP:(t % half + 1) * N_EXP],
                                       ALU.add))
            c.then(v.tensor_tensor(more[:, :, :], base[:, NT, :].unsqueeze(2).broadcast_to([R, N_EXP, MAX_BLK]),
                                   steps[:R, :].unsqueeze(1).broadcast_to([R, N_EXP, MAX_BLK]), ALU.is_gt))
            c.then(reduce(nblk[:, :], more[:, :, :], ALU.add))
            c.then(v.tensor_tensor_scan(ends[:, :], ones[:R, 0:N_EXP], nblk[:, :], 0.0, ALU.mult, ALU.add))
            c.then(v.tensor_tensor(first[:, :], ends[:, :], nblk[:, :], ALU.subtract))
            for h in range(2):
                th = slice(h * half, (h + 1) * half)
                last = v.tensor_tensor(e1[:, th, :], base[:, th, :],
                                       bank[:R, h, 0:half * N_EXP].rearrange("r (t e) -> r t e", e=N_EXP), ALU.add)
            c.then(last)
            c.then(v.scalar_tensor_tensor(e1[:, :, :], first[:, :].unsqueeze(1).broadcast_to([R, NT, N_EXP]), float(BT), e1[:, :, :],
                                          ALU.mult, ALU.add))
            c.then(v.tensor_tensor(pick[:, :, :, :].rearrange("r j t e -> r j (t e)"), pick[:, :, :, :].rearrange("r j t e -> r j (t e)"),
                                   e1[:, :, :].rearrange("r t e -> r (t e)").unsqueeze(1).broadcast_to([R, 2, NT * N_EXP]), ALU.mult))
            for j in range(2):
                last = reduce(slot_f[:, :, j], pick[:, j, :, :], ALU.add)
            c.then(last)
            v.tensor_copy(slot_i[:, :, :], slot_f[:, :, :]).then_inc(slots_rdy, 1)
            c.then(v.tensor_tensor(done[:, :, :], ends[0:1, :].unsqueeze(1).broadcast_to([1, N_BLK, N_EXP]),
                                   iota[0:1, :].unsqueeze(2).broadcast_to([1, N_BLK, N_EXP]), ALU.is_le))
            c.then(v.tensor_reduce(tab_f[:, 0:N_BLK], done[:, :, :], AX.X, ALU.add))
            c.then(v.tensor_scalar(tab_f[:, 0:N_BLK], tab_f[:, 0:N_BLK], float(N_EXP - 1), None, ALU.min))
            c.then(v.tensor_scalar(done[:, :, 0], iota[0:1, :], ends[0:1, N_EXP - 1:N_EXP], None, ALU.is_lt))
            c.then(v.tensor_reduce(tab_f[:, N_BLK:], done[:, 0:N_BLK:2, 0], AX.X, ALU.add))
            v.tensor_copy(tab_i[:, :], tab_f[:, :]).then_inc(tab_rdy, 1)
            v.wait_ge(ac, 2)
            c.then(reduce(col[:, GSUM, :], g1[:, :, :], ALU.add))
            c.then(v.reciprocal(col[:, PG, :], col[:, GSUM, :]))
            c.then(v.tensor_scalar(col[:, DEN, :], col[:, EX, :], 1.0, None, ALU.add))
            c.then(v.reciprocal(col[:, DEN, :], col[:, DEN, :]))
            c.then(v.tensor_tensor(wt[:, :, 0], col[:, DEN, :], col[:, PG, :], ALU.mult))
            v.tensor_tensor(wt[:, :, 1], wt[:, :, 0], col[:, EX, :], ALU.mult).then_inc(wt_rdy, 1)

        @block.scalar
        def _(a):
            a.sem_inc(hnT_rdy, 2)
            for q in hn_st:
                a.sem_inc(q, 16)
            with a.Fori(0, half) as i:
                for s in range(2):
                    a.wait_ge(x_ld[s], i * 16 + 16)
                    a.activation(junk[:R, :], x_in[:R, s, :], ACT.Square, accum_out=ssq[:R, s:s + 1]).then_inc(ssq_rdy, 1)
                    a.wait_ge(hn_rdy, 2 * i + s + 3)
                    a.dma_start(hn_d[ds(i * (2 * R) + s * R, R), :], hn[:R, s, :]).then_inc(hn_st[s], 16)
                    a.wait_ge(tr_done, 2 * i + s + 3)
                    for b in range(2):
                        last = a.activation(hnT[:, s, 4 * b:4 * b + 4, :].rearrange("p k r -> p (k r)"),
                                            bank[:, 2 * s + b, 0:4 * R], ACT.Copy)
                    last.then_inc(hnT_rdy, 1)
            c = Steps(a, ac)
            a.wait_ge(dv, at["shifted"])
            c.then(a.activation(g1[:, :, :], g1[:, :, :], ACT.Exp))
            a.wait_ge(dv, at["gap"])
            c.then(a.activation(col[:, 5, :], col[:, 5, :], ACT.Exp))
            for q in hn_st:
                a.wait_ge(q, 16 * (half + 1))

        @block.tensor
        def _(t):
            t.sem_inc(tr_done, 2)
            t.wait_ge(cst, n_cst)
            with t.Fori(0, half) as i:
                for s in range(2):
                    t.wait_ge(hn_rdy, 2 * i + s + 3)
                    t.wait_ge(hnT_rdy, 2 * i + s + 1)
                    for k in range(KT):
                        last = t.transpose(bank[:, 2 * s + k // 4, (k % 4) * R:(k % 4 + 1) * R], hn[:R, s, k * P:(k + 1) * P], ident[:R, :R])
                    last.then_inc(tr_done, 1)
                    t.wait_ge(hnT_rdy, 2 * i + s + 3)
                    t.wait_ge(lg_rdy, 2 * i + s + 1)
                    for k in range(KT):
                        last = t.matmul(bank[:R, 4 + s, 0:N_LOG], hnT[:, s, k, :], wr[:, k, :], start=(k == 0), stop=(k == KT - 1))
                    last.then_inc(lg_done, 1)
            t.wait_ge(dv, at["picked"])
            t.wait_ge(lg_rdy, NT + 2)
            for n, m in enumerate((before, ones)):
                for h in range(2):
                    last = t.matmul(bank[:R, 2 * n + h, 0:half * N_EXP], m[:R, :R],
                                    both[:, h * half:(h + 1) * half, :].rearrange("r t e -> r (t e)"), start=True, stop=True)
            last.then_inc(pre_done, 1)

        @block.gpsimd
        def _(g):
            g.wait_ge(cst, n_cst)
            with g.Fori(0, half) as i:
                for s in range(2):
                    g.wait_ge(ms_rdy, 2 * i + s + 1)
                    g.tensor_tensor(rstd[:R, s:s + 1], ms[:R, s:s + 1], neghalf[:R, :], ALU.pow).then_inc(rstd_rdy, 1)
            g.wait_ge(slots_rdy, 1)
            g.wait_ge(zeroed, 16)
            for t in range(NT):
                for j in range(2):
                    g.indirect_dma_start(out=slot_tok, out_offset=bass.IndirectOffsetOnAxis(ap=slot_i[:, t, j:j + 1], axis=0),
                                         in_=tok_id[:, t:t + 1], in_offset=None).then_inc(scat, 16)
            g.wait_ge(scat, 16 * 2 * NT)


def expert_blocks(nc, hn_d, slot_tok, table_d, wg_d, wu_d, wd_d, ident_d, yb_d):
    with ExitStack() as ctx:
        st = Stage(nc, ctx, "ex")
        PAIRS = N_BLK // 2
        M = D_EXP // P
        ident = st.sb("ident", [P, P])
        table = st.sb("table", [1, N_BLK + 1], I32)
        slots = st.sb("slots", [N_BLK, BT])
        idx_all = st.sb("idx_all", [BT, N_BLK + 1], I32)
        idx = st.sb("idx", [BT, 2], I32)
        x = st.sb("x", [BT, 2, D])
        xT = st.sb("xT", [P, 2, KT, BT])
        wg = st.sb("w_gate", [P, 2, KT, D_EXP])
        wu = st.sb("w_up", [P, 2, KT, D_EXP])
        wd = st.sb("w_down", [P, 2, M, D])
        sg = st.sb("silu_g", [P, 2, M, BT])
        hT = st.sb("hT", [P, 2, M, BT])
        y = st.sb("y", [BT, 2, D])
        zero = st.sb("zero", [BT, D])
        bank = st.ps("bank", [P, 8, 512])

        cst = st.sem("consts_loaded")
        idx_tr = st.sem("idx_transposed")
        idx_rdy = st.sem("idx_ready")
        idx_cp = st.sem("idx_copied")
        x_ld = st.sems("x_gathered")
        w_ld = st.sems("w_loaded")
        d_ld = st.sems("w_down_loaded")
        tr_done = st.sem("transposed")
        xT_rdy = st.sem("xT_ready")
        gu_done = st.sem("gate_up_done")
        pe_turn = st.sem("pe_turn")
        pool_turn = st.sem("pool_turn")
        zero_rdy = st.sem("zero_ready")
        sg_rdy = st.sem("silu_ready")
        h_rdy = st.sem("hidden_ready")
        y_done = st.sem("y_done")
        y0_rdy = st.sem("y_first_half_ready")
        y1_rdy = st.sem("y_second_half_ready")
        stored = st.sems("y_stored")
        block = ctx.enter_context(nc.Block())

        def in_use(eng, i):
            return eng.If(i < pairs[eng])

        pairs = {}

        def load_pairs(eng):
            eng.wait_ge(cst, 48)
            pairs[eng] = eng.value_load(table[0:1, N_BLK:N_BLK + 1], min_val=1, max_val=PAIRS)

        @block.sync
        def _(sp):
            sp.dma_start(ident[:, :], ident_d).then_inc(cst, 16)
            sp.dma_start(table[:, :], table_d).then_inc(cst, 16)
            sp.dma_start(slots[:, :], slot_tok.rearrange("(b p) a -> b (p a)", p=BT)).then_inc(cst, 16)
            load_pairs(sp)
            with sp.Fori(0, PAIRS) as i:
                with in_use(sp, i):
                    for s in range(2):
                        e = sp.value_load(table[0:1, ds(2 * i + s, 1)], min_val=0, max_val=N_EXP - 1)
                        sp.wait_ge(gu_done, 2 * i + s + 1)
                        sp.dma_start(wg[:, s, :, :].rearrange("p k f -> p (k f)"),
                                     wg_d[ds(e, 1), :, :].rearrange("a (p k) f -> (a p) (k f)", k=KT)).then_inc(w_ld[s], 16)
                        sp.dma_start(wu[:, s, :, :].rearrange("p k f -> p (k f)"),
                                     wu_d[ds(e, 1), :, :].rearrange("a (p k) f -> (a p) (k f)", k=KT)).then_inc(w_ld[s], 16)
                        sp.wait_ge(y_done, 2 * i + s + 1)
                        sp.dma_start(wd[:, s, :, :].rearrange("p m d -> p (m d)"),
                                     wd_d[ds(e, 1), :, :].rearrange("a (p m) d -> (a p) (m d)", m=M)).then_inc(d_ld[s], 16)

        @block.gpsimd
        def _(g):
            load_pairs(g)
            g.wait_ge(idx_rdy, 1)

            def gather(block_no, turn, s):
                g.wait_ge(tr_done, 2 * turn + s + 1)
                g.tensor_copy(idx[:, s:s + 1], idx_all[:, ds(block_no, 1)]).then_inc(idx_cp, 1)
                g.wait_ge(idx_cp, block_no + 1)
                g.sem_inc(pool_turn, 1)
                g.indirect_dma_start(out=x[:, s, :], out_offset=None, in_=hn_d,
                                     in_offset=bass.IndirectOffsetOnAxis(ap=idx[:, s:s + 1], axis=0)).then_inc(x_ld[s], 16)

            gather(0, 0, 0)
            with g.Fori(0, PAIRS) as i:
                with in_use(g, i):
                    gather(2 * i + 1, i, 1)
                    gather(2 * i + 2, i + 1, 0)
            g.wait_ge(x_ld[0], 16 * pairs[g] + 16)

        @block.tensor
        def _(t):
            t.sem_inc(tr_done, 2)
            t.sem_inc(gu_done, 2)
            t.sem_inc(y_done, 2)
            load_pairs(t)
            t.transpose(bank[:BT, 4, 0:N_BLK], slots[:, :], ident[:N_BLK, :N_BLK]).then_inc(idx_tr, 1)
            t.wait_ge(idx_rdy, 1)

            def transpose_x(turn, s):
                t.wait_ge(x_ld[s], turn * 16 + 16)
                t.wait_ge(xT_rdy, 2 * turn + s + 1)
                t.sem_inc(pe_turn, 1)
                for k in range(KT):
                    last = t.transpose(bank[:, s, k * BT:(k + 1) * BT], x[:, s, k::KT], ident[:BT, :BT])
                last.then_inc(tr_done, 1)

            def gate_up(turn, s):
                t.wait_ge(xT_rdy, 2 * turn + s + 3)
                t.wait_ge(w_ld[s], turn * 32 + 32)
                t.wait_ge(h_rdy, 2 * turn + s + 1)
                for n, w in enumerate((wg, wu)):
                    for m in range(M):
                        for k in range(KT):
                            last = t.matmul(bank[:, 2 + s, (n * M + m) * BT:(n * M + m + 1) * BT], w[:, s, k, m::M], xT[:, s, k, :],
                                            start=(k == 0), stop=(k == KT - 1))
                last.then_inc(gu_done, 1)

            def down(turn, s):
                t.wait_ge(h_rdy, 2 * turn + s + 3)
                t.wait_ge(d_ld[s], turn * 16 + 16)
                t.wait_ge(y0_rdy, 2 * turn + s + 1)
                t.wait_ge(y1_rdy, 2 * turn + s + 1)
                for c in range(2):
                    for m in range(M):
                        last = t.matmul(bank[:BT, 4 + 2 * s + c, :], hT[:, s, m, :], wd[:, s, m, c * 512:(c + 1) * 512],
                                        start=(m == 0), stop=(m == M - 1))
                last.then_inc(y_done, 1)

            transpose_x(0, 0)
            with t.Fori(0, PAIRS) as i:
                with in_use(t, i):
                    gate_up(i, 0)
                    transpose_x(i, 1)
                    down(i, 0)
                    gate_up(i, 1)
                    transpose_x(i + 1, 0)
                    down(i, 1)

        @block.scalar
        def _(a):
            for q in stored:
                a.sem_inc(q, 16)
            a.sem_inc(y0_rdy, 2)
            load_pairs(a)
            a.wait_ge(zero_rdy, 1)
            with a.Fori(0, PAIRS) as i:
                with in_use(a, i):
                    for s in range(2):
                        a.wait_ge(gu_done, 2 * i + s + 3)
                        a.wait_ge(h_rdy, 2 * i + s + 1)
                        a.activation(sg[:, s, :, :].rearrange("p m t -> p (m t)"), bank[:, 2 + s, 0:M * BT], ACT.Silu).then_inc(sg_rdy, 1)
                        a.wait_ge(y_done, 2 * i + s + 3)
                        a.wait_ge(stored[s], i * 16 + 16)
                        a.activation(y[:, s, 0:512], bank[:BT, 4 + 2 * s, :], ACT.Copy).then_inc(y0_rdy, 1)
                        a.wait_ge(y0_rdy, 2 * i + s + 3)
                        a.wait_ge(y1_rdy, 2 * i + s + 3)
                        a.dma_start(yb_d[ds(i * (2 * BT) + s * BT, BT), :], y[:, s, :]).then_inc(stored[s], 16)
                with a.Else():
                    for s in range(2):
                        a.wait_ge(stored[s], i * 16 + 16)
                        a.dma_start(yb_d[ds(i * (2 * BT) + s * BT, BT), :], zero[:, :]).then_inc(stored[s], 16)
            for q in stored:
                a.wait_ge(q, 16 * PAIRS + 16)

        @block.vector
        def _(v):
            v.sem_inc(xT_rdy, 2)
            v.sem_inc(h_rdy, 2)
            v.sem_inc(y1_rdy, 2)
            v.memset(zero[:, :], 0.0).then_inc(zero_rdy, 1)
            v.memset(idx_all[:, N_BLK:], 0)
            v.wait_ge(idx_tr, 1)
            v.tensor_copy(idx_all[:, 0:N_BLK], bank[:BT, 4, 0:N_BLK]).then_inc(idx_rdy, 1)
            load_pairs(v)

            def take_x(turn, s):
                v.wait_ge(tr_done, 2 * turn + s + 3)
                v.wait_ge(gu_done, 2 * turn + s + 1)
                v.tensor_copy(xT[:, s, :, :].rearrange("p k t -> p (k t)"), bank[:, s, :]).then_inc(xT_rdy, 1)

            def take_h(turn, s):
                v.wait_ge(sg_rdy, 2 * turn + s + 1)
                v.wait_ge(y_done, 2 * turn + s + 1)
                v.tensor_tensor(hT[:, s, :, :].rearrange("p m t -> p (m t)"), sg[:, s, :, :].rearrange("p m t -> p (m t)"),
                                bank[:, 2 + s, M * BT:2 * M * BT], ALU.mult).then_inc(h_rdy, 1)

            def take_y(turn, s):
                v.wait_ge(y_done, 2 * turn + s + 3)
                v.wait_ge(stored[s], turn * 16 + 16)
                v.tensor_copy(y[:, s, 512:], bank[:BT, 5 + 2 * s, :]).then_inc(y1_rdy, 1)

            take_x(0, 0)
            with v.Fori(0, PAIRS) as i:
                with in_use(v, i):
                    take_h(i, 0)
                    take_x(i, 1)
                    take_y(i, 0)
                    take_h(i, 1)
                    take_x(i + 1, 0)
                    take_y(i, 1)


def combine(nc, resid2, yb_d, slot_d, weight_d, gain_d, neghalf_d, out):
    with ExitStack() as ctx:
        st = Stage(nc, ctx, "out")
        NT = SEQ // P
        gain = st.sb("gain", [P, D])
        neghalf = st.sb("neghalf", [P, 1])
        res = st.sb("res", [P, 2, D])
        idx = st.sb("idx", [P, 2, 2], I32)
        wt = st.sb("wt", [P, 2, 2])
        y = st.sb("y", [P, 2, 2, D])
        acc = st.sb("acc", [P, 2, 2, D])
        junk = st.sb("junk", [P, 2, D])
        ssq = st.sb("ssq", [P, 2])
        ms = st.sb("ms", [P, 2])
        rstd = st.sb("rstd", [P, 2])
        o = st.sb("o", [P, 2, D])
        cst = st.sem("consts_loaded")
        ld = st.sems("loaded")
        y_ld = [st.sems(f"y{j}_gathered") for j in range(2)]
        turn_of_pool = st.sem("pool_turn")
        half = st.sem("first_added")
        acc_rdy = st.sem("sum_ready")
        ssq_rdy = st.sem("ssq_ready")
        ms_rdy = st.sem("ms_ready")
        rstd_rdy = st.sem("rstd_ready")
        o_rdy = st.sem("out_ready")
        stored = st.sems("stored")
        block = ctx.enter_context(nc.Block())

        @block.sync
        def _(sp):
            sp.dma_start(gain[:, :], gain_d.rearrange("(a d) -> a d", a=1).broadcast_to([P, D])).then_inc(cst, 16)
            sp.dma_start(neghalf[:, :], neghalf_d).then_inc(cst, 16)
            with sp.Fori(0, NT // 2) as i:
                for s in range(2):
                    sp.wait_ge(acc_rdy, 2 * i + s + 1)
                    rows = ds(i * (2 * P) + (N_META + s * P), P)
                    sp.dma_start(idx[:, s, :], slot_d[rows, :]).then_inc(ld[s], 16)
                    sp.dma_start(wt[:, s, :], weight_d[rows, :]).then_inc(ld[s], 16)
                    sp.dma_start(res[:, s, :], resid2[rows, :]).then_inc(ld[s], 16)

        @block.gpsimd
        def _(g):
            g.wait_ge(cst, 32)
            with g.Fori(0, NT // 2) as i:
                for s in range(2):
                    g.wait_ge(ld[s], i * 48 + 48)
                    g.wait_ge(acc_rdy, 2 * i + s + 1)
                    g.sem_inc(turn_of_pool, 1)
                    for j in range(2):
                        g.indirect_dma_start(out=y[:, s, j, :], out_offset=None, in_=yb_d,
                                             in_offset=bass.IndirectOffsetOnAxis(ap=idx[:, s, j:j + 1], axis=0)).then_inc(y_ld[j][s], 16)
                for s in range(2):
                    g.wait_ge(ms_rdy, 2 * i + s + 1)
                    g.tensor_tensor(rstd[:, s:s + 1], ms[:, s:s + 1], neghalf[:, :], ALU.pow).then_inc(rstd_rdy, 1)

        @block.vector
        def _(v):
            v.sem_inc(acc_rdy, 2)
            v.wait_ge(cst, 32)
            with v.Fori(0, NT // 2) as i:
                for s in range(2):
                    v.wait_ge(ld[s], i * 48 + 48)
                    v.wait_ge(y_ld[0][s], i * 16 + 16)
                    v.scalar_tensor_tensor(acc[:, s, 0, :], y[:, s, 0, :], wt[:, s, 0:1], res[:, s, :], ALU.mult, ALU.add).then_inc(half, 1)
                    v.wait_ge(half, 2 * i + s + 1)
                    v.wait_ge(y_ld[1][s], i * 16 + 16)
                    v.scalar_tensor_tensor(acc[:, s, 1, :], y[:, s, 1, :], wt[:, s, 1:2], acc[:, s, 0, :], ALU.mult, ALU.add).then_inc(acc_rdy, 1)
                for s in range(2):
                    v.wait_ge(ssq_rdy, 2 * i + s + 1)
                    v.tensor_scalar(ms[:, s:s + 1], ssq[:, s:s + 1], 1.0 / D, EPS, ALU.mult, ALU.add).then_inc(ms_rdy, 1)
                for s in range(2):
                    v.wait_ge(rstd_rdy, 2 * i + s + 1)
                    v.wait_ge(stored[s], i * 16 + 16)
                    v.scalar_tensor_tensor(o[:, s, :], acc[:, s, 1, :], rstd[:, s:s + 1], gain[:, :], ALU.mult, ALU.mult).then_inc(o_rdy, 1)

        @block.scalar
        def _(a):
            for q in stored:
                a.sem_inc(q, 16)
            with a.Fori(0, NT // 2) as i:
                for s in range(2):
                    a.wait_ge(acc_rdy, 2 * i + s + 3)
                    a.activation(junk[:, s, :], acc[:, s, 1, :], ACT.Square, accum_out=ssq[:, s:s + 1]).then_inc(ssq_rdy, 1)
                for s in range(2):
                    a.wait_ge(o_rdy, 2 * i + s + 1)
                    a.dma_start(out[ds(i * (2 * P) + s * P, P), :], o[:, s, :]).then_inc(stored[s], 16)
            for q in stored:
                a.wait_ge(q, 16 * (NT // 2 + 1))




def constants():
    t = np.arange(P)
    one = np.ones((P, P))
    same = np.kron(np.eye(2), np.ones((64, 64)))
    up_strict, up, low_strict = (t[:, None] < t[None, :]), (t[:, None] <= t[None, :]), (t[:, None] > t[None, :])
    cnt = np.minimum(np.arange(1, SEQ + 1)[None, :], np.array(POOL_WINDOWS)[:, None])
    r, s = np.arange(ROWS)[:, None], np.arange(ROWS)[None, :]
    ang_c = 2 * np.pi * (np.outer(t, t) % P) / P
    u = np.arange(LEN)
    ang_s = 2 * np.pi * (np.outer(u, u) % LEN) / LEN
    c = {
        "ident": np.eye(P),
        "neghalf": np.full((P, 1), -0.5),
        "blockones": same,
        "blockmean": same / 64,
        "chunk_mask": (np.arange(SEQ) % RC != 0)[None, :],
        "masks": np.concatenate([up_strict, up, up_strict, up, low_strict], axis=1),
        "inv_cnt": 1.0 / cnt,
        "ones": one,
        "chunk_mask2": (np.arange(LEN) % ROWS != 0)[None, :],
        "dirs": np.arange(HD)[:, None] // HEADS == np.arange(2)[None, :],
        "dmask": np.where(np.stack([s <= r, s >= r], axis=1), 3e38, -1e4),
        "strict": s != r,
        "chan": np.concatenate([np.cos(ang_c), -np.sin(ang_c)], axis=1),
        "iota": np.arange(N_BLK)[None, :],
        "block_steps": BT * np.arange(MAX_BLK)[None, :],
        "tok_id": np.arange(LEN).reshape(NCH, ROWS).T,
        "seq": np.stack([np.cos(ang_s), np.sin(ang_s)]) / np.sqrt(LEN * P),
    }
    return {k: np.ascontiguousarray(v, dtype=np.float32) for k, v in c.items()}


def columns(v):
    return np.ascontiguousarray(v.reshape(-1, P).T)


def laid_out(a):
    mu = a["mu_shift"][0]
    per_channel = [a[k][0].reshape(-1) for k in ("rwkv_w0", "rwkv_a0", "rwkv_k_k", "rwkv_k_a", "rwkv_r_k")]
    return {
        "pre_norm_cols": columns(a["pre_norm_w"][0]),
        "conv_taps_cols": np.ascontiguousarray(a["conv_w"][0].T),
        "pool_scale_cols": columns(a["pool_scale"][0]),
        "gn_w_cols": columns(a["rwkv_gn_w"][0]),
        "gn_b_cols": columns(a["rwkv_gn_b"][0]),
        "rwkv_columns": np.ascontiguousarray(np.stack(per_channel + list(mu[:4 * C_BR].reshape(4, C_BR)), axis=1)),
        "norm1_cols": columns(a["norm1_g_2"][0]),
        "conv2_taps_cols": np.ascontiguousarray(a["conv_w_2"][0].T),
        "a_log_cols": np.concatenate([a["a_log_fwd_2"][0], a["a_log_bwd_2"][0]]).reshape(HD, 1),
        "dt_bias_cols": np.concatenate([a["dt_bias_fwd_2"][0], a["dt_bias_bwd_2"][0]]).reshape(HD, 1),
        "out_norm_cols": columns(a["out_norm_g_2"][0]),
        "mu_lora": np.ascontiguousarray(mu[4 * C_BR:].reshape(P, 1)),
    }


def build(nc, t, c, out):
    def scratch(name, shape, dt=F32):
        return nc.dram_tensor(f"scr_{name}", shape, dt, kind="Internal").ap()

    x = t["x"][0]
    pT = scratch("pT", [N_IN, SEQ])
    ybT = scratch("ybT", [C_BR, SEQ])
    ycT = scratch("ycT", [C_BR, SEQ])
    yaT = scratch("yaT", [C_BR, SEQ])
    ar_d = scratch("ar", [C_BR, RCH, 2 * RC])
    bk_d = scratch("bk", [C_BR, RCH, 2 * RC])
    v_d = scratch("v", [C_BR, SEQ])
    wc_d = scratch("wc", [C_BR, RCH])
    bonus_d = scratch("bonus", [C_BR, SEQ])
    sz_d = scratch("sz", [C_BR, SEQ])
    yT_d = scratch("yT", [C_BR, SEQ])
    resid = scratch("resid", [LEN, D])

    norm_project(nc, "in1", x, SEQ, P, t["pre_norm_cols"], t["w_in"][0], 2 * CT, (4 * C_BR, P),
                 (N_RWKV_IN, (N_IN - N_RWKV_IN) // (2 * P)), pT, c["ident"], c["neghalf"])
    conv_branch(nc, pT, t["conv_taps_cols"], ybT)
    pool_branch(nc, pT, t["pool_w"][0], t["pool_scale_cols"], c["inv_cnt"], ycT)
    prm = (t["rwkv_columns"], t["mu_lora"], t["rwkv_w_up"][0], t["rwkv_a_up"][0])
    rwkv_prepare(nc, pT, prm, c["blockones"], c["chunk_mask"], ar_d, bk_d, v_d, wc_d, bonus_d, sz_d)
    rwkv_scan(nc, ar_d, bk_d, v_d, wc_d, c["ident"], c["masks"], yT_d)
    rwkv_finish(nc, yT_d, bonus_d, sz_d, t["gn_w_cols"], t["gn_b_cols"], c["blockmean"], yaT)
    gates = [pT[GATE_AT + n * D:GATE_AT + (n + 1) * D, :] for n in range(3)]
    wb = t["w_branch"][0]
    gate_merge_out(nc, "mix1", SEQ, P, [(wb[n], y) for n, y in enumerate((yaT, ybT, ycT))], gates,
                   t["w_out"][0], t["post_norm_w"][0], x, resid[N_META:, :], c["neghalf"],
                   copy=(resid[0:N_META, :], t["meta_tokens_2"]))

    p2T = scratch("p2T", [IN2, LEN])
    qT_d, kT_d, vT_d, ydT = (scratch(n, [HEADS * DK, LEN]) for n in ("qT", "kT", "vT", "ydT"))
    yfT = scratch("yfT", [F_W, LEN])
    gc_d = scratch("gc", [HD, LEN])
    egc_d = scratch("egc", [HD, LEN])
    tot_d = scratch("tot", [HD, NCH])
    etot_d = scratch("etot", [HD, NCH])
    sc_d = scratch("sc", [HD, ROWS, 5 * NCH])
    resid2 = scratch("resid2", [LEN, D])
    norm_project(nc, "in2", resid, LEN, ROWS, t["norm1_cols"], t["w_in_2"][0], AB_AT // (2 * P), (AB_AT, 4 * HEADS),
                 (GF_AT, D // P), p2T, c["ident"], c["neghalf"])
    qkv_conv(nc, p2T, t["conv2_taps_cols"], c["ones"], qT_d, kT_d, vT_d)
    delta_decays(nc, p2T, t["a_log_cols"], t["dt_bias_cols"], c["dirs"], c["chunk_mask2"], c["ident"],
                 gc_d, egc_d, tot_d, etot_d, sc_d)
    delta_scan(nc, p2T, qT_d, kT_d, vT_d, gc_d, egc_d, etot_d, sc_d, c["dmask"], c["strict"], c["ident"], c["ones"],
               t["out_norm_cols"], ydT)
    fourier(nc, p2T, c["chan"], c["seq"], yfT)
    gate_merge_out(nc, "mix2", LEN, ROWS, [(t["w_fourier_2"][0], yfT), (t["w_delta_2"][0], ydT)],
                   [p2T[GF_AT:GF_AT + D, :], p2T[GF_AT + D:, :]], t["w_out_2"][0], None, resid, resid2, c["neghalf"])

    hn_d = scratch("hn", [LEN, D])
    slot_tok = scratch("slot_tok", [N_SLOT, 1])
    slot_d = scratch("slot", [LEN, 2], I32)
    weight_d = scratch("weight", [LEN, 2])
    table_d = scratch("table", [1, N_BLK + 1], I32)
    yb = scratch("yb", [N_SLOT, D])
    route(nc, resid2, t["norm2_g_2"][0], t["w_router_group_2"][0], t["b_router_group_2"][0], t["w_router_expert_2"][0],
          t["b_router_expert_2"][0], c, hn_d, slot_tok, slot_d, weight_d, table_d)
    expert_blocks(nc, hn_d, slot_tok, table_d, t["w_gate_e_2"][0], t["w_up_e_2"][0], t["w_down_e_2"][0], c["ident"], yb)
    combine(nc, resid2, yb, slot_d, weight_d, t["final_norm_g_2"], c["neghalf"], out)


def kernel(**inputs):
    import concourse.bacc as bacc
    from concourse.bass_utils import run_bass_kernel_spmd

    nc = bacc.Bacc("TRN2", target_bir_lowering=False, num_devices=1)
    given = {k: np.ascontiguousarray(v) for k, v in inputs.items()}
    arrays, t, c = {}, {}, {}
    for aps, prefix, values in ((t, "in_", {**given, **laid_out(given)}), (c, "const_", constants())):
        for name, a in values.items():
            if a.size:
                arrays[prefix + name] = a
                aps[name] = nc.dram_tensor(prefix + name, a.shape, mybir.dt.from_np(a.dtype), kind="ExternalInput").ap()
    out = nc.dram_tensor("out", (1, SEQ, D), F32, kind="ExternalOutput").ap()
    build(nc, t, c, out[0])
    r = run_bass_kernel_spmd(nc, [arrays], core_ids=[0])
    return r.results[0]["out"]
```

```python
from contextlib import ExitStack, nullcontext

import numpy as np

import concourse.bass as bass
from concourse import mybir

F32 = mybir.dt.float32
I32 = mybir.dt.int32
F32R = mybir.dt.float32r
ALU = mybir.AluOpType
ACT = mybir.ActivationFunctionType
AX = mybir.AxisListType
ds = bass.ds

P = 128
D = 1024
KT = D // P
EPS = 1e-6

SEQ = 1024
N_META = 16
LEN = SEQ + N_META

C_BR = 512
CT = C_BR // P
N_RWKV_IN = 4 * C_BR + 128
N_CONV_IN = 4 * C_BR
N_POOL_IN = 2 * C_BR
N_IN = N_RWKV_IN + N_CONV_IN + N_POOL_IN + 3 * D
CONV_AT = N_RWKV_IN
POOL_AT = CONV_AT + N_CONV_IN
GATE_AT = POOL_AT + N_POOL_IN
RC = 64
RCH = SEQ // RC
DECAY = float(np.exp(-0.5))
GN_EPS = 64 * 1e-5
POOL_WINDOWS = (2, 4, 8, 16)

HEADS = 8
DK = 128
F_W = 512
QKV_AT = F_W
Z_AT = QKV_AT + 3 * HEADS * DK
AB_AT = Z_AT + HEADS * DK
GF_AT = AB_AT + 4 * HEADS
IN2 = GF_AT + 2 * D
ROWS = 104
NCH = LEN // ROWS
HD = 2 * HEADS
HALF_W = -(-(LEN // 2 + 1) // 48) * 48
GROUPS = ((0, 4), (4, 4), (8, 2))

N_GRP = 8
N_EXP = 64
D_EXP = 256
BT = 96
N_BLK = (2 * LEN + N_EXP * (BT - 1)) // BT
TURN = 6
N_BLK += -N_BLK % TURN
N_SLOT = N_BLK * BT
MAX_BLK = -(-LEN // BT)
VACANT = 1 << 20
N_LOG = N_GRP + N_EXP


def pieces(n):
    if n <= 512:
        return [(0, n)]
    k = -(-n // 512)
    w = -(-n // (8 * k)) * 8
    return [(a, min(w, n - a)) for a in range(0, n, w)]


class Steps:

    def __init__(self, eng, sem, base=0):
        self.eng, self.sem, self.base, self.n = eng, sem, base, 0

    def then(self, instruction):
        instruction.then_inc(self.sem, 1)
        self.n += 1
        self.eng.wait_ge(self.sem, self.base + self.n)


class Plan:

    def __init__(self, sem, keys):
        self.sem, self.keys, self.n = sem, keys, len(keys)
        self.value = {k: i + 2 for i, k in enumerate(keys)}
        assert len(self.value) == self.n
        self.done = 0

    def begin(self, eng):
        eng.sem_inc(self.sem, 1)

    def wait_turn(self, eng, turn):
        eng.wait_ge(self.sem, turn * self.n + 1)

    def step(self, instruction, *key):
        assert self.keys[self.done % self.n] == key, (self.keys[self.done % self.n], key)
        self.done += 1
        instruction.then_inc(self.sem, 1)

    def wait(self, eng, turn, *key):
        eng.wait_ge(self.sem, turn * self.n + self.value[key])

    def wait_all(self, eng, turn, *keys):
        self.wait(eng, turn, *max(keys, key=self.value.get))


class Beside:

    def __init__(self, program):
        self.program = program
        self.place = next(program)

    def upto(self, place):
        while self.place is not None and self.place <= place:
            self.place = next(self.program, None)


class Stage:

    def __init__(self, nc, ctx, name):
        self.nc, self.ctx, self.name, self.taken = nc, ctx, name, []
        ctx.callback(self.give_back)

    def give_back(self):
        self.nc.clear_and_free_semaphores(self.taken)
        self.nc.all_engine_barrier()

    def sb(self, name, shape, dt=F32):
        return self.ctx.enter_context(self.nc.sbuf_tensor(f"{self.name}_{name}_sb", shape, dt))

    def ps(self, name, shape, dt=F32):
        return self.ctx.enter_context(self.nc.psum_tensor(f"{self.name}_{name}_ps", shape, dt))

    def sem(self, name):
        self.taken.append(self.nc.alloc_semaphore(name=f"{self.name}_{name}"))
        return self.taken[-1]

    def sems(self, name, n=2):
        return [self.sem(f"{name}{k}") for k in range(n)]


def norm_project(nc, name, src, n_tok, rows, gain, w, first_pairs, peeled, second, dst, ident_d, rms_d, kept=None):
    n_tiles = n_tok // rows
    pcs = pieces(n_tok)
    w_v = w.rearrange("(k p) n -> p k n", p=P)
    pc, pw = peeled
    sc, sp_ = second
    mid = 2 * first_pairs
    none = nullcontext()
    with ExitStack() as ctx:
        st = Stage(nc, ctx, name)
        h = st.sb("h", [P, 2, KT, rows])
        h_hi, h_lo = kept or [st.sb(n, [P, KT, n_tok], F32R) for n in ("h_hi", "h_lo")]
        ident = st.sb("ident", [P, P])
        rms_cols = st.sb("rms_cols", [P, 2])
        gain_sb = st.sb("gain", [P, KT])
        x_in = st.sb("x_in", [P, 2, D])
        junk = st.sb("junk", [P, D])
        ssq = st.sb("ssq", [P, 2])
        ms = st.sb("ms", [P, 2])
        rstd = st.sb("rstd", [P, 2])
        xn = st.sb("xn", [P, 2, D])
        w_sb = st.sb("w", [P, 2, KT, P])
        w_hi = st.sb("w_hi", [P, 2, KT, P], F32R)
        w_lo = st.sb("w_lo", [P, 2, KT, P], F32R)
        o_sb = st.sb("o", [P, 2, n_tok])
        bank = st.ps("bank", [P, 8, 512])

        consts = st.sem("consts_loaded")
        x_ld = st.sems("x_loaded")
        ssq_rdy = st.sem("ssq_ready")
        ms_rdy = st.sem("ms_ready")
        rstd_rdy = st.sem("rstd_ready")
        xn_rdy = st.sem("xn_ready")
        tr_done = st.sem("transposed")
        hT_rdy = st.sem("hT_ready")
        w_ld = st.sems("w_loaded")
        w_hi_rdy = st.sem("w_hi_ready")
        w_split = st.sem("w_split")
        h_step = st.sem("h_step")
        mm_done = st.sem("product_done")
        evac = st.sem("evacuated")
        stored = st.sems("tile_stored")
        block = ctx.enter_context(nc.Block())

        @block.sync
        def _(sp):
            sp.dma_start(ident[:, :], ident_d).then_inc(consts, 16)
            sp.dma_start(rms_cols[:, :], rms_d).then_inc(consts, 16)
            sp.dma_start(gain_sb[:, :], gain).then_inc(consts, 16)
            with sp.Fori(0, n_tiles // 2) as i:
                for s in range(2):
                    sp.wait_ge(xn_rdy, 2 * i + s + 1)
                    sp.dma_start(x_in[:rows, s, :], src[ds(i * (2 * rows) + s * rows, rows), :]).then_inc(x_ld[s], 16)

            def load_w(i, c, col, width):
                sp.wait_ge(w_split, 2 * i + c + 1)
                sp.dma_start(w_sb[:, c % 2, :, 0:width], w_v[:, :, ds(col, width)]).then_inc(w_ld[c % 2], 16)

            with sp.Fori(0, first_pairs) as i:
                for s in range(2):
                    load_w(i, s, i * (2 * P) + s * P, P)
            load_w(0, mid, pc, pw)
            with sp.Fori(0, sp_) if sp_ else none as i:
                for s in range(2 if sp_ else 0):
                    load_w(i, mid + 1 + s, i * (2 * P) + (sc + s * P), P)

        @block.scalar
        def _(act):
            act.sem_inc(xn_rdy, 2)
            act.sem_inc(evac, 2)
            for q in stored:
                act.sem_inc(q, 16)
            act.wait_ge(consts, 48)
            with act.Fori(0, n_tiles // 2) as i:
                for s in range(2):
                    act.wait_ge(x_ld[s], i * 16 + 16)
                    act.activation(junk[:rows, :], x_in[:rows, s, :], ACT.Square, scale=D ** -0.5,
                                   accum_out=ssq[:rows, s:s + 1]).then_inc(ssq_rdy, 1)
                    act.wait_ge(rstd_rdy, 2 * i + s + 1)
                    act.wait_ge(tr_done, 2 * i + s + 1)
                    act.activation(xn[:rows, s, :], x_in[:rows, s, :], ACT.Copy,
                                   scale=rstd[:rows, s:s + 1]).then_inc(xn_rdy, 1)

            def evacuate(i, c, row, width):
                s = c % 2
                act.wait_ge(mm_done, 2 * i + c + 3)
                act.wait_ge(stored[s], i * 16 + (c // 2 + 1) * 16)
                for n, (a, m) in enumerate(pcs):
                    last = act.activation(o_sb[:width, s, a:a + m], bank[:width, 4 * s + n, 0:m], ACT.Copy)
                last.then_inc(evac, 1)
                act.wait_ge(evac, 2 * i + c + 3)
                act.dma_start(dst[ds(row, width), :], o_sb[:width, s, :]).then_inc(stored[s], 16)

            with act.Fori(0, first_pairs) as i:
                for s in range(2):
                    evacuate(i, s, i * (2 * P) + s * P, P)
            evacuate(0, mid, pc, pw)
            with act.Fori(0, sp_) if sp_ else none as i:
                for s in range(2 if sp_ else 0):
                    evacuate(i, mid + 1 + s, i * (2 * P) + (sc + s * P), P)
            total = mid + 1 + 2 * sp_
            act.wait_ge(stored[0], 16 * ((total + 1) // 2 + 1))
            act.wait_ge(stored[1], 16 * (total // 2 + 1))

        @block.vector
        def _(dve):
            dve.sem_inc(hT_rdy, 2)
            dve.sem_inc(w_split, 2)
            dve.wait_ge(consts, 48)
            with dve.Fori(0, n_tiles // 2) as i:
                for s in range(2):
                    dve.wait_ge(tr_done, 2 * i + s + 3)
                    rows_at = ds(i * (2 * rows) + s * rows, rows)
                    for b in range(2):
                        last = dve.tensor_tensor(h[:, s, 4 * b:4 * b + 4, :],
                                                 bank[:, 2 * s + b, 0:4 * rows].rearrange("p (k r) -> p k r", k=4),
                                                 gain_sb[:, 4 * b:4 * b + 4].unsqueeze(2).broadcast_to([P, 4, rows]), ALU.mult)
                    c = Steps(dve, h_step, 4 * i + 2 * s)
                    c.then(last)
                    c.then(dve.tensor_copy(h_hi[:, :, rows_at], h[:, s, :, :]))
                    dve.tensor_tensor(h_lo[:, :, rows_at], h[:, s, :, :], h_hi[:, :, rows_at].bitcast(F32), ALU.subtract).then_inc(hT_rdy, 1)

            def split(i, c, width):
                s = c % 2
                dve.wait_ge(w_ld[s], i * 16 + (c // 2 + 1) * 16)
                dve.wait_ge(mm_done, 2 * i + c + 1)
                dve.tensor_copy(w_hi[:, s, :, 0:width], w_sb[:, s, :, 0:width]).then_inc(w_hi_rdy, 1)
                dve.wait_ge(w_hi_rdy, 2 * i + c + 1)
                dve.tensor_tensor(w_lo[:, s, :, 0:width], w_sb[:, s, :, 0:width], w_hi[:, s, :, 0:width].bitcast(F32), ALU.subtract).then_inc(w_split, 1)

            with dve.Fori(0, first_pairs) as i:
                for s in range(2):
                    split(i, s, P)
            split(0, mid, pw)
            with dve.Fori(0, sp_) if sp_ else none as i:
                for s in range(2 if sp_ else 0):
                    split(i, mid + 1 + s, P)

        @block.gpsimd
        def _(pool):
            pool.wait_ge(consts, 48)
            with pool.Fori(0, n_tiles // 2) as i:
                for s in range(2):
                    pool.wait_ge(ssq_rdy, 2 * i + s + 1)
                    pool.tensor_tensor(ms[:rows, s:s + 1], ssq[:rows, s:s + 1], rms_cols[:rows, 0:1], ALU.add).then_inc(ms_rdy, 1)
                    pool.wait_ge(ms_rdy, 2 * i + s + 1)
                    pool.tensor_tensor(rstd[:rows, s:s + 1], ms[:rows, s:s + 1], rms_cols[:rows, 1:2],
                                       ALU.pow).then_inc(rstd_rdy, 1)

        @block.tensor
        def _(pe):
            pe.sem_inc(tr_done, 2)
            pe.sem_inc(mm_done, 2)
            pe.wait_ge(consts, 48)
            with pe.Fori(0, n_tiles // 2) as i:
                for s in range(2):
                    pe.wait_ge(xn_rdy, 2 * i + s + 3)
                    pe.wait_ge(hT_rdy, 2 * i + s + 1)
                    for k in range(KT):
                        last = pe.transpose(bank[:, 2 * s + k // 4, (k % 4) * rows:(k % 4 + 1) * rows],
                                            xn[:rows, s, k * P:(k + 1) * P], ident[:rows, :rows])
                    last.then_inc(tr_done, 1)
            pe.wait_ge(hT_rdy, n_tiles + 2)

            def product(i, c, width):
                s = c % 2
                pe.wait_ge(w_split, 2 * i + c + 3)
                pe.wait_ge(evac, 2 * i + c + 1)
                for n, (a, m) in enumerate(pcs):
                    for k in range(KT):
                        for z, (w_, h_) in enumerate(((w_hi, h_hi), (w_hi, h_lo), (w_lo, h_hi))):
                            last = pe.matmul(bank[:width, 4 * s + n, 0:m], w_[:, s, k, 0:width], h_[:, k, a:a + m],
                                             start=(k == 0 and z == 0), stop=(k == KT - 1 and z == 2))
                last.then_inc(mm_done, 1)

            with pe.Fori(0, first_pairs) as i:
                for s in range(2):
                    product(i, s, P)
            product(0, mid, pw)
            with pe.Fori(0, sp_) if sp_ else none as i:
                for s in range(2 if sp_ else 0):
                    product(i, mid + 1 + s, P)


class ProjectBeside:

    def __init__(self, st, kept, n_tok, w, dst, column, per):
        self.h_hi, self.h_lo = kept
        self.w, self.dst, self.column, self.per = w.rearrange("(k p) n -> p k n", p=P), dst, column, per
        self.pcs = pieces(n_tok)
        self.w_sb = st.sb("tile_w", [P, 2, KT, P])
        self.w_hi = st.sb("tile_w_hi", [P, 2, KT, P], F32R)
        self.w_lo = st.sb("tile_w_lo", [P, 2, KT, P], F32R)
        self.o_sb = st.sb("tile_o", [P, 2, n_tok])
        self.bank = st.ps("tile_bank", [P, 2, len(self.pcs), 512])
        self.w_ld = st.sems("tile_w_loaded")
        self.w_hi_rdy = st.sem("tile_w_hi_ready")
        self.w_split = st.sem("tile_w_split")
        self.mm_done = st.sem("tile_product_done")
        self.evac = st.sem("tile_evacuated")
        self.stored = st.sems("tile_stored")

    def column_of(self, i, u):
        return ds(i * (self.per * P) + (self.column + u * P), P)

    def load(self, sp, i, u):
        sp.wait_ge(self.w_split, i * self.per + u + 1)
        sp.dma_start(self.w_sb[:, u % 2, :, :], self.w[:, :, self.column_of(i, u)]).then_inc(self.w_ld[u % 2], 16)

    def begin_split(self, dve):
        dve.sem_inc(self.w_split, 2)

    def split(self, dve, i, u):
        s = u % 2
        dve.wait_ge(self.w_ld[s], i * (8 * self.per) + 16 * (u // 2 + 1))
        dve.wait_ge(self.mm_done, i * self.per + u + 1)
        dve.tensor_copy(self.w_hi[:, s, :, :], self.w_sb[:, s, :, :]).then_inc(self.w_hi_rdy, 1)
        dve.wait_ge(self.w_hi_rdy, i * self.per + u + 1)
        dve.tensor_tensor(self.w_lo[:, s, :, :], self.w_sb[:, s, :, :], self.w_hi[:, s, :, :].bitcast(F32), ALU.subtract).then_inc(self.w_split, 1)

    def begin_product(self, pe):
        pe.sem_inc(self.mm_done, 2)

    def product(self, pe, i, u):
        s = u % 2
        pe.wait_ge(self.w_split, i * self.per + u + 3)
        pe.wait_ge(self.evac, i * self.per + u + 1)
        for n, (a, m) in enumerate(self.pcs):
            for k in range(KT):
                for z, (w_, h_) in enumerate(((self.w_hi, self.h_hi), (self.w_hi, self.h_lo), (self.w_lo, self.h_hi))):
                    last = pe.matmul(self.bank[:, s, n, 0:m], w_[:, s, k, :], h_[:, k, a:a + m],
                                     start=(k == 0 and z == 0), stop=(k == KT - 1 and z == 2))
        last.then_inc(self.mm_done, 1)

    def begin_store(self, act):
        act.sem_inc(self.evac, 2)
        for q in self.stored:
            act.sem_inc(q, 16)

    def store(self, act, i, u):
        s = u % 2
        act.wait_ge(self.mm_done, i * self.per + u + 3)
        act.wait_ge(self.stored[s], i * (8 * self.per) + 16 * (u // 2 + 1))
        for n, (a, m) in enumerate(self.pcs):
            last = act.activation(self.o_sb[:, s, a:a + m], self.bank[:, s, n, 0:m], ACT.Copy)
        last.then_inc(self.evac, 1)
        act.wait_ge(self.evac, i * self.per + u + 3)
        act.dma_start(self.dst[self.column_of(i, u), :], self.o_sb[:, s, :]).then_inc(self.stored[s], 16)

    def end_store(self, act, turns):
        for q in self.stored:
            act.wait_ge(q, turns * (8 * self.per) + 16)


def conv_branch(nc, pT, conv_w, ybT, project):
    with ExitStack() as ctx:
        st = Stage(nc, ctx, "conv")
        tiles = ProjectBeside(st, *project)
        W = conv_w.shape[1]
        pad = W - 1
        inp = st.sb("bcuz", [P, 4, SEQ])
        taps_j = st.sb("taps_j", [P, W])
        cu = st.sb("cu", [P, pad + SEQ])
        y = st.sb("y", [P, 2, SEQ])
        sz = st.sb("silu_z", [P, SEQ])
        o = st.sb("o", [P, SEQ])
        ld = st.sem("loaded")
        tp = st.sem("taps_loaded")
        silu = st.sem("silu_ready")
        step = st.sem("dve_step")
        out_rdy = st.sem("out_ready")
        stored = st.sem("stored")
        block = ctx.enter_context(nc.Block())
        src = pT[CONV_AT:CONV_AT + N_CONV_IN, :].rearrange("(q r) t -> r q t", q=4)

        @block.sync
        def _(sp):
            with sp.Fori(0, CT) as j:
                for u in range(2):
                    tiles.load(sp, j, u)
                sp.wait_ge(out_rdy, j + 1)
                sp.dma_start(inp[:, :, :], src[ds(j * P, P), :, :]).then_inc(ld, 16)
                sp.dma_start(taps_j[:, :], conv_w[ds(j * P, P), :]).then_inc(tp, 16)
                for u in range(2, tiles.per):
                    tiles.load(sp, j, u)

        @block.tensor
        def _(pe):
            tiles.begin_product(pe)
            with pe.Fori(0, CT) as j:
                for u in range(tiles.per):
                    tiles.product(pe, j, u)

        @block.scalar
        def _(act):
            act.sem_inc(stored, 16)
            tiles.begin_store(act)
            with act.Fori(0, CT) as j:
                act.wait_ge(ld, j * 16 + 16)
                act.wait_ge(out_rdy, j + 1)
                act.activation(sz[:, :], inp[:, 3, :], ACT.Silu).then_inc(silu, 1)
                for u in range(2):
                    tiles.store(act, j, u)
                act.wait_ge(out_rdy, j + 2)
                act.dma_start(ybT[ds(j * P, P), :], o[:, :]).then_inc(stored, 16)
                for u in range(2, tiles.per):
                    tiles.store(act, j, u)
            act.wait_ge(stored, 16 * (CT + 1))
            tiles.end_store(act, CT)

        @block.vector
        def _(dve):
            dve.sem_inc(out_rdy, 1)
            tiles.begin_split(dve)
            dve.memset(cu[:, 0:pad], 0.0).then_inc(step, 1)
            dve.wait_ge(step, 1)
            with dve.Fori(0, CT) as j:
                for u in range(2):
                    tiles.split(dve, j, u)
                dve.wait_ge(ld, j * 16 + 16)
                dve.wait_ge(tp, j * 16 + 16)
                c = Steps(dve, step, j * 5 + 1)
                c.then(dve.tensor_tensor(cu[:, pad:pad + SEQ], inp[:, 1, :], inp[:, 2, :], ALU.mult))
                c.then(dve.tensor_scalar(y[:, 0, :], cu[:, 0:SEQ], taps_j[:, 0:1], None, ALU.mult))
                for k in range(1, W):
                    c.then(dve.scalar_tensor_tensor(y[:, k % 2, :], cu[:, k:k + SEQ], taps_j[:, k:k + 1],
                                                    y[:, (k - 1) % 2, :], ALU.mult, ALU.add))
                c.then(dve.tensor_tensor(y[:, W % 2, :], y[:, (W - 1) % 2, :], inp[:, 0, :], ALU.mult))
                assert c.n == 5
                dve.wait_ge(silu, j + 1)
                dve.wait_ge(stored, j * 16 + 16)
                dve.tensor_tensor(o[:, :], y[:, W % 2, :], sz[:, :], ALU.mult).then_inc(out_rdy, 1)
                for u in range(2, tiles.per):
                    tiles.split(dve, j, u)


def pool_branch(nc, pT, pool_w, pool_scale, inv_cnt_d, ycT):
    with ExitStack() as ctx:
        st = Stage(nc, ctx, "pool")
        G = len(POOL_WINDOWS)
        pad = max(POOL_WINDOWS)
        u = st.sb("u", [P, G, pad + SEQ])
        z = st.sb("z", [P, G, SEQ])
        w = st.sb("w", [P, G, P])
        scale = st.sb("scale", [P, G])
        inv = st.sb("inv_cnt", [P, G, SEQ])
        sums = st.sb("sums", [P, 2, pad + SEQ])
        pooled = st.sb("pooled", [P, G, SEQ])
        sz = st.sb("silu_z", [P, G, SEQ])
        o = st.sb("o", [P, G, SEQ])
        ps = st.ps("mixed", [P, G, 2, 512])
        ld = st.sem("loaded")
        step = st.sem("dve_step")
        pooled_rdy = st.sem("pooled_ready")
        silu = st.sem("silu_ready")
        mixed = st.sem("mixed")
        out_rdy = st.sem("out_ready")
        stored = st.sem("stored")
        block = ctx.enter_context(nc.Block())
        n_ld = 4 + G

        @block.sync
        def _(sp):
            up = pT[POOL_AT:POOL_AT + C_BR, :].rearrange("(g p) t -> p g t", p=P)
            zp = pT[POOL_AT + C_BR:POOL_AT + 2 * C_BR, :].rearrange("(g p) t -> p g t", p=P)
            sp.dma_start(u[:, :, pad:], up).then_inc(ld, 16)
            sp.dma_start(z[:, :, :], zp).then_inc(ld, 16)
            sp.dma_start(w[:, :, :], pool_w.rearrange("g c d -> c g d")).then_inc(ld, 16)
            sp.dma_start(scale[:, :], pool_scale).then_inc(ld, 16)
            for g in range(G):
                sp.dma_start(inv[:, g, :], inv_cnt_d[g:g + 1, :].broadcast_to([P, SEQ])).then_inc(ld, 16)
            for g in range(G):
                sp.wait_ge(out_rdy, g + 1)
                sp.dma_start(ycT[g * P:(g + 1) * P, :], o[:, g, :]).then_inc(stored, 16)
            sp.wait_ge(stored, 16 * G)

        @block.scalar
        def _(act):
            act.wait_ge(ld, 16 * n_ld)
            for g in range(G):
                act.activation(sz[:, g, :], z[:, g, :], ACT.Silu).then_inc(silu, 1)

        @block.vector
        def _(dve):
            c = Steps(dve, step)
            c.then(dve.memset(u[:, :, 0:pad], 0.0))
            c.then(dve.memset(sums[:, :, 0:pad], 0.0))
            dve.wait_ge(ld, 16 * n_ld)
            for g, win in enumerate(POOL_WINDOWS):
                src, k, n = u[:, g, :], 1, 0
                while k < win:
                    c.then(dve.tensor_tensor(sums[:, n, pad:], src[:, pad:], src[:, pad - k:pad + SEQ - k], ALU.add))
                    src, k, n = sums[:, n, :], 2 * k, 1 - n
                c.then(dve.tensor_tensor(sums[:, n, pad:], src[:, pad:], inv[:, g, :], ALU.mult))
                dve.tensor_tensor(pooled[:, g, :], sums[:, n, pad:], u[:, g, pad:], ALU.subtract).then_inc(pooled_rdy, 1)
                dve.wait_ge(pooled_rdy, g + 1)
            dve.wait_ge(silu, G)
            for g in range(G):
                dve.wait_ge(mixed, g + 1)
                for h in range(2):
                    last = dve.scalar_tensor_tensor(o[:, g, h * 512:(h + 1) * 512], ps[:, g, h, :], scale[:, g:g + 1],
                                                    sz[:, g, h * 512:(h + 1) * 512], ALU.mult, ALU.mult)
                last.then_inc(out_rdy, 1)

        @block.tensor
        def _(pe):
            pe.wait_ge(ld, 16 * n_ld)
            for g in range(G):
                pe.wait_ge(pooled_rdy, g + 1)
                for h in range(2):
                    last = pe.matmul(ps[:, g, h, :], w[:, g, :], pooled[:, g, h * 512:(h + 1) * 512], start=True, stop=True)
                last.then_inc(mixed, 1)


def rwkv_prepare(nc, pT, prm, blockones_d, chunk_mask_d, ar_d, bk_d, v_d, wc_d, bonus_d, sz_d, project):
    columns, mu_lora, w_up, a_up = prm
    with ExitStack() as ctx:
        st = Stage(nc, ctx, "prep")
        tiles = ProjectBeside(st, *project)
        N = SEQ
        lora = st.sb("lora", [P, 1 + N])
        lora_s = st.sb("lora_shifted", [P, N])
        lora_t = st.sb("lora_tanh", [64, N])
        mu_l = st.sb("mu_lora", [P, 1])
        raw = st.sb("rkvz", [P, 4, 1 + N])
        par = st.sb("params", [P, 9])
        W0, A0, KK_, KA_, RK_, MU = 0, 1, 2, 3, 4, 5
        up = st.sb("lora_up", [P, P])
        blk = st.sb("blockones", [P, P])
        cmask = st.sb("chunk_mask", [P, N])
        sh = st.sb("shifted", [P, 4, N])
        diff = st.sb("diff", [P, N])
        sgw = st.sb("sgw", [P, N])
        a = st.sb("a", [P, N])
        cs = st.sb("cs", [P, N])
        w_t = st.sb("w_t", [P, N])
        w_p, w_i = diff, sgw
        kk = st.sb("kk", [P, N])
        sq = st.sb("sq", [P, N])
        rn = st.sb("rn", [P, N])
        k2 = st.sb("k2", [P, N])
        tmp = st.sb("tmp", [P, N])
        ar = st.sb("ar", [P, RCH, 2, RC])
        bk = st.sb("bk", [P, RCH, 2, RC])
        bon = st.sb("bonus", [P, N])
        sz = sh[:, 3, :]
        wc = st.sb("chunk_decay", [P, RCH])
        pre = st.ps("pre", [P, 2, 2, 512])
        sums = pre

        cst = st.sem("consts_loaded")
        ld = st.sem("inputs_loaded")
        step = st.sem("dve_step")
        free = st.sem("turn_done")
        shifted = st.sem("lora_shifted")
        tanhed = st.sem("lora_tanhed")
        pre_done = st.sem("lora_product_done")
        sig = st.sem("sigmoids_ready")
        cum = st.sem("cumsum_ready")
        exps = st.sem("exps_ready")
        sq_rdy = st.sem("square_ready")
        sum_done = st.sem("head_sum_done")
        ss_rdy = st.sem("clamped_ready")
        root = st.sem("root_ready")
        act_step = st.sem("act_step")
        z_sh = st.sem("z_shifted")
        z_rdy = st.sem("silu_ready")
        stored = st.sem("stored")
        block = ctx.enter_context(nc.Block())
        src = pT[0:4 * C_BR, :].rearrange("(q r) t -> r q t", q=4)
        n_par = 4

        @block.sync
        def _(sp):
            sp.dma_start(blk[:, :], blockones_d).then_inc(cst, 16)
            sp.dma_start(cmask[:, :], chunk_mask_d.broadcast_to([P, N])).then_inc(cst, 16)
            sp.dma_start(lora[:, 1:], pT[4 * C_BR:N_RWKV_IN, :]).then_inc(cst, 16)
            sp.dma_start(mu_l[:, :], mu_lora).then_inc(cst, 16)
            with sp.Fori(0, CT) as j:
                for u in range(2):
                    tiles.load(sp, j, u)
                sp.wait_ge(free, j + 1)
                sp.wait_ge(stored, j * 96 + 96)
                sp.dma_start(raw[:, :, 1:], src[ds(j * P, P), :, :]).then_inc(ld, 16)
                sp.dma_start(par[:, :], columns[ds(j * P, P), :]).then_inc(ld, 16)
                sp.dma_start(up[0:64, :], w_up[:, ds(j * P, P)]).then_inc(ld, 16)
                sp.dma_start(up[64:128, :], a_up[:, ds(j * P, P)]).then_inc(ld, 16)
                for u in range(2, tiles.per):
                    tiles.load(sp, j, u)
                sp.wait_ge(free, j + 2)
                sp.dma_start(ar_d[ds(j * P, P), :, :], ar[:, :, :, :].rearrange("p c w t -> p c (w t)")).then_inc(stored, 16)
                sp.dma_start(bk_d[ds(j * P, P), :, :], bk[:, :, :, :].rearrange("p c w t -> p c (w t)")).then_inc(stored, 16)
                sp.dma_start(v_d[ds(j * P, P), :], sh[:, 2, :]).then_inc(stored, 16)
                sp.dma_start(wc_d[ds(j * P, P), :], wc[:, :]).then_inc(stored, 16)
                sp.dma_start(bonus_d[ds(j * P, P), :], bon[:, :]).then_inc(stored, 16)
                sp.dma_start(sz_d[ds(j * P, P), :], sz).then_inc(stored, 16)
            sp.wait_ge(stored, 96 * (CT + 1))

        @block.scalar
        def _(act):
            act.sem_inc(stored, 96)
            tiles.begin_store(act)
            act.wait_ge(shifted, 1)
            act.activation(lora_t[:, :], lora_s[0:64, :], ACT.Tanh).then_inc(tanhed, 1)
            with act.Fori(0, CT) as j:
                for u in range(2):
                    tiles.store(act, j, u)
                act.wait_ge(ld, j * (16 * n_par) + 16 * n_par)
                act.wait_ge(pre_done, 2 * j + 2)
                act.wait_ge(free, j + 1)
                for h in range(2):
                    act.activation(sgw[:, h * 512:(h + 1) * 512], pre[:, 0, h, :], ACT.Sigmoid, bias=par[:, W0:W0 + 1])
                for h in range(2):
                    last = act.activation(a[:, h * 512:(h + 1) * 512], pre[:, 1, h, :], ACT.Sigmoid, bias=par[:, A0:A0 + 1])
                last.then_inc(sig, 1)
                act.wait_ge(z_sh, j + 1)
                act.activation(sz, sz, ACT.Silu).then_inc(z_rdy, 1)
                act.wait_ge(cum, j + 1)
                act.activation(w_t[:, :], cs[:, :], ACT.Exp, scale=-DECAY)
                act.activation(w_i[:, :], cs[:, :], ACT.Exp, scale=DECAY)
                act.activation(w_p[:, :], diff[:, :], ACT.Exp, scale=-DECAY).then_inc(exps, 1)
                for u in range(2, 4):
                    tiles.store(act, j, u)
                act.wait_ge(ss_rdy, j + 1)
                act.activation(rn[:, :], tmp[:, :], ACT.Sqrt).then_inc(root, 1)
                for u in range(4, tiles.per):
                    tiles.store(act, j, u)
            tiles.end_store(act, CT)

        @block.tensor
        def _(pe):
            tiles.begin_product(pe)
            with pe.Fori(0, CT) as j:
                for u in range(2):
                    tiles.product(pe, j, u)
                pe.wait_ge(cst, 64)
                pe.wait_ge(tanhed, 1)
                pe.wait_ge(ld, j * (16 * n_par) + 16 * n_par)
                pe.wait_ge(free, j + 1)
                for h in range(2):
                    last = pe.matmul(pre[:, 0, h, :], up[0:64, :], lora_t[:, h * 512:(h + 1) * 512], start=True, stop=True)
                last.then_inc(pre_done, 1)
                for h in range(2):
                    last = pe.matmul(pre[:, 1, h, :], up[64:128, :], lora_s[64:128, h * 512:(h + 1) * 512], start=True, stop=True)
                last.then_inc(pre_done, 1)
                for u in range(2, 4):
                    tiles.product(pe, j, u)
                for m in range(2):
                    pe.wait_ge(sq_rdy, 2 * j + m + 1)
                    for h in range(2):
                        last = pe.matmul(sums[:, m, h, :], blk[:, :], sq[:, h * 512:(h + 1) * 512], start=True, stop=True)
                    last.then_inc(sum_done, 1)
                    tiles.product(pe, j, 4 + m)

        @block.vector
        def _(dve):
            dve.sem_inc(free, 1)
            tiles.begin_split(dve)
            c = Steps(dve, step)
            c.then(dve.memset(lora[:, 0:1], 0.0))
            c.then(dve.memset(raw[:, :, 0:1], 0.0))
            dve.wait_ge(cst, 64)
            c.then(dve.tensor_tensor(diff[:, :], lora[:, 0:N], lora[:, 1:], ALU.subtract))
            dve.scalar_tensor_tensor(lora_s[:, :], diff[:, :], mu_l[:, 0:1], lora[:, 1:], ALU.mult, ALU.add).then_inc(shifted, 1)
            dve.wait_ge(shifted, 1)
            PER = 18
            with dve.Fori(0, CT) as j:
                for u in range(2):
                    tiles.split(dve, j, u)
                c = Steps(dve, step, j * PER + 3)
                dve.wait_ge(ld, j * (16 * n_par) + 16 * n_par)
                for q in (3, 0, 1, 2):
                    c.then(dve.tensor_tensor(diff[:, :], raw[:, q, 0:N], raw[:, q, 1:], ALU.subtract))
                    ins = dve.scalar_tensor_tensor(sh[:, q, :], diff[:, :], par[:, MU + q:MU + q + 1], raw[:, q, 1:], ALU.mult, ALU.add)
                    if q == 3:
                        ins.then_inc(z_sh, 1)
                        dve.wait_ge(z_sh, j + 1)
                    else:
                        c.then(ins)
                tiles.split(dve, j, 2)
                r, k, v = sh[:, 0, :], sh[:, 1, :], sh[:, 2, :]
                dve.wait_ge(sig, j + 1)
                c.then(dve.tensor_tensor_scan(cs[:, :], cmask[:, :], sgw[:, :], 0.0, ALU.mult, ALU.add))
                dve.tensor_tensor(diff[:, :], cs[:, :], sgw[:, :], ALU.subtract).then_inc(cum, 1)
                c.then(dve.tensor_scalar(kk[:, :], k, par[:, KK_:KK_ + 1], None, ALU.mult))
                dve.tensor_tensor(sq[:, :], kk[:, :], kk[:, :], ALU.mult).then_inc(sq_rdy, 1)
                tiles.split(dve, j, 3)
                c.then(dve.tensor_scalar(k2[:, :], a[:, :], 1.0, par[:, KA_:KA_ + 1], ALU.subtract, ALU.mult))
                c.then(dve.scalar_tensor_tensor(k2[:, :], k2[:, :], 1.0, k, ALU.add, ALU.mult))
                tiles.split(dve, j, 4)
                dve.wait_ge(sum_done, 2 * j + 1)
                for h in range(2):
                    ins = dve.tensor_scalar(tmp[:, h * 512:(h + 1) * 512], sums[:, 0, h, :], 1e-24, None, ALU.max)
                ins.then_inc(ss_rdy, 1)
                dve.scalar_tensor_tensor(sq[:, :], r, par[:, RK_:RK_ + 1], k2[:, :], ALU.mult, ALU.mult).then_inc(sq_rdy, 1)
                tiles.split(dve, j, 5)
                dve.wait_ge(root, j + 1)
                c.then(dve.reciprocal(rn[:, :], rn[:, :]))
                c.then(dve.tensor_tensor(kk[:, :], kk[:, :], rn[:, :], ALU.mult))
                dve.wait_ge(exps, j + 1)
                dve.tensor_copy(wc[:, :], w_t[:, :].rearrange("p (c t) -> p c t", t=RC)[:, :, RC - 1])
                ch = lambda t: t[:, :].rearrange("p (c t) -> p c t", t=RC)
                c.then(dve.scalar_tensor_tensor(ar[:, :, 0, :], ch(kk), -1.0, ch(w_p), ALU.mult, ALU.mult))
                c.then(dve.tensor_tensor(ar[:, :, 1, :], sh[:, 0, :].rearrange("p (c t) -> p c t", t=RC), ch(w_t), ALU.mult))
                c.then(dve.tensor_tensor(rn[:, :], kk[:, :], a[:, :], ALU.mult))
                c.then(dve.tensor_tensor(bk[:, :, 0, :], ch(rn), ch(w_i), ALU.mult))
                c.then(dve.tensor_tensor(bk[:, :, 1, :], ch(k2), ch(w_i), ALU.mult))
                dve.wait_ge(sum_done, 2 * j + 2)
                dve.wait_ge(z_rdy, j + 1)
                for h in range(2):
                    last = dve.tensor_tensor(bon[:, h * 512:(h + 1) * 512], sums[:, 1, h, :], sh[:, 2, h * 512:(h + 1) * 512], ALU.mult)
                last.then_inc(free, 1)
                assert c.n == PER, c.n


def rwkv_scan(nc, ar_d, bk_d, v_d, wc_d, ident_d, masks_d, yT_d):
    NP = CT
    ROUNDS = 5
    SLOTS = 4
    with ExitStack() as ctx:
        st = Stage(nc, ctx, "scan")
        ident = st.sb("ident", [P, P])
        masks = st.sb("masks", [P, 4, P])
        lower = st.sb("lower", [P, P])
        ar = st.sb("ar", [P, SLOTS, NP, 2, P])
        bk = st.sb("bk", [P, SLOTS, NP, 2, P])
        vb = st.sb("v", [P, SLOTS, NP, P])
        wc = st.sb("wc", [P, NP, RCH])
        S = st.sb("S", [P, 2, NP, P])
        gb = st.sb("gb", [P, 2, NP, 2, P])
        gk = st.sb("gk", [P, 2, NP, 2, P])
        tok = st.sb("tok", [P, 2, NP, 3, P])
        pp = st.sb("p", [P, 2, NP, P])
        n_ = st.sb("n", [P, 2, NP, P])
        nt = st.sb("nt", [P, 2, NP, P])
        rhs = st.sb("rhs", [P, NP, P])
        U = st.sb("U", [P, NP, P])
        yo = st.sb("y", [P, 2, NP, RC])
        bank = st.ps("bank", [P, 8, 512])
        GB_B, GK_B, NT_B, TOK_B, P_B, U_B, Y_B, DS_B = 0, 2, 4, (3, 4, 2), 2, 5, 6, 7

        cst = st.sem("consts_loaded")
        ld = st.sems("chunk_loaded", SLOTS)
        zero = st.sem("zeroed")
        stored = st.sems("y_stored")
        later = range(2, ROUNDS + 1)
        pe = Plan(st.sem("pe_prepared"), [("gb",), ("gk",), ("nT",), ("tok", 0), ("tok", 1), ("tok", 2), ("N", 1), ("T", 1)]
                  + [k for r in later for k in ([("N", r)] if r < ROUNDS else []) + [("T", r), ("P", r - 1)]] + [("P", ROUNDS)])
        dv = Plan(st.sem("dve_prepared"), [("gb",), ("gk",), ("nT",), ("p0",), ("N", 1)]
                  + [k for r in later for k in ([("N", r)] if r < ROUNDS else []) + [("P", r - 1)]] + [("P", ROUNDS)])
        ac = Plan(st.sem("act_prepared"), [("tok", m) for m in range(3)] + [("T", r) for r in range(1, ROUNDS + 1)])
        pr = Plan(st.sem("pe_recurred"), [("rhs",), ("U",), ("dS",), ("Y",)])
        dr = Plan(st.sem("dve_recurred"), [("rhs",), ("sum",), ("S",)])
        ar_ = Plan(st.sem("act_recurred"), [("U",), ("Y",)])
        block = ctx.enter_context(nc.Block())
        N_LD = 2 * 5
        bv = lambda b, n=P: bank[:, b, :].rearrange("p (a t) -> p a t", t=n)
        PLACES = 5
        place_of = lambda *key: -(-(pe.value[key] - 1) * PLACES // pe.n) - 1

        def chunks(eng, prepare, recur):
            Beside(prepare(0, 0)).upto(PLACES)

            def turn(first, last):
                for q in range(SLOTS):
                    if last and q == SLOTS - 1:
                        recur(first + q, q, lambda place: None)
                    else:
                        beside = Beside(prepare(first + q + 1, (q + 1) % SLOTS))
                        recur(first + q, q, beside.upto)
                        beside.upto(PLACES)

            with eng.Fori(0, RCH // SLOTS - 1) as i:
                turn(SLOTS * i, False)
            turn(RCH - SLOTS, True)

        @block.sync
        def _(sp):
            sp.dma_start(ident[:, :], ident_d).then_inc(cst, 16)
            sp.dma_start(masks[:, :, :], masks_d[:, 0:4 * P].rearrange("p (a t) -> p a t", a=4)).then_inc(cst, 16)
            sp.dma_start(wc[:, :, :], wc_d.rearrange("(p c) n -> c p n", c=P)).then_inc(cst, 16)
            sp.dma_start(lower[:, :], masks_d[:, 4 * P:5 * P]).then_inc(cst, 16)
            sp.wait_ge(zero, 1)
            ar_v = ar_d.rearrange("(p c) n (w t) -> c n p w t", c=P, w=2)
            bk_v = bk_d.rearrange("(p c) n (w t) -> c n p w t", c=P, w=2)
            v_v = v_d.rearrange("(p c) (n t) -> c n p t", c=P, t=RC)

            def load(c, q):
                for x in range(2):
                    h = slice(64 * x, 64 * x + 64)
                    for dst, src in ((ar, ar_v), (bk, bk_v)):
                        for w in range(2):
                            sp.dma_start(dst[h, q, :, w, h], src[h, ds(c, 1), :, w, :].rearrange("c n p t -> c (n p) t")).then_inc(ld[q], 16)
                    sp.dma_start(vb[h, q, :, h], v_v[h, ds(c, 1), :, :].rearrange("c n p t -> c (n p) t")).then_inc(ld[q], 16)

            for q in range(SLOTS):
                load(q, q)
            with sp.Fori(0, RCH // SLOTS - 1) as i:
                for q in range(SLOTS):
                    pr.wait_turn(sp, SLOTS * i + (q + 1))
                    load(SLOTS * i + (SLOTS + q), q)

        @block.tensor
        def _(t):
            pe.begin(t)
            pr.begin(t)
            t.wait_ge(cst, 64)
            t.wait_ge(zero, 1)

            def prepare(c, q):
                s = q % 2
                yield place_of("gb")
                t.wait_ge(ld[q], (c - q) * (16 * N_LD // SLOTS) + 16 * N_LD)
                dv.wait_turn(t, c)
                ac.wait_turn(t, c)
                for x, b, src in (("gb", GB_B, 0), ("gk", GK_B, 1)):
                    if src:
                        yield place_of(x)
                    for p in range(NP):
                        last = t.matmul(bank[:, b + p // 2, (p % 2) * 256:(p % 2) * 256 + 256], bk[:, q, p, src, :],
                                        ar[:, q, p, :, :].rearrange("c w t -> c (w t)"), start=True, stop=True)
                    pe.step(last, x)
                yield place_of("nT")
                for p in range(NP):
                    last = t.matmul(bv(NT_B)[:, p, :], ar[:, q, p, 0, :], bk[:, q, p, 0, :], start=True, stop=True)
                pe.step(last, "nT")
                for m in range(3):
                    yield place_of("tok", m)
                    if m < 2:
                        dv.wait(t, c, ("gk", "nT")[m])
                    for p in range(NP):
                        src = bk[:, q, p, m, :] if m < 2 else vb[:, q, p, :]
                        last = t.transpose(bv(TOK_B[m])[:, p, :], src, ident[:, :])
                    pe.step(last, "tok", m)

                def product(r):
                    yield place_of("P", r)
                    if r > 1:
                        dv.wait(t, c, "P", r - 1)
                    else:
                        dv.wait(t, c, "p0")
                        ac.wait(t, c, "tok", 2)
                    ac.wait(t, c, "T", r)
                    for p in range(NP):
                        last = t.matmul(bv(P_B)[:, p, :], nt[:, r % 2, p, :], pp[:, s, p, :], start=True, stop=True)
                    pe.step(last, "P", r)

                for r in range(1, ROUNDS + 1):
                    o = (r + 1) % 2
                    yield place_of("N" if r < ROUNDS else "T", r)
                    if r > 1:
                        dv.wait(t, c, "N", r - 1)
                        ac.wait(t, c, "T", r - 1)
                    else:
                        dv.wait(t, c, "nT")
                    cur = (lambda p: gb[:, s, p, 0, :]) if r == 1 else (lambda p: n_[:, o, p, :])
                    if r < ROUNDS:
                        for p in range(NP):
                            last = t.matmul(bv(0)[:, p, :], nt[:, o, p, :], cur(p), start=True, stop=True)
                        pe.step(last, "N", r)
                        yield place_of("T", r)
                    for p in range(NP):
                        last = t.matmul(bv(1)[:, p, :], cur(p), nt[:, o, p, :], start=True, stop=True)
                    pe.step(last, "T", r)
                    if r > 1:
                        yield from product(r - 1)
                yield from product(ROUNDS)

            def recur(c, q, beside):
                s = q % 2
                dv.wait(t, c, "P", ROUNDS)
                ac.wait(t, c, "tok", 2)
                dr.wait_turn(t, c)
                ar_.wait_turn(t, c)
                for p in range(NP):
                    t.matmul(bv(U_B)[:, p, :], ar[:, q, p, 0, :], S[:, s, p, :], start=True, stop=False)
                    last = t.matmul(bv(U_B)[:, p, :], gk[:, s, p, 0, :], tok[:, s, p, 2, :], start=False, stop=True)
                pr.step(last, "rhs")
                beside(0)
                dr.wait(t, c, "rhs")
                for p in range(NP):
                    last = t.matmul(bv(U_B)[:, p, :], pp[:, s, p, :], rhs[:, p, :], start=True, stop=True)
                pr.step(last, "U")
                beside(1)
                ar_.wait(t, c, "U")
                for p in range(NP):
                    o = bv(DS_B)[:, p, :]
                    t.matmul(o, tok[:, s, p, 0, :], U[:, p, :], start=True, stop=False)
                    last = t.matmul(o, tok[:, s, p, 1, :], tok[:, s, p, 2, :], start=False, stop=True)
                pr.step(last, "dS")
                beside(2)
                for p in range(NP):
                    o = bv(Y_B)[:, p, :]
                    t.matmul(o, S[:, s, p, :], ar[:, q, p, 1, :], start=True, stop=False)
                    t.matmul(o, U[:, p, :], gb[:, s, p, 1, :], start=False, stop=False)
                    last = t.matmul(o, tok[:, s, p, 2, :], gk[:, s, p, 1, :], start=False, stop=True)
                pr.step(last, "Y")
                beside(3)

            chunks(t, prepare, recur)

        @block.vector
        def _(v):
            dv.begin(v)
            dr.begin(v)
            for b in (ar, bk):
                v.memset(b[:, :, :, :, :].rearrange("c s p w t -> c (s p w t)"), 0.0)
            v.memset(vb[:, :, :, :].rearrange("c s p t -> c (s p t)"), 0.0)
            v.memset(S[:, 0, :, :], 0.0)
            v.drain().then_inc(zero, 1)
            v.wait_ge(cst, 64)

            def prepare(c, q):
                s = q % 2
                for x, b, g in (("gb", GB_B, gb), ("gk", GK_B, gk)):
                    yield place_of(x)
                    if x == "gb" and (not isinstance(c, int) or c > 1):
                        pr.wait_turn(v, c - 1)
                    pe.wait(v, c, x)
                    for h in range(2):
                        last = v.tensor_tensor(g[:, s, 2 * h:2 * h + 2, :, :].rearrange("c p w t -> c (p w) t"),
                                               bv(b + h), masks[:, :, :], ALU.mult)
                    dv.step(last, x)
                yield place_of("nT")
                pe.wait(v, c, "nT")
                dv.step(v.tensor_tensor(nt[:, 0, :, :], bv(NT_B), lower[:, :].unsqueeze(1).broadcast_to([P, NP, P]), ALU.mult), "nT")
                dv.wait(v, c, "gb")
                dv.step(v.tensor_tensor(pp[:, s, :, :], gb[:, s, :, 0, :], ident[:, :].unsqueeze(1).broadcast_to([P, NP, P]), ALU.add), "p0")

                def add(r):
                    yield place_of("P", r)
                    pe.wait(v, c, "P", r)
                    dv.step(v.tensor_tensor(pp[:, s, :, :], pp[:, s, :, :], bv(P_B), ALU.add), "P", r)

                for r in range(1, ROUNDS + 1):
                    if r < ROUNDS:
                        yield place_of("N", r)
                        pe.wait(v, c, "N", r)
                        dv.step(v.tensor_copy(n_[:, r % 2, :, :], bv(0)), "N", r)
                    if r > 1:
                        yield from add(r - 1)
                yield from add(ROUNDS)

            def recur(c, q, beside):
                s = q % 2
                pr.wait(v, c, "rhs")
                dr.step(v.tensor_copy(rhs[:, :, :], bv(U_B)), "rhs")
                beside(0)
                beside(1)
                pr.wait(v, c, "dS")
                dr.step(v.tensor_tensor(S[:, 1 - s, :, :], S[:, s, :, :], bv(DS_B), ALU.add), "sum")
                dr.wait(v, c, "sum")
                dr.step(v.tensor_tensor(S[:, 1 - s, :, :], S[:, 1 - s, :, :], wc[:, :, ds(c, 1)].broadcast_to([P, NP, P]), ALU.mult), "S")
                beside(2)
                beside(3)

            chunks(v, prepare, recur)

        @block.scalar
        def _(a):
            ac.begin(a)
            ar_.begin(a)
            for q in stored:
                a.sem_inc(q, 32)
            a.wait_ge(cst, 64)
            y_v = yT_d.rearrange("(p c) (n t) -> c n p t", c=P, t=RC)

            def prepare(c, q):
                for m in range(3):
                    yield place_of("tok", m)
                    if m == 0 and (not isinstance(c, int) or c > 1):
                        pr.wait_turn(a, c - 1)
                    pe.wait(a, c, "tok", m)
                    ac.step(a.activation(tok[:, q % 2, :, m, :], bv(TOK_B[m]), ACT.Copy), "tok", m)
                for r in range(1, ROUNDS + 1):
                    yield place_of("T", r)
                    pe.wait(a, c, "T", r)
                    ac.step(a.activation(nt[:, r % 2, :, :], bv(1), ACT.Copy), "T", r)

            def recur(c, q, beside):
                s = q % 2
                beside(0)
                pr.wait(a, c, "U")
                ar_.step(a.activation(U[:, :, :], bv(U_B), ACT.Copy), "U")
                beside(1)
                beside(2)
                pr.wait(a, c, "Y")
                a.wait_ge(stored[s], (c - s) * 16 + 32)
                for x in range(2):
                    h = slice(64 * x, 64 * x + 64)
                    last = a.activation(yo[h, s, :, :], bv(Y_B)[h, :, h], ACT.Copy)
                ar_.step(last, "Y")
                ar_.wait(a, c, "Y")
                for x in range(2):
                    h = slice(64 * x, 64 * x + 64)
                    a.dma_start(y_v[h, ds(c, 1), :, :].rearrange("c n p t -> c (n p) t"), yo[h, s, :, :]).then_inc(stored[s], 16)
                beside(3)

            chunks(a, prepare, recur)
            for q in stored:
                a.wait_ge(q, 32 * (RCH // 2 + 1))


def rwkv_finish(nc, yT_d, bonus_d, sz_d, gn_w, gn_b, blockmean_d, yaT, project):
    with ExitStack() as ctx:
        st = Stage(nc, ctx, "fin")
        tiles = ProjectBeside(st, *project)
        N = SEQ
        blk = st.sb("blockmean", [P, P])
        y = st.sb("y", [P, 2, N])
        bon = st.sb("bonus", [P, 2, N])
        sz = st.sb("silu_z", [P, 2, N])
        par = st.sb("par", [P, 2, CT])
        d = st.sb("d", [P, 2, N])
        sq = st.sb("sq", [P, 2, N])
        rn = st.sb("rn", [P, 2, N])
        o = st.sb("o", [P, 2, N])
        mean = st.ps("mean", [P, 2, 2, 512])
        var = mean
        cst = st.sem("consts_loaded")
        ld = st.sems("loaded")
        mean_rdy = st.sem("mean_ready")
        d_rdy = st.sem("deviation_ready")
        sq_rdy = st.sem("square_ready")
        var_rdy = st.sem("var_ready")
        ve_rdy = st.sem("var_eps_ready")
        root = st.sem("root_ready")
        step = st.sem("dve_step")
        out_rdy = st.sem("out_ready")
        stored = st.sems("stored")
        block = ctx.enter_context(nc.Block())

        @block.sync
        def _(sp):
            sp.dma_start(blk[:, :], blockmean_d).then_inc(cst, 16)
            sp.dma_start(par[:, 0, :], gn_w).then_inc(cst, 16)
            sp.dma_start(par[:, 1, :], gn_b).then_inc(cst, 16)
            for j in range(CT):
                s, rows = j % 2, slice(j * P, (j + 1) * P)
                for u in range(tiles.per):
                    tiles.load(sp, j, u)
                if j >= 2:
                    sp.wait_ge(out_rdy, j - 1)
                for dst, src in ((y, yT_d), (bon, bonus_d), (sz, sz_d)):
                    sp.dma_start(dst[:, s, :], src[rows, :]).then_inc(ld[s], 16)

        @block.tensor
        def _(pe):
            tiles.begin_product(pe)
            pe.wait_ge(cst, 48)
            for j in range(CT):
                s = j % 2
                for u in range(2):
                    tiles.product(pe, j, u)
                pe.wait_ge(ld[s], 48 * (j // 2 + 1))
                if j >= 2:
                    pe.wait_ge(out_rdy, j - 1)
                for h in range(2):
                    last = pe.matmul(mean[:, s, h, :], blk[:, :], y[:, s, h * 512:(h + 1) * 512], start=True, stop=True)
                last.then_inc(mean_rdy, 1)
                tiles.product(pe, j, 2)
                pe.wait_ge(sq_rdy, j + 1)
                for h in range(2):
                    last = pe.matmul(var[:, s, h, :], blk[:, :], sq[:, s, h * 512:(h + 1) * 512], start=True, stop=True)
                last.then_inc(var_rdy, 1)
                tiles.product(pe, j, 3)

        @block.scalar
        def _(act):
            tiles.begin_store(act)
            for j in range(CT):
                s = j % 2
                for u in range(2):
                    tiles.store(act, j, u)
                act.wait_ge(d_rdy, j + 1)
                act.activation(sq[:, s, :], d[:, s, :], ACT.Square).then_inc(sq_rdy, 1)
                tiles.store(act, j, 2)
                act.wait_ge(ve_rdy, j + 1)
                act.activation(rn[:, s, :], rn[:, s, :], ACT.Sqrt).then_inc(root, 1)
                tiles.store(act, j, 3)
                act.wait_ge(out_rdy, j + 1)
                act.dma_start(yaT[j * P:(j + 1) * P, :], o[:, s, :]).then_inc(stored[s], 16)
            for q in stored:
                act.wait_ge(q, 16 * (CT // 2))
            tiles.end_store(act, CT)

        @block.vector
        def _(dve):
            tiles.begin_split(dve)
            dve.wait_ge(cst, 48)
            c = Steps(dve, step)
            tiles.split(dve, 0, 0)
            for j in range(CT):
                s = j % 2
                tiles.split(dve, j, 1)
                dve.wait_ge(mean_rdy, j + 1)
                for h in range(2):
                    last = dve.tensor_tensor(d[:, s, h * 512:(h + 1) * 512], y[:, s, h * 512:(h + 1) * 512], mean[:, s, h, :], ALU.subtract)
                last.then_inc(d_rdy, 1)
                tiles.split(dve, j, 2)
                dve.wait_ge(var_rdy, j + 1)
                for h in range(2):
                    last = dve.tensor_scalar(rn[:, s, h * 512:(h + 1) * 512], var[:, s, h, :], GN_EPS, None, ALU.add)
                last.then_inc(ve_rdy, 1)
                tiles.split(dve, j, 3)
                if j < CT - 1:
                    tiles.split(dve, j + 1, 0)
                dve.wait_ge(root, j + 1)
                c.then(dve.reciprocal(rn[:, s, :], rn[:, s, :]))
                c.then(dve.tensor_tensor(d[:, s, :], d[:, s, :], rn[:, s, :], ALU.mult))
                c.then(dve.tensor_scalar(d[:, s, :], d[:, s, :], par[:, 0, j:j + 1], par[:, 1, j:j + 1], ALU.mult, ALU.add))
                c.then(dve.tensor_tensor(d[:, s, :], d[:, s, :], bon[:, s, :], ALU.add))
                if j >= 2:
                    dve.wait_ge(stored[s], 16 * (j // 2))
                dve.tensor_tensor(o[:, s, :], d[:, s, :], sz[:, s, :], ALU.mult).then_inc(out_rdy, 1)


def gate_merge_out(nc, name, n_tok, rows, branches, gates, w_out, post_gain, resid_in, resid_out, neghalf_d, copy=None):
    NB = len(branches)
    PART = 2
    pcs = pieces(n_tok)
    NPC = len(pcs)
    n_tiles = n_tok // rows
    kts = [w.shape[0] // P for w, _ in branches]
    with ExitStack() as ctx:
        st = Stage(nc, ctx, name)
        KY = sum(kts)
        y_hi = st.sb("y_hi", [P, KY, n_tok], F32R)
        y_lo = st.sb("y_lo", [P, KY, n_tok], F32R)
        spare = st.sb("spare", [P, 2, PART, n_tok])
        more = st.sb("more", [P, 2, D])
        wb = st.sb("wb", [P, 2, max(kts), P])
        wb_hi = st.sb("wb_hi", [P, 2, max(kts), P], F32R)
        wb_lo = st.sb("wb_lo", [P, 2, max(kts), P], F32R)
        gate = st.sb("gate", [P, 2, n_tok])
        tmp = st.sb("tmp", [P, n_tok])
        acc = st.sb("acc", [P, n_tok])
        mT = st.sb("mT", [P, KT, n_tok])
        neghalf = st.sb("neghalf", [P, 1])
        ssq = st.sb("ssq", [P, 2, 2])
        ms = st.sb("ms", [P, 2])
        rstd = st.sb("rstd", [P, 2])
        flat = lambda z: z[:, :, :].rearrange("p k t -> p (k t)")
        wo_hi = flat(y_hi)[:, 0:KT * D].rearrange("p (k d) -> p k d", k=KT)
        wo_lo = flat(y_lo)[:, 0:KT * D].rearrange("p (k d) -> p k d", k=KT)
        stg_at = KT * D
        stg_hi, stg_lo = (flat(y)[:, stg_at:stg_at + 2 * KT * rows].rearrange("p (s k r) -> p s k r", s=2, k=KT) for y in (y_hi, y_lo))
        wo_raw = [spare[:, k // PART, k % PART, 0:D] for k in range(2 * PART)] + [more[:, k, :] for k in range(2)]
        wo_raw = [wo_raw[k % len(wo_raw)] for k in range(KT)]
        res = st.sb("res", [P, 2, D])
        gain = st.sb("gain", [P, D]) if post_gain is not None else None
        bank = st.ps("bank", [P, 8, 512])

        parts = [(n, at, k) for n in range(NB) for at, k in [(sum(kts[:n]) + a, PART) for a in range(0, kts[n], PART)]]
        upto = [max(i + 1 for i, q in enumerate(parts) if q[0] == n) for n in range(NB)]
        y_ld = st.sems("y_loaded")
        y_split = st.sem("y_split")
        y_hi_rdy = st.sem("y_hi_ready")
        wb_hi_rdy = st.sem("unit_weights_high_ready")
        wb_split = st.sem("unit_weights_split")
        wo_hi_rdy = st.sem("w_out_high_ready")
        wo_split = st.sem("w_out_split")
        gain_ld = st.sem("gain_loaded")
        neghalf_ld = st.sem("neghalf_loaded")
        stg_hi_rdy = st.sem("staged_high_ready")
        wo_ld = st.sems("w_out_loaded", KT)
        wb_ld = st.sems("unit_weights_loaded")
        gate_ld = st.sems("unit_gate_loaded")
        sig = st.sem("sigmoid_ready")
        prod = st.sem("product_done")
        used = st.sem("unit_used")
        step = st.sem("sum_step")
        o_step = st.sem("out_step")
        merged = st.sem("merged_tile_ready")
        staged = st.sem("staged")
        o_done = st.sem("out_product_done")
        r_ld = st.sems("resid_loaded")
        ssq_rdy = st.sem("ssq_ready")
        ms_rdy = st.sem("ms_ready")
        rstd_rdy = st.sem("rstd_ready")
        o_rdy = st.sem("out_ready")
        stored = st.sems("out_stored")
        copied = st.sem("copied")
        block = ctx.enter_context(nc.Block())
        M = 2
        UPT = M * NB
        k0 = [sum(kts[:n]) for n in range(NB)]
        units = [(m, n) for m in range(M) for n in range(NB)]
        n_units = KT // M * UPT

        @block.sync
        def _(sp):
            if copy:
                sp.dma_start(*copy).then_inc(copied, 16)

            def load_weights(i, u):
                m, n = units[u % UPT]
                sp.wait_ge(wb_split, i * UPT + u + 1)
                sp.dma_start(wb[:, u % 2, 0:kts[n], :], branches[n][0].rearrange("(k p) d -> p k d", p=P)
                             [:, :, ds((i * (M * P) + m * P) if u < UPT else 0, P)]).then_inc(wb_ld[u % 2], 16)

            if post_gain is not None:
                sp.dma_start(gain[:, :], post_gain.rearrange("(a d) -> a d", a=1).broadcast_to([P, D])).then_inc(gain_ld, 16)
            sp.dma_start(neghalf[:, :], neghalf_d).then_inc(neghalf_ld, 16)
            with sp.Fori(0, KT // M) as i:
                for u, (m, n) in enumerate(units):
                    load_weights(i, u)
                    sp.wait_ge(used, i * UPT + u + 1)
                    sp.dma_start(gate[:, u % 2, :], gates[n][ds(i * (M * P) + m * P, P), :]).then_inc(gate_ld[u % 2], 16)
            load_weights(KT // M - 1, UPT)
            sp.wait_ge(y_split, len(parts))
            for k in range(KT):
                if k >= KT - 2:
                    sp.wait_ge(wo_split, k - (KT - 2) + 1)
                sp.dma_start(wo_raw[k], w_out[k * P:(k + 1) * P, :]).then_inc(wo_ld[k], 16)
            with sp.Fori(0, n_tiles // 2) as i:
                for s in range(2):
                    sp.wait_ge(stored[s], i * 16 + 16)
                    sp.dma_start(res[:rows, s, :], resid_in[ds(i * (2 * rows) + s * rows, rows), :]).then_inc(r_ld[s], 16)
            if copy:
                sp.wait_ge(copied, 16)

        @block.tensor
        def _(pe):
            pe.sem_inc(prod, 2)
            with pe.Fori(0, KT // M) as i:
                for u, (m, n) in enumerate(units):
                    s = u % 2
                    pe.wait_ge(wb_split, i * UPT + u + 3)
                    pe.wait_ge(y_split, upto[n])
                    pe.wait_ge(used, i * UPT + u + 1)
                    for c, (a, w) in enumerate(pcs):
                        for k in range(kts[n]):
                            for z, (w_, y_) in enumerate(((wb_hi, y_hi), (wb_hi, y_lo), (wb_lo, y_hi))):
                                last = pe.matmul(bank[:, 4 * s + c, 0:w], w_[:, s, k, :], y_[:, k0[n] + k, a:a + w],
                                                 start=(k == 0 and z == 0), stop=(k == kts[n] - 1 and z == 2))
                    last.then_inc(prod, 1)
            pe.wait_ge(used, KT // M * UPT + 2)
            with pe.Fori(0, n_tiles // 2) as i:
                for s in range(2):
                    pe.wait_ge(staged, 2 * i + s + 3)
                    pe.wait_ge(o_rdy, 2 * i + s + 1)
                    for c in range(2):
                        for k in range(KT):
                            if c == 0:
                                pe.wait_ge(wo_split, k + 1)
                            for z, (m_, w_) in enumerate(((stg_hi, wo_hi), (stg_hi, wo_lo), (stg_lo, wo_hi))):
                                last = pe.matmul(bank[:rows, 4 * s + c, :], m_[:, s, k, :], w_[:, k, c * 512:(c + 1) * 512],
                                                 start=(k == 0 and z == 0), stop=(k == KT - 1 and z == 2))
                    last.then_inc(o_done, 1)

        @block.scalar
        def _(act):
            for q in stored:
                act.sem_inc(q, 16)
            for j, (n, at, k) in enumerate(parts):
                if j >= 2:
                    act.wait_ge(y_split, j - 1)
                y_at = (at - k0[n]) * P
                act.dma_start(spare[:, j % 2, 0:k, :], branches[n][1][y_at:y_at + k * P, :].rearrange("(k p) t -> p k t", p=P)).then_inc(y_ld[j % 2], 16)
            with act.Fori(0, KT // M) as i:
                for u, (m, n) in enumerate(units):
                    s = u % 2
                    act.wait_ge(gate_ld[s], i * (8 * UPT) + 16 * (u // 2 + 1))
                    act.activation(gate[:, s, :], gate[:, s, :], ACT.Sigmoid).then_inc(sig, 1)
            with act.Fori(0, n_tiles // 2) as i:
                for s in range(2):
                    if post_gain is not None:
                        act.wait_ge(o_done, 2 * i + s + 1)
                        act.wait_ge(o_rdy, 2 * i + s + 1)
                        for c in range(2):
                            last = act.activation(bank[:rows, 4 * s + 2 + c, :], bank[:rows, 4 * s + c, :], ACT.Square,
                                                  accum_out=ssq[:rows, s, c:c + 1])
                        last.then_inc(ssq_rdy, 1)
                    act.wait_ge(o_rdy, 2 * i + s + 3)
                    act.dma_start(resid_out[ds(i * (2 * rows) + s * rows, rows), :], res[:rows, s, :]).then_inc(stored[s], 16)
            for q in stored:
                act.wait_ge(q, 16 * (n_tiles // 2 + 1))

        @block.gpsimd
        def _(pool):
            pool.wait_ge(neghalf_ld, 16)
            if post_gain is not None:
                with pool.Fori(0, n_tiles // 2) as i:
                    for s in range(2):
                        pool.wait_ge(ms_rdy, 2 * i + s + 1)
                        pool.tensor_tensor(rstd[:rows, s:s + 1], ms[:rows, s:s + 1], neghalf[:rows, :], ALU.pow).then_inc(rstd_rdy, 1)

        @block.vector
        def _(dve):
            dve.sem_inc(used, 2)
            dve.sem_inc(o_rdy, 2)
            dve.sem_inc(staged, 2)
            dve.sem_inc(wb_split, 2)
            PER = M * (NB - 2)

            def split_unit(i, u):
                s, k = u % 2, kts[units[u % UPT][1]]
                dve.wait_ge(wb_ld[s], i * (8 * UPT) + 16 * (u // 2 + 1))
                dve.wait_ge(prod, i * UPT + u + 1)
                dve.tensor_copy(wb_hi[:, s, 0:k, :], wb[:, s, 0:k, :]).then_inc(wb_hi_rdy, 1)
                dve.wait_ge(wb_hi_rdy, i * UPT + u + 1)
                dve.tensor_tensor(wb_lo[:, s, 0:k, :], wb[:, s, 0:k, :], wb_hi[:, s, 0:k, :].bitcast(F32), ALU.subtract).then_inc(wb_split, 1)

            split_unit(0, 0)
            for n, (_, at, k) in enumerate(parts):
                dve.wait_ge(y_ld[n % 2], 16 * (n // 2) + 16)
                dve.tensor_copy(y_hi[:, at:at + k, :], spare[:, n % 2, 0:k, :]).then_inc(y_hi_rdy, 1)
                dve.wait_ge(y_hi_rdy, n + 1)
                dve.tensor_tensor(y_lo[:, at:at + k, :], spare[:, n % 2, 0:k, :], y_hi[:, at:at + k, :].bitcast(F32), ALU.subtract).then_inc(y_split, 1)
            with dve.Fori(0, KT // M) as i:
                c = Steps(dve, step, i * PER)
                for u, (m, n) in enumerate(units):
                    s = u % 2
                    split_unit(i, u + 1)
                    dve.wait_ge(prod, i * UPT + u + 3)
                    dve.wait_ge(sig, i * UPT + u + 1)
                    dst = acc if n == 0 else tmp
                    for q, (a, w) in enumerate(pcs):
                        ins = dve.tensor_tensor(dst[:, a:a + w], gate[:, s, a:a + w], bank[:, 4 * s + q, 0:w], ALU.mult)
                    ins.then_inc(used, 1)
                    dve.wait_ge(used, i * UPT + u + 3)
                    if n == NB - 1:
                        dve.tensor_tensor(mT[:, ds(i * M + m, 1), :].rearrange("p a t -> p (a t)"), acc[:, :], tmp[:, :],
                                          ALU.add).then_inc(merged, 1)
                        dve.wait_ge(merged, i * M + m + 1)
                    elif n:
                        c.then(dve.tensor_tensor(acc[:, :], acc[:, :], tmp[:, :], ALU.add))
                assert c.n == PER, c.n
            dve.wait_ge(prod, n_units + 2)

            def stage(i, s):
                at = mT[:, :, ds(i * (2 * rows) + s * rows, rows)]
                dve.tensor_copy(stg_hi[:, s, :, :], at).then_inc(stg_hi_rdy, 1)
                dve.wait_ge(stg_hi_rdy, 2 * i + s + 1)
                dve.tensor_tensor(stg_lo[:, s, :, :], at, stg_hi[:, s, :, :].bitcast(F32), ALU.subtract).then_inc(staged, 1)

            stage(0, 0)
            for k in range(KT):
                dve.wait_ge(wo_ld[k], 16)
                dve.tensor_copy(wo_hi[:, k, :], wo_raw[k]).then_inc(wo_hi_rdy, 1)
                dve.wait_ge(wo_hi_rdy, k + 1)
                dve.tensor_tensor(wo_lo[:, k, :], wo_raw[k], wo_hi[:, k, :].bitcast(F32), ALU.subtract).then_inc(wo_split, 1)
            stage(0, 1)
            if post_gain is not None:
                dve.wait_ge(gain_ld, 16)

            def finish(i, s):
                dve.wait_ge(r_ld[s], i * 16 + 16)
                b = lambda c_: bank[:rows, 4 * s + c_, :]
                rs = lambda c_: res[:rows, s, c_ * 512:(c_ + 1) * 512]
                if post_gain is None:
                    dve.wait_ge(o_done, 2 * i + s + 1)
                    for c_ in range(2):
                        last = dve.tensor_tensor(rs(c_), rs(c_), b(c_), ALU.add)
                else:
                    c = Steps(dve, o_step, 4 * i + 2 * s)
                    dve.wait_ge(ssq_rdy, 2 * i + s + 1)
                    c.then(dve.tensor_tensor(ms[:rows, s:s + 1], ssq[:rows, s, 0:1], ssq[:rows, s, 1:2], ALU.add))
                    dve.tensor_scalar(ms[:rows, s:s + 1], ms[:rows, s:s + 1], 1.0 / D, EPS, ALU.mult, ALU.add).then_inc(ms_rdy, 1)
                    dve.wait_ge(rstd_rdy, 2 * i + s + 1)
                    for c_ in range(2):
                        last = dve.scalar_tensor_tensor(tmp[:rows, c_ * 512:(c_ + 1) * 512], b(c_), rstd[:rows, s:s + 1],
                                                        gain[:rows, c_ * 512:(c_ + 1) * 512], ALU.mult, ALU.mult)
                    c.then(last)
                    last = dve.tensor_tensor(res[:rows, s, :], res[:rows, s, :], tmp[:rows, 0:D], ALU.add)
                last.then_inc(o_rdy, 1)

            turns = n_tiles // 2
            with dve.Fori(0, turns - 1) as i:
                for s in range(2):
                    finish(i, s)
                    stage(i + 1, s)
            for s in range(2):
                finish(turns - 1, s)


def qkv_and_fourier(nc, p2T, taps_d, ones_d, eps_d, qT_d, kT_d, vT_d, chan_d, seq_d, yfT):
    with ExitStack() as ctx:
        st = Stage(nc, ctx, "qkv")
        N, W, R = LEN, taps_d.shape[1], ROWS
        pad = W // 2
        pcs = pieces(N)
        half = N // 2 + 1
        half_pcs = [(i * (HALF_W // 3), HALF_W // 3) for i in range(3)]
        B_AT = 256
        G = F_W // P
        PER = HEADS // G
        ones = st.sb("ones", [P, P])
        eps = st.sb("eps", [P, 2])
        x = st.sb("x", [P, PER, 3, N + 2 * pad])
        taps = st.sb("taps", [P, PER, 3, W])
        y = st.sb("y", [P, 3, 2, N])
        s = st.sb("s", [P, 3, N])
        sq = st.sb("sq", [P, 2, N])
        rn = st.sb("rn", [P, 2, N])
        o = st.sb("o", [P, 2, N])
        chan = st.sb("chan", [P, 2 * P])
        seq = st.sb("seq", [R, 2, NCH, HALF_W])
        f = st.sb("f", [P, N])
        z = st.sb("z", [R, NCH, 2, P])
        ya = st.sb("ya", [P, HALF_W])
        yf = st.sb("yf", [P, N])
        bank = st.ps("bank", [P, 8, 512])
        Z_B, Y_B, S_B = 0, 2, 5
        cst = st.sem("consts_loaded")
        ld = st.sems("head_loaded", PER)
        f_ld = st.sem("group_loaded")
        x_used = st.sem("x_used")
        cst_seq = st.sem("sines_loaded")
        pool_turn = st.sem("pool_turn")
        zero = st.sem("padding_zeroed")
        stored = st.sem("stored")
        f_stored = st.sem("yf_stored")
        dv = Plan(st.sem("dve_step"), [("conv", q, k) for q in range(3) for k in range(W)] + [("out", 0), ("out", 1)])
        ac = Plan(st.sem("act_step"), [("silu", 0), ("square", 0), ("silu", 1), ("square", 1), ("ln", 0), ("root", 0), ("silu", 2),
                                       ("ln", 1), ("root", 1)])
        pp = Plan(st.sem("sums_step"), [("sum", 0), ("sum", 1)])
        pz = Plan(st.sem("fourier_step"), [("z", c) for c in range(NCH // 2)] + [("y",)])
        az = Plan(st.sem("fourier_copy"), [("z", c) for c in range(NCH // 2)] + [("y",)])
        dy = Plan(st.sem("fourier_sum"), [("y",)])
        block = ctx.enter_context(nc.Block())
        src = p2T[QKV_AT:Z_AT, :].rearrange("(q r) t -> r q t", q=3)
        tp = taps_d.rearrange("(q r) w -> r q w", q=3)

        @block.sync
        def _(sp):
            sp.dma_start(ones[:, :], ones_d).then_inc(cst, 16)
            sp.dma_start(eps[:, :], eps_d).then_inc(cst, 16)
            sp.dma_start(chan[:, :], chan_d).then_inc(cst, 16)
            with sp.Fori(0, G) as g:
                for u in range(PER):
                    sp.wait_ge(x_used, PER * g + u + 1)
                    sp.dma_start(x[:, u, :, pad:pad + N], src[ds(g * (PER * P) + u * P, P), :, :]).then_inc(ld[u], 16)
                    sp.dma_start(taps[:, u, :, :], tp[ds(g * (PER * P) + u * P, P), :, :]).then_inc(ld[u], 16)

        @block.gpsimd
        def _(p):
            for m in range(2):
                p.dma_start(seq[:, m, :, :], seq_d[m].rearrange("(c t) u -> t c u", t=R)).then_inc(cst_seq, 16)
            with p.Fori(0, G) as g:
                pz.wait_turn(p, g)
                p.sem_inc(pool_turn, 1)
                p.dma_start(f[:, :], p2T[ds(g * P, P), :]).then_inc(f_ld, 16)

        @block.vector
        def _(v):
            dv.begin(v)
            dy.begin(v)
            v.sem_inc(x_used, PER)
            v.memset(x[:, :, :, 0:pad], 0.0)
            v.memset(x[:, :, :, pad + N:], 0.0).then_inc(zero, 1)
            v.wait_ge(zero, 1)
            with v.Fori(0, G) as g:
                for u in range(PER):
                    h = PER * g + u
                    v.wait_ge(ld[u], g * 32 + 32)
                    for q in range(3):
                        for k in range(W):
                            if k:
                                dv.wait(v, h, "conv", q, k - 1)
                                ins = v.scalar_tensor_tensor(y[:, q, k % 2, :], x[:, u, q, k:k + N], taps[:, u, q, k:k + 1],
                                                             y[:, q, (k - 1) % 2, :], ALU.mult, ALU.add)
                            else:
                                ins = v.tensor_scalar(y[:, q, 0, :], x[:, u, q, 0:N], taps[:, u, q, 0:1], None, ALU.mult)
                            dv.step(ins, "conv", q, k)
                    dv.wait(v, h, "conv", 2, W - 1)
                    v.sem_inc(x_used, 1)
                    for q in range(2):
                        ac.wait(v, h, "root", q)
                        v.wait_ge(stored, h * 48 + 48)
                        dv.step(v.scalar_tensor_tensor(o[:, q, :], s[:, q, :], float(DK) ** -0.5 if q == 0 else 1.0, rn[:, q, :],
                                                       ALU.mult, ALU.mult), "out", q)
                az.wait(v, g, "y")
                v.wait_ge(f_stored, g * 16 + 16)
                for i, (a, w) in enumerate(half_pcs):
                    b = min(a + w, half)
                    second = bank[:, Y_B + i, B_AT:B_AT + w]
                    v.tensor_tensor(yf[:, a:b], ya[:, a:b], second[:, 0:b - a], ALU.add)
                    a_, b_ = max(a, 1), min(a + w, N - half + 1)
                    last = v.tensor_tensor(yf[:, N - a_:N - b_:-1], ya[:, a_:b_], second[:, a_ - a:b_ - a], ALU.subtract)
                dy.step(last, "y")

        @block.tensor
        def _(t):
            pp.begin(t)
            pz.begin(t)
            t.wait_ge(cst, 48)
            t.wait_ge(cst_seq, 32)

            def sums(h):
                for q in range(2):
                    ac.wait(t, h, "square", q)
                    if q:
                        ac.wait(t, h, "ln", 0)
                    for c, (a, w) in enumerate(pcs):
                        last = t.matmul(bank[:, S_B + c, 0:w], ones[:, :], sq[:, q, a:a + w], start=True, stop=True)
                    pp.step(last, "sum", q)

            def tokens(i):
                a, w = half_pcs[i]
                for m, at in enumerate((0, B_AT)):
                    for c in range(NCH):
                        last = t.matmul(bank[:, Y_B + i, at:at + w], z[:, c, m, :], seq[:, m, c, a:a + w],
                                        start=(c == 0), stop=(c == NCH - 1))
                return last

            with t.Fori(0, G) as g:
                t.wait_ge(f_ld, g * 16 + 16)
                az.wait_turn(t, g)
                dy.wait_turn(t, g)
                for k in range(NCH // 2):
                    if k >= 2:
                        az.wait(t, g, "z", k - 2)
                    for j in range(2):
                        c = 2 * k + j
                        last = t.matmul(bank[:R, Z_B + k % 2, j * 256:(j + 1) * 256], f[:, c * R:(c + 1) * R], chan[:, :], start=True, stop=True)
                    pz.step(last, "z", k)
                az.wait(t, g, "z", NCH // 2 - 1)
                tokens(0)
                sums(PER * g)
                tokens(1)
                pz.step(tokens(2), "y")
                sums(PER * g + 1)

        @block.scalar
        def _(a_):
            ac.begin(a_)
            az.begin(a_)
            a_.sem_inc(stored, 48)
            a_.sem_inc(f_stored, 16)
            a_.wait_ge(cst, 48)

            def root(h, q):
                pp.wait(a_, h, "sum", q)
                for c, (a, w) in enumerate(pcs):
                    last = a_.activation(rn[:, q, a:a + w], bank[:, S_B + c, 0:w], ACT.Ln, bias=eps[:, 0:1])
                ac.step(last, "ln", q)
                ac.wait(a_, h, "ln", q)
                ac.step(a_.activation(rn[:, q, :], rn[:, q, :], ACT.Exp, scale=-0.5), "root", q)

            def silu(h, q):
                dv.wait(a_, h, "conv", q, W - 1)
                if q == 2:
                    a_.wait_ge(stored, h * 48 + 48)
                ac.step(a_.activation(s[:, q, :], y[:, q, (W - 1) % 2, :], ACT.Silu), "silu", q)
                if q < 2:
                    ac.wait(a_, h, "silu", q)
                    ac.step(a_.activation(sq[:, q, :], s[:, q, :], ACT.Square), "square", q)

            def store(h, row):
                ac.wait(a_, h, "silu", 2)
                a_.dma_start(vT_d[ds(row, P), :], s[:, 2, :]).then_inc(stored, 16)
                for q, dst in ((0, qT_d), (1, kT_d)):
                    dv.wait(a_, h, "out", q)
                    a_.dma_start(dst[ds(row, P), :], o[:, q, :]).then_inc(stored, 16)

            with a_.Fori(0, G) as g:
                for k in range(NCH // 2):
                    pz.wait(a_, g, "z", k)
                    az.step(a_.activation(z[:, 2 * k:2 * k + 2, :, :].rearrange("t c m w -> t (c m w)"), bank[:R, Z_B + k % 2, :], ACT.Copy), "z", k)
                for u in range(PER):
                    h = PER * g + u
                    silu(h, 0)
                    silu(h, 1)
                    root(h, 0)
                    silu(h, 2)
                    root(h, 1)
                    if u == PER - 1:
                        pz.wait(a_, g, "y")
                        for i, (a, w) in enumerate(half_pcs):
                            last = a_.activation(ya[:, a:a + w], bank[:, Y_B + i, 0:w], ACT.Copy)
                        az.step(last, "y")
                    store(h, g * (PER * P) + u * P)
                dy.wait(a_, g, "y")
                a_.dma_start(yfT[ds(g * P, P), :], yf[:, :]).then_inc(f_stored, 16)
            a_.wait_ge(stored, HEADS * 48 + 48)
            a_.wait_ge(f_stored, G * 16 + 16)


def delta_decays(nc, p2T, alog_d, dtb_d, dirs_d, chunk_mask_d, ident_d, gc_d, egc_d, tot_d, etot_d, sc_d):
    with ExitStack() as ctx:
        st = Stage(nc, ctx, "dec")
        N = LEN
        par = st.sb("par", [HD, 2])
        dirs = st.sb("dirs", [HD, 2])
        cmask = st.sb("cmask", [HD, N])
        ident = st.sb("ident", [P, P])
        a = st.sb("a", [HD, N])
        b = st.sb("b", [HD, N])
        x = st.sb("x", [HD, N])
        ab = st.sb("ab", [HD, N])
        ea = st.sb("ea", [HD, 1])
        g = st.sb("g", [HD, N])
        pre = st.sb("pre", [HD, N])
        suf = st.sb("suf", [HD, N])
        gc = st.sb("gc", [HD, N])
        egc = st.sb("egc", [HD, N])
        tot = st.sb("tot", [HD, NCH])
        totb = st.sb("totb", [P, HD, NCH])
        etot = st.sb("etot", [P, HD, NCH])
        tok = st.sb("tok", [ROWS, HD, 5, NCH])
        tmp = st.sb("tmp", [ROWS, HD, 2, NCH])
        ps = st.ps("tr", [ROWS, 2, 512])
        ld = st.sem("loaded")
        dv = st.sem("dve_step")
        ac = st.sem("act_step")
        pe = st.sem("transposed")
        gc_half = st.sem("half_ready")
        tt = st.sem("tot_stored")
        tb = st.sem("tot_loaded")
        stored = st.sem("stored")
        block = ctx.enter_context(nc.Block())
        rows = p2T[AB_AT:GF_AT, :].rearrange("(d w h) t -> w d h t", d=2, w=2)
        by_chunk = lambda z: z[:, :].rearrange("p (c t) -> p c t", t=ROWS)

        @block.sync
        def _(sp):
            for d in range(2):
                sp.dma_start(a[8 * d:8 * d + 8, :], rows[0, d]).then_inc(ld, 16)
                sp.dma_start(b[8 * d:8 * d + 8, :], rows[1, d]).then_inc(ld, 16)
            sp.dma_start(par[:, 0:1], alog_d).then_inc(ld, 16)
            sp.dma_start(par[:, 1:2], dtb_d).then_inc(ld, 16)
            sp.dma_start(dirs[:, :], dirs_d).then_inc(ld, 16)
            sp.dma_start(cmask[:, :], chunk_mask_d.broadcast_to([HD, N])).then_inc(ld, 16)
            sp.dma_start(ident[:, :], ident_d).then_inc(ld, 16)
            sp.wait_ge(dv, 9)
            sp.dma_start(tot_d, tot[:, :]).then_inc(tt, 16)
            sp.dma_start(gc_d, gc[:, :]).then_inc(stored, 16)
            sp.wait_ge(tt, 16)
            sp.dma_start(totb[:, :, :].rearrange("p h c -> p (h c)"),
                         tot_d.rearrange("(a h) c -> a (h c)", a=1).broadcast_to([P, HD * NCH])).then_inc(tb, 16)
            sp.wait_ge(ac, 5)
            sp.dma_start(egc_d, egc[:, :]).then_inc(stored, 16)
            sp.wait_ge(ac, 8)
            sp.dma_start(etot_d.rearrange("(a h) c -> a (h c)", a=1), etot[0:1, :, :].rearrange("p h c -> p (h c)")).then_inc(stored, 16)
            sp.wait_ge(dv, 14)
            sp.dma_start(sc_d.rearrange("h t k -> t h k"), tok[:, :, :, :].rearrange("t h k c -> t h (k c)")).then_inc(stored, 16)
            sp.wait_ge(stored, 64)

        @block.vector
        def _(v):
            c = Steps(v, dv)
            v.wait_ge(ld, 16 * 9)
            c.then(v.tensor_scalar(x[:, :], a[:, :], par[:, 1:2], None, ALU.add))
            c.then(v.scalar_tensor_tensor(ab[:, :], x[:, :], -1.0, x[:, :], ALU.mult, ALU.max))
            v.wait_ge(ac, 4)
            c.then(v.scalar_tensor_tensor(x[:, :], x[:, :], 0.0, ab[:, :], ALU.max, ALU.add))
            c.then(v.tensor_scalar(g[:, :], x[:, :], ea[:, 0:1], -1.0, ALU.mult, ALU.mult))
            c.then(v.tensor_tensor_scan(pre[:, :], cmask[:, :], g[:, :], 0.0, ALU.mult, ALU.add))
            c.then(v.tensor_copy(tot[:, :], by_chunk(pre)[:, :, ROWS - 1]))
            c.then(v.tensor_tensor(suf[:, :], g[:, :], pre[:, :], ALU.subtract))
            c.then(v.tensor_tensor(by_chunk(suf), by_chunk(suf), tot[:, :].unsqueeze(2).broadcast_to([HD, NCH, ROWS]), ALU.add))
            v.tensor_scalar(gc[:, :], pre[:, :], dirs[:, 0:1], None, ALU.mult).then_inc(gc_half, 1)
            v.wait_ge(gc_half, 1)
            c.then(v.scalar_tensor_tensor(gc[:, :], suf[:, :], dirs[:, 1:2], gc[:, :], ALU.mult, ALU.add))
            v.wait_ge(pe, 2)
            tr = lambda n: ps[:, n, 0:NCH * HD].rearrange("t (c h) -> t h c", h=HD)
            c.then(v.tensor_copy(tok[:, :, 0, :], tr(0)))
            c.then(v.tensor_copy(tok[:, :, 1, :], tr(1)))
            v.wait_ge(tb, 16)
            c.then(v.tensor_tensor(tmp[:, :, 1, :], totb[0:ROWS, :, :], tok[:, :, 0, :], ALU.subtract))
            v.tensor_scalar(tok[:, :, 2, :], tok[:, :, 1, :], -1.0, None, ALU.mult).then_inc(gc_half, 1)
            v.wait_ge(gc_half, 2)
            v.wait_ge(ac, 7)
            c.then(v.tensor_tensor(tok[:, :, 3, :], tok[:, :, 2, :], tmp[:, :, 0, :], ALU.mult))
            c.then(v.tensor_copy(tok[:, :, 4, :], tmp[:, :, 1, :]))
            assert c.n == 14

        @block.scalar
        def _(s):
            c = Steps(s, ac)
            s.wait_ge(ld, 16 * 9)
            c.then(s.activation(b[:, :], b[:, :], ACT.Sigmoid))
            c.then(s.activation(ea[:, :], par[:, 0:1], ACT.Exp))
            s.wait_ge(dv, 2)
            c.then(s.activation(ab[:, :], ab[:, :], ACT.Exp, scale=-1.0))
            c.then(s.activation(ab[:, :], ab[:, :], ACT.Ln, bias=1.0))
            s.wait_ge(dv, 9)
            c.then(s.activation(egc[:, :], gc[:, :], ACT.Exp))
            s.wait_ge(dv, 12)
            c.then(s.activation(tmp[:, :, 0, :], tok[:, :, 0, :], ACT.Exp))
            c.then(s.activation(tmp[:, :, 1, :], tmp[:, :, 1, :], ACT.Exp))
            c.then(s.activation(etot[:, :, :], totb[:, :, :], ACT.Exp))

        @block.tensor
        def _(t):
            t.wait_ge(ld, 16 * 9)
            for n, (src, q) in enumerate(((gc, (dv, 9)), (b, (ac, 1)))):
                t.wait_ge(*q)
                for c in range(NCH):
                    last = t.transpose(ps[:, n, c * HD:(c + 1) * HD], src[:, c * ROWS:(c + 1) * ROWS], ident[:HD, :HD])
                last.then_inc(pe, 1)


def delta_scan(nc, p2T, qT_d, kT_d, vT_d, gc_d, egc_d, etot_d, sc_d, dmask_d, strict_d, ident_d, ones_d, gout_d, eps_d, ydT):
    ROUNDS = 6
    R = ROWS
    with ExitStack() as ctx:
        st = Stage(nc, ctx, "dlt")
        N = LEN
        pcs = pieces(N)
        NG = len(GROUPS)
        ident = st.sb("ident", [P, P])
        ones = st.sb("ones", [P, P])
        dmask = st.sb("dmask", [R, 2, R])
        strict = st.sb("strict", [R, R])
        gout = st.sb("gout", [P, 1])
        eps = st.sb("eps", [P, 2])
        kT = st.sb("kT", [P, 2, N])
        qd = st.sb("qdec", [P, 2, 2, N])
        sc = st.sb("sc", [R, 2, 2, 5, NCH])
        GCT, BETA, NBETA, NBEG, KDEC = range(5)
        et = st.sb("etot", [P, 2, 2, NCH])
        bv = st.sb("bv", [R, 2, 2, NCH, P])
        kd = st.sb("kd", [R, 2, 2, NCH, P])
        qkT = st.sb("qkT", [R, 2, 2, NCH, R])
        pp = st.sb("p", [R, 2, 2, NCH, R])
        qT = st.sb("qT", [P, N])
        vT = st.sb("vT", [P, N])
        gcr = st.sb("gcr", [R, 2, N])
        ktok = st.sb("ktok", [R, NCH, P])
        vtok = st.sb("vtok", [R, NCH, P])
        dd = st.sb("dd", [R, 2, NCH, R])
        n_ = st.sb("n", [R, 2, 2, NCH, R])
        nt = st.sb("nt", [R, 2, 2, NCH, R])
        zT = st.sb("zT", [P, N])
        S = st.sb("S", [P, 2, 2, P])
        U = st.sb("U", [R, 2, 2, P])
        rh = st.sb("rh", [R, 2, P])
        oT = st.sb("oT", [P, 2, N])
        sq = st.sb("sq", [P, N])
        rn = st.sb("rn", [P, N])
        yo = st.sb("yo", [P, N])
        bank = st.ps("bank", [P, 8, 512])
        VTOK_B, KTOK_B, KK_B, QK_B, P_B, O_B, U_B, DS_B = (3, 4, 2), (0, 1, 2), (0, 2, 4), (1, 3, 0), 4, 5, 6, 7

        cst = st.sem("consts_loaded")
        k_ld = st.sems("k_and_decays_loaded")
        v_ld = st.sem("q_and_v_loaded")
        z_ld = st.sem("z_loaded")
        stored = st.sem("y_stored")
        units = [(d, g) for g in range(NG) for d in range(2)]
        dirs = range(2)
        chunk = lambda k, d: k if d == 0 else NCH - 1 - k

        powers = [(r, *u) for r in range(1, ROUNDS + 1) for u in units]

        def powers_steps(*names):
            keys = []
            for j, w in enumerate(powers):
                keys += [(x, *w) for x in names if x == "T" or x == "N" and w[0] < ROUNDS]
                if j and "P" in names:
                    keys.append(("P", *powers[j - 1]))
            return keys + ([("P", *powers[-1])] if "P" in names else [])

        pe = Plan(st.sem("pe_prepared"), [(x, g) for x in ("vtok", "ktok") for g in range(NG)]
                  + [(x, g) for g in range(NG) for x in ("kk", "qk")]
                  + [(x, *u) for u in units for x in ("n", "qkT")]
                  + powers_steps("N", "T", "P"))
        dv = Plan(st.sem("dve_prepared"), [(x, d) for d in dirs for x in ("diff", "clamp")]
                  + [(x, *u) for g in range(NG) for x in ("nt", "qk") for u in ((0, g), (1, g))]
                  + [("qdec",)] + [("p0", *u) for u in units]
                  + powers_steps("N", "P"))
        ac = Plan(st.sem("act_prepared"), [(x, g) for x in ("vtok", "ktok") for g in range(NG)]
                  + [("exp", d) for d in dirs]
                  + [(x, *u) for u in units for x in ("n", "qkT")]
                  + powers_steps("T"))
        po = Plan(st.sem("pool_prepared"), [(x, d) for d in dirs for x in ("nbeta", "strict")]
                  + [(x, d) for d in dirs for x in ("kd", "bv")])
        pr = Plan(st.sem("pe_recurred"), [(x, k, d) for k in range(NCH) for x in ("KS", "U", "dS", "O") for d in dirs
                                          if not (x == "KS" and k == 0) and not (x == "dS" and k == NCH - 1)]
                  + [("sum", i) for i in range(len(pcs))])
        dr = Plan(st.sem("dve_recurred"), [(x, k, d) for k in range(NCH) for x in ("rhs", "S") for d in dirs
                                           if not (x == "rhs" and k == 0) and not (x == "S" and k == NCH - 1)]
                  + [("osum",), ("onorm",), ("y",)])
        ar = Plan(st.sem("act_recurred"), [(x, k, d) for k in range(NCH) for x in ("U", "O") for d in dirs]
                  + [("square",)] + [("ln", i) for i in range(len(pcs))] + [("root",), ("silu",)])
        block = ctx.enter_context(nc.Block())
        N_V, N_K = 4, 7
        PLACES = 3 * NCH + 4
        place_of = lambda *key: -(-(pe.value[key] - 1) * PLACES // pe.n) - 1

        k_loads = lambda h, s: (h - s) * (8 * N_K) + 16 * N_K

        def slot(b, g, w):
            return bank[:, b, 0:GROUPS[g][1] * w].rearrange("p (c w) -> p c w", w=w)

        def cs(g):
            return slice(GROUPS[g][0], GROUPS[g][0] + GROUPS[g][1])

        def chunks(g):
            return enumerate(range(GROUPS[g][0], GROUPS[g][0] + GROUPS[g][1]))

        def tk(c):
            return slice(c * R, (c + 1) * R)

        def heads(eng, prepare, recur):
            Beside(prepare(0, 0)).upto(PLACES)
            with eng.Fori(0, HEADS // 2 - 1) as i:
                for s in range(2):
                    beside = Beside(prepare(2 * i + s + 1, 1 - s))
                    recur(2 * i + s, s, beside.upto)
                    beside.upto(PLACES)
            beside = Beside(prepare(HEADS - 1, 1))
            recur(HEADS - 2, 0, beside.upto)
            beside.upto(PLACES)
            recur(HEADS - 1, 1, lambda place: None)

        @block.sync
        def _(sp):
            sp.sem_inc(stored, 16)
            for dst, src in ((ident[:, :], ident_d), (ones[:, :], ones_d), (dmask[:, :, :], dmask_d),
                             (strict[:, :], strict_d), (gout[:, :], gout_d), (eps[:, :], eps_d)):
                sp.dma_start(dst, src).then_inc(cst, 16)

            def load_v(h):
                dv.wait(sp, h - 1, "qdec") if not isinstance(h, int) or h else None
                sp.dma_start(vT[:, :], vT_d[ds(h * P, P), :]).then_inc(v_ld, 16)
                sp.dma_start(qT[:, :], qT_d[ds(h * P, P), :]).then_inc(v_ld, 16)
                for d in dirs:
                    sp.dma_start(gcr[:, d, :], gc_d[ds(h + d * HEADS, 1), :].broadcast_to([R, N])).then_inc(v_ld, 16)

            def load_k(h, s):
                sp.dma_start(kT[:, s, :], kT_d[ds(h * P, P), :]).then_inc(k_ld[s], 16)
                for d in dirs:
                    hd = h + d * HEADS
                    sp.dma_start(sc[:, s, d, :, :].rearrange("t k c -> t (k c)"),
                                 sc_d[ds(hd, 1), :, :].rearrange("a t k -> (a t) k")).then_inc(k_ld[s], 16)
                    sp.dma_start(qd[:, s, d, :], egc_d[ds(hd, 1), :].broadcast_to([P, N])).then_inc(k_ld[s], 16)
                    sp.dma_start(et[:, s, d, :], etot_d[ds(hd, 1), :].broadcast_to([P, NCH])).then_inc(k_ld[s], 16)

            def load_z(h):
                sp.dma_start(zT[:, :], p2T[ds(h * P + Z_AT, P), :]).then_inc(z_ld, 16)

            def store_y(h):
                dr.wait(sp, h, "y")
                sp.dma_start(ydT[ds(h * P, P), :], yo[:, :]).then_inc(stored, 16)

            load_v(0)
            load_k(0, 0)
            load_k(1, 1)
            load_z(0)
            load_v(1)
            with sp.Fori(0, HEADS // 2 - 1) as i:
                for s in range(2):
                    h = 2 * i + s
                    load_v(h + 2)
                    store_y(h)
                    load_z(h + 1)
                    load_k(h + 2, s)
            store_y(HEADS - 2)
            load_z(HEADS - 1)
            store_y(HEADS - 1)
            sp.wait_ge(stored, 16 * HEADS + 16)

        @block.tensor
        def _(t):
            pe.begin(t)
            pr.begin(t)
            t.wait_ge(cst, 96)

            def prepare(h, s):
                yield place_of("vtok", 0)
                dv.wait_turn(t, h)
                ac.wait_turn(t, h)
                for x, src, b, sem, n in (("vtok", vT[:, :], VTOK_B, v_ld, (h + 1) * (16 * N_V)),
                                          ("ktok", kT[:, s, :], KTOK_B, k_ld[s], k_loads(h, s))):
                    for g in range(NG):
                        yield place_of(x, g)
                        if g == 0:
                            t.wait_ge(sem, n)
                        if x == "ktok" and g == NG - 1:
                            ac.wait(t, h, "vtok", NG - 1)
                        for j, c in chunks(g):
                            last = t.transpose(bank[:R, b[g], j * P:(j + 1) * P], src[:, tk(c)], ident[:, :])
                        pe.step(last, x, g)
                for g in range(NG):
                    for x, src, b in (("kk", kT[:, s, :], KK_B), ("qk", qT[:, :], QK_B)):
                        yield place_of(x, g)
                        ac.wait(t, h, "ktok", NG - 1)
                        if b[g] == 0 and g:
                            dv.wait(t, h, "nt", 1, 0)
                        for j, c in chunks(g):
                            last = t.matmul(bank[:R, b[g], j * R:(j + 1) * R], src[:, tk(c)], kT[:, s, tk(c)], start=True, stop=True)
                        pe.step(last, x, g)
                for i, (d, g) in enumerate(units):
                    b = 2 * (i % 2)
                    for x, src, bb in (("n", nt[:, 0], b), ("qkT", dd, b + 1)):
                        yield place_of(x, d, g)
                        if x == "n":
                            if i < 2:
                                dv.wait(t, h, "qk", 1, NG - 1)
                            else:
                                dv.wait_all(t, h, ("p0", *units[i - 2]), ("qk", d, g))
                                ac.wait_all(t, h, ("n", *units[i - 2]), ("qkT", *units[i - 2]))
                        for j, c in chunks(g):
                            last = t.transpose(bank[:R, bb, j * R:(j + 1) * R], src[:, d, c, :], ident[:R, :R])
                        pe.step(last, x, d, g)
                def product(r, d, g):
                    yield place_of("P", r, d, g)
                    j_ = powers.index((r, d, g))
                    if j_:
                        dv.wait(t, h, "P", *powers[j_ - 1])
                    ac.wait(t, h, "T", r, d, g)
                    for j, c in chunks(g):
                        last = t.matmul(bank[:R, P_B, j * R:(j + 1) * R], nt[:, r % 2, d, c, :], pp[:, s, d, c, :], start=True, stop=True)
                    pe.step(last, "P", r, d, g)

                for i, (r, d, g) in enumerate(powers):
                    o, b = (r - 1) % 2, 2 * (i % 2)
                    yield place_of("N" if r < ROUNDS else "T", r, d, g)
                    if i == 0:
                        dv.wait(t, h, "p0", *units[-1])
                        ac.wait(t, h, "qkT", *units[-1])
                    elif i >= 2:
                        needed = [powers[i - 2]] + ([(r - 1, d, g)] if r > 1 else [])
                        dv.wait_all(t, h, *(("N", *w) for w in needed if w[0] < ROUNDS))
                        ac.wait_all(t, h, *(("T", *w) for w in needed))
                    if r < ROUNDS:
                        for j, c in chunks(g):
                            last = t.matmul(bank[:R, b, j * R:(j + 1) * R], nt[:, o, d, c, :], n_[:, o, d, c, :], start=True, stop=True)
                        pe.step(last, "N", r, d, g)
                        yield place_of("T", r, d, g)
                    for j, c in chunks(g):
                        last = t.matmul(bank[:R, b + 1, j * R:(j + 1) * R], n_[:, o, d, c, :], nt[:, o, d, c, :], start=True, stop=True)
                    pe.step(last, "T", r, d, g)
                    if i:
                        yield from product(*powers[i - 1])
                yield from product(*powers[-1])

            def recur(h, s, beside):
                dv.wait(t, h, "P", *powers[-1])
                po.wait(t, h, "bv", 1)
                ar.wait_turn(t, h)
                dr.wait_turn(t, h)
                for k in range(NCH):
                    if k:
                        dr.wait(t, h, "S", k - 1, 1)
                        for d in dirs:
                            pr.step(t.matmul(bank[:R, U_B, d * P:(d + 1) * P], kT[:, s, tk(chunk(k, d))], S[:, (k - 1) % 2, d, :],
                                             start=True, stop=True), "KS", k, d)
                    beside(3 * k)
                    if k:
                        dr.wait(t, h, "rhs", k, 1)
                    for d in dirs:
                        c = chunk(k, d)
                        pr.step(t.matmul(bank[:R, U_B, (2 + d) * P:(3 + d) * P], pp[:, s, d, c, :], rh[:, d, :] if k else bv[:, s, d, c, :],
                                         start=True, stop=True), "U", k, d)
                    beside(3 * k + 1)
                    ar.wait(t, h, "U", k, 1)
                    if k < NCH - 1:
                        for d in dirs:
                            pr.step(t.matmul(bank[:, DS_B, d * P:(d + 1) * P], kd[:, s, d, chunk(k, d), :], U[:, k % 2, d, :],
                                             start=True, stop=True), "dS", k, d)
                    for d in dirs:
                        c = chunk(k, d)
                        o = bank[:, O_B, d * P:d * P + R]
                        if k:
                            t.matmul(o, S[:, (k - 1) % 2, d, :], qd[:, s, d, tk(c)], start=True, stop=False)
                        pr.step(t.matmul(o, U[:, k % 2, d, :], qkT[:, s, d, c, :], start=(k == 0), stop=True), "O", k, d)
                    beside(3 * k + 2)
                beside(3 * NCH + 1)
                ar.wait(t, h, "square")
                for i, (a, w) in enumerate(pcs):
                    pr.step(t.matmul(bank[:, O_B + i, 0:w], ones[:, :], sq[:, a:a + w], start=True, stop=True), "sum", i)
                beside(3 * NCH + 2)

            heads(t, prepare, recur)

        @block.vector
        def _(v):
            dv.begin(v)
            dr.begin(v)
            v.wait_ge(cst, 96)

            def prepare(h, s):
                for d in dirs:
                    yield place_of("vtok", 0)
                    if d == 0:
                        v.wait_ge(v_ld, h * (16 * N_V) + 16 * N_V)
                        v.wait_ge(k_ld[s], k_loads(h, s))
                    dv.step(v.tensor_tensor(dd[:, d, :, :], sc[:, s, d, GCT, :].unsqueeze(2).broadcast_to([R, NCH, R]),
                                            gcr[:, d, :].rearrange("t (c s) -> t c s", s=R), ALU.subtract), "diff", d)
                    dv.wait(v, h, "diff", d)
                    dv.step(v.tensor_tensor(dd[:, d, :, :], dd[:, d, :, :], dmask[:, d, :].unsqueeze(1).broadcast_to([R, NCH, R]),
                                            ALU.min), "clamp", d)
                for g in range(NG):
                    for d in dirs:
                        yield place_of("kk", g)
                        po.wait(v, h, "strict", d)
                        pe.wait(v, h, "kk", g)
                        dv.step(v.tensor_tensor(nt[:, 0, d, cs(g), :], nt[:, 0, d, cs(g), :], slot(KK_B[g], g, R)[:R], ALU.mult), "nt", d, g)
                    for d in dirs:
                        yield place_of("qk", g)
                        pe.wait(v, h, "qk", g)
                        dv.step(v.tensor_tensor(dd[:, d, cs(g), :], dd[:, d, cs(g), :], slot(QK_B[g], g, R)[:R], ALU.mult), "qk", d, g)
                yield place_of("qk", NG - 1)
                for d in dirs:
                    last = v.tensor_tensor(qd[:, s, d, :], qd[:, s, d, :], qT[:, :], ALU.mult)
                dv.step(last, "qdec")
                for i, (d, g) in enumerate(units):
                    yield place_of("qkT", d, g)
                    ac.wait(v, h, "n", d, g)
                    dv.step(v.tensor_tensor(pp[:, s, d, cs(g), :], slot(2 * (i % 2), g, R)[:R],
                                            ident[:R, :R].unsqueeze(1).broadcast_to([R, GROUPS[g][1], R]), ALU.add), "p0", d, g)
                def add(r, d, g):
                    yield place_of("P", r, d, g)
                    pe.wait(v, h, "P", r, d, g)
                    dv.step(v.tensor_tensor(pp[:, s, d, cs(g), :], pp[:, s, d, cs(g), :], slot(P_B, g, R)[:R], ALU.add), "P", r, d, g)

                for i, (r, d, g) in enumerate(powers):
                    if r < ROUNDS:
                        yield place_of("N", r, d, g)
                        pe.wait(v, h, "N", r, d, g)
                        dv.step(v.tensor_copy(n_[:, r % 2, d, cs(g), :], slot(2 * (i % 2), g, R)[:R]), "N", r, d, g)
                    if i:
                        yield from add(*powers[i - 1])
                yield from add(*powers[-1])

            def recur(h, s, beside):
                for k in range(NCH):
                    for d in dirs:
                        c = chunk(k, d)
                        if k:
                            pr.wait(v, h, "KS", k, 1)
                            dr.step(v.scalar_tensor_tensor(rh[:, d, :], bank[:R, U_B, d * P:(d + 1) * P], sc[:, s, d, NBEG, c:c + 1], bv[:, s, d, c, :],
                                                           ALU.mult, ALU.add), "rhs", k, d)
                    beside(3 * k)
                    beside(3 * k + 1)
                    if k < NCH - 1:
                        for d in dirs:
                            c = chunk(k, d)
                            pr.wait(v, h, "dS", k, 1)
                            if k:
                                ins = v.scalar_tensor_tensor(S[:, k % 2, d, :], S[:, (k - 1) % 2, d, :], et[:, s, d, c:c + 1],
                                                             bank[:, DS_B, d * P:(d + 1) * P], ALU.mult, ALU.add)
                            else:
                                ins = v.tensor_copy(S[:, 0, d, :], bank[:, DS_B, d * P:(d + 1) * P])
                            dr.step(ins, "S", k, d)
                    beside(3 * k + 2)
                ar.wait(v, h, "O", NCH - 1, 1)
                dr.step(v.tensor_tensor(oT[:, 0, :], oT[:, 0, :], oT[:, 1, :], ALU.add), "osum")
                beside(3 * NCH + 2)
                ar.wait(v, h, "root")
                dr.step(v.tensor_tensor(rn[:, :], rn[:, :], oT[:, 0, :], ALU.mult), "onorm")
                dr.wait(v, h, "onorm")
                ar.wait(v, h, "silu")
                v.wait_ge(stored, h * 16 + 16)
                dr.step(v.scalar_tensor_tensor(yo[:, :], rn[:, :], gout[:, 0:1], zT[:, :], ALU.mult, ALU.mult), "y")

            heads(v, prepare, recur)

        @block.scalar
        def _(a_):
            ac.begin(a_)
            ar.begin(a_)
            a_.wait_ge(cst, 96)

            def prepare(h, s):
                for x, dst, b in (("vtok", vtok, VTOK_B), ("ktok", ktok, KTOK_B)):
                    for g in range(NG):
                        yield place_of(x, g)
                        pe.wait(a_, h, x, g)
                        if g == 0:
                            po.wait_turn(a_, h)
                        ac.step(a_.activation(dst[:, cs(g), :], slot(b[g], g, P)[:R], ACT.Copy), x, g)
                for d in dirs:
                    yield place_of("ktok", NG - 1)
                    dv.wait(a_, h, "clamp", d)
                    ac.step(a_.activation(dd[:, d, :, :], dd[:, d, :, :], ACT.Exp), "exp", d)
                for i, (d, g) in enumerate(units):
                    yield place_of("n", d, g)
                    pe.wait(a_, h, "n", d, g)
                    ac.step(a_.activation(n_[:, 0, d, cs(g), :], slot(2 * (i % 2), g, R)[:R], ACT.Copy), "n", d, g)
                    yield place_of("qkT", d, g)
                    pe.wait(a_, h, "qkT", d, g)
                    ac.step(a_.activation(qkT[:, s, d, cs(g), :], slot(2 * (i % 2) + 1, g, R)[:R], ACT.Copy), "qkT", d, g)
                for i, (r, d, g) in enumerate(powers):
                    yield place_of("T", r, d, g)
                    pe.wait(a_, h, "T", r, d, g)
                    ac.step(a_.activation(nt[:, r % 2, d, cs(g), :], slot(2 * (i % 2) + 1, g, R)[:R], ACT.Copy), "T", r, d, g)

            def recur(h, s, beside):
                for k in range(NCH):
                    beside(3 * k)
                    for d in dirs:
                        pr.wait(a_, h, "U", k, 1)
                        ar.step(a_.activation(U[:, k % 2, d, :], bank[:R, U_B, (2 + d) * P:(3 + d) * P], ACT.Copy), "U", k, d)
                    beside(3 * k + 1)
                    for d in dirs:
                        pr.wait(a_, h, "O", k, 1)
                        ar.step(a_.activation(oT[:, d, tk(chunk(k, d))], bank[:, O_B, d * P:d * P + R], ACT.Copy), "O", k, d)
                    beside(3 * k + 2)
                dr.wait(a_, h, "osum")
                ar.step(a_.activation(sq[:, :], oT[:, 0, :], ACT.Square), "square")
                beside(3 * NCH + 1)
                for i, (a, w) in enumerate(pcs):
                    pr.wait(a_, h, "sum", i)
                    ar.step(a_.activation(rn[:, a:a + w], bank[:, O_B + i, 0:w], ACT.Ln, scale=1.0 / DK, bias=eps[:, 0:1]), "ln", i)
                beside(3 * NCH + 2)
                ar.wait(a_, h, "ln", len(pcs) - 1)
                ar.step(a_.activation(rn[:, :], rn[:, :], ACT.Exp, scale=-0.5), "root")
                a_.wait_ge(z_ld, h * 16 + 16)
                ar.step(a_.activation(zT[:, :], zT[:, :], ACT.Silu), "silu")

            heads(a_, prepare, recur)

        @block.gpsimd
        def _(g_):
            po.begin(g_)
            g_.wait_ge(cst, 96)

            def prepare(h, s):
                for d in dirs:
                    ac.wait(g_, h, "exp", d)
                    po.step(g_.tensor_tensor(nt[:, 0, d, :, :], dd[:, d, :, :], sc[:, s, d, NBETA, :].unsqueeze(2).broadcast_to([R, NCH, R]),
                                             ALU.mult), "nbeta", d)
                    po.wait(g_, h, "nbeta", d)
                    po.step(g_.tensor_tensor(nt[:, 0, d, :, :], nt[:, 0, d, :, :], strict[:, :].unsqueeze(1).broadcast_to([R, NCH, R]),
                                             ALU.mult), "strict", d)
                pr.wait_turn(g_, h - 1) if not isinstance(h, int) or h else None
                for d in dirs:
                    po.step(g_.tensor_tensor(kd[:, s, d, :, :], ktok[:, :, :], sc[:, s, d, KDEC, :].unsqueeze(2).broadcast_to([R, NCH, P]),
                                             ALU.mult), "kd", d)
                    po.step(g_.tensor_tensor(bv[:, s, d, :, :], vtok[:, :, :], sc[:, s, d, BETA, :].unsqueeze(2).broadcast_to([R, NCH, P]),
                                             ALU.mult), "bv", d)

            prepare(0, 0)
            with g_.Fori(0, HEADS // 2 - 1) as i:
                for s in range(2):
                    prepare(2 * i + s + 1, 1 - s)
            prepare(HEADS - 1, 1)


def route(nc, resid2, gain_d, w_rg, b_rg, w_re, b_re, cst_d, hn_d, slot_asg, weight_d, table_d):
    with ExitStack() as ctx:
        st = Stage(nc, ctx, "rt")
        R, NT = ROWS, NCH
        half = NT // 2
        ident = st.sb("ident", [P, P])
        rms_cols = st.sb("rms_cols", [P, 2])
        gain = st.sb("gain", [P, D])
        wr = st.sb("w_router", [P, KT, N_LOG])
        bias = st.sb("bias", [P, N_LOG])
        iota = st.sb("iota", [P, N_BLK])
        steps = st.sb("block_steps", [P, MAX_BLK])
        before = st.sb("before", [P, P])
        ones = st.sb("ones", [P, P])
        asg_id = st.sb("asg_id", [R, NT, 2])
        x_in = st.sb("x_in", [P, 2, D])
        junk = st.sb("junk", [P, D])
        ssq = st.sb("ssq", [P, 2])
        ms = st.sb("ms", [P, 2])
        rstd = st.sb("rstd", [P, 2])
        hn = st.sb("hn", [P, 2, D])
        hnT = st.sb("hnT", [P, 2, KT, R])
        gl = st.sb("gl", [R, NT, N_GRP])
        el = st.sb("el", [R, NT, N_EXP])
        g1 = st.sb("g1", [R, NT, N_GRP])
        g2 = st.sb("g2", [R, NT, N_GRP])
        gsel = st.sb("gsel", [R, NT, N_GRP])
        col = st.sb("col", [R, 8, NT])
        elm = st.sb("elm", [R, NT, N_EXP])
        e1 = st.sb("e1", [R, NT, N_EXP])
        pick = st.sb("pick", [R, 2, NT, N_EXP])
        both = st.sb("both", [R, NT, N_EXP])
        base = st.sb("base", [R, NT + 1, N_EXP])
        more = st.sb("more", [R, N_EXP, MAX_BLK])
        nblk = st.sb("nblk", [R, N_EXP])
        ends = st.sb("ends", [R, N_EXP])
        first = st.sb("first", [R, N_EXP])
        wt = st.sb("wt", [R, NT, 2])
        slot_f = st.sb("slot_f", [R, NT, 2])
        slot_i = st.sb("slot_i", [R, NT, 2], I32)
        done = st.sb("done", [1, N_BLK, N_EXP])
        tab_f = st.sb("tab_f", [1, N_BLK + 1])
        tab_i = st.sb("tab_i", [1, N_BLK + 1], I32)
        bank = st.ps("bank", [P, 8, 512])

        cst = st.sem("consts_loaded")
        x_ld = st.sems("x_loaded")
        ssq_rdy = st.sem("ssq_ready")
        ms_rdy = st.sem("ms_ready")
        rstd_rdy = st.sem("rstd_ready")
        hn_rdy = st.sem("hn_ready")
        hn_st = st.sems("hn_stored")
        tr_done = st.sem("transposed")
        hnT_rdy = st.sem("hnT_ready")
        lg_done = st.sem("logits_done")
        lg_rdy = st.sem("logits_ready")
        vacant = st.sem("slots_vacant")
        dv = st.sem("dve_step")
        ac = st.sem("act_step")
        pre_done = st.sem("prefix_done")
        slots_rdy = st.sem("slots_ready")
        tab_rdy = st.sem("table_ready")
        wt_rdy = st.sem("weights_ready")
        scat = st.sem("scattered")
        stored = st.sem("stored")
        block = ctx.enter_context(nc.Block())
        row = lambda v: v.rearrange("(a d) -> a d", a=1).broadcast_to([P, v.shape[0]])
        loads = [(ident[:, :], cst_d["ident"]), (rms_cols[:, :], cst_d["rms_cols"]), (gain[:, :], row(gain_d)),
                 (wr[:, :, 0:N_GRP], w_rg.rearrange("(k p) n -> p k n", p=P)),
                 (wr[:, :, N_GRP:], w_re.rearrange("(k p) n -> p k n", p=P)),
                 (bias[:, 0:N_GRP], row(b_rg)), (bias[:, N_GRP:], row(b_re)),
                 (iota[:, :], cst_d["iota"].broadcast_to([P, N_BLK])), (steps[:, :], cst_d["block_steps"].broadcast_to([P, MAX_BLK])),
                 (before[:, :], cst_d["masks"][:, 0:P]), (ones[:, :], cst_d["ones"]), (asg_id[:, :, :], cst_d["asg_id"])]
        n_cst = 16 * len(loads)

        at = {}

        @block.sync
        def _(sp):
            for dst, src in loads:
                sp.dma_start(dst, src).then_inc(cst, 16)
            sp.dma_start(slot_asg.rearrange("(p c) a -> p (c a)", p=BT), cst_d["vacant"]).then_inc(vacant, 16)
            with sp.Fori(0, half) as i:
                for s in range(2):
                    sp.wait_ge(hn_rdy, 2 * i + s + 1)
                    sp.dma_start(x_in[:R, s, :], resid2[ds(i * (2 * R) + s * R, R), :]).then_inc(x_ld[s], 16)
            sp.wait_ge(tab_rdy, 1)
            sp.dma_start(table_d, tab_i[:, :]).then_inc(stored, 16)
            sp.wait_ge(wt_rdy, 1)
            sp.dma_start(weight_d.rearrange("(t r) j -> r t j", r=R), wt[:, :, :]).then_inc(stored, 16)
            sp.wait_ge(stored, 32)

        @block.vector
        def _(v):
            v.sem_inc(hn_rdy, 2)
            v.sem_inc(lg_rdy, 2)
            v.wait_ge(cst, n_cst)
            with v.Fori(0, half) as i:
                for s in range(2):
                    v.wait_ge(rstd_rdy, 2 * i + s + 1)
                    v.wait_ge(hn_st[s], i * 16 + 16)
                    v.wait_ge(tr_done, 2 * i + s + 1)
                    v.scalar_tensor_tensor(hn[:R, s, :], x_in[:R, s, :], rstd[:R, s:s + 1], gain[:R, :], ALU.mult, ALU.mult).then_inc(hn_rdy, 1)
                    v.wait_ge(lg_done, 2 * i + s + 1)
                    tile = lambda z: z[:, ds(2 * i + s, 1), :].rearrange("r a e -> r (a e)")
                    v.tensor_tensor(tile(gl), bank[:R, 4 + s, 0:N_GRP], bias[:R, 0:N_GRP], ALU.add)
                    v.tensor_tensor(tile(el), bank[:R, 4 + s, N_GRP:N_LOG], bias[:R, N_GRP:], ALU.add).then_inc(lg_rdy, 1)
            v.wait_ge(lg_rdy, NT + 2)
            c = Steps(v, dv)
            over = lambda x, n: x.unsqueeze(2).broadcast_to([R, NT, n])
            ids = lambda n: iota[:R, 0:n].unsqueeze(1).broadcast_to([R, NT, n])
            reduce = lambda dst, src, op: v.tensor_reduce(dst, src, AX.X, op)
            GMAX, GSUM, M1, M2, IDX, EX, DEN, PG = range(8)
            c.then(reduce(col[:, GMAX, :], gl[:, :, :], ALU.max))
            c.then(v.tensor_tensor(g2[:, :, :], gl[:, :, :], over(col[:, GMAX, :], N_GRP), ALU.is_ge))
            c.then(v.scalar_tensor_tensor(g2[:, :, :], g2[:, :, :], -256.0, ids(N_GRP), ALU.mult, ALU.add))
            c.then(reduce(col[:, IDX, :], g2[:, :, :], ALU.min))
            c.then(v.tensor_tensor(gsel[:, :, :], g2[:, :, :], over(col[:, IDX, :], N_GRP), ALU.is_equal))
            c.then(v.tensor_tensor(g1[:, :, :], gl[:, :, :], over(col[:, GMAX, :], N_GRP), ALU.subtract))
            c.then(v.tensor_scalar(g2[:, :, :], gsel[:, :, :], -1.0, 1e30, ALU.add, ALU.mult))
            by_group = lambda z: z[:, :, :].rearrange("r t (g e) -> r (t g) e", g=N_GRP)
            spread = lambda z: z[:, :, :].rearrange("r t g -> r (t g)").unsqueeze(2).broadcast_to([R, NT * N_GRP, N_EXP // N_GRP])
            c.then(v.tensor_tensor(by_group(elm), by_group(el), spread(gsel), ALU.mult))
            c.then(v.tensor_tensor(by_group(elm), by_group(elm), spread(g2), ALU.add))
            at["shifted"] = 6
            for j, m in enumerate((M1, M2)):
                c.then(reduce(col[:, m, :], elm[:, :, :], ALU.max))
                c.then(v.tensor_tensor(e1[:, :, :], elm[:, :, :], over(col[:, m, :], N_EXP), ALU.is_ge))
                c.then(v.scalar_tensor_tensor(e1[:, :, :], e1[:, :, :], -256.0, ids(N_EXP), ALU.mult, ALU.add))
                c.then(reduce(col[:, IDX, :], e1[:, :, :], ALU.min))
                c.then(v.tensor_tensor(pick[:, j, :, :], e1[:, :, :], over(col[:, IDX, :], N_EXP), ALU.is_equal))
                if j == 0:
                    c.then(v.scalar_tensor_tensor(elm[:, :, :], pick[:, 0, :, :], -3e30, elm[:, :, :], ALU.mult, ALU.add))
            c.then(v.tensor_tensor(both[:, :, :], pick[:, 0, :, :], pick[:, 1, :, :], ALU.add))
            at["picked"] = c.n
            c.then(v.tensor_tensor(col[:, EX, :], col[:, M2, :], col[:, M1, :], ALU.subtract))
            at["gap"] = c.n
            c.then(v.memset(base[:, 0, :], 0.0))
            v.wait_ge(pre_done, 1)
            for t in range(NT):
                c.then(v.tensor_tensor(base[:, t + 1, :], base[:, t, :], bank[:R, 2 + t // half, (t % half) * N_EXP:(t % half + 1) * N_EXP],
                                       ALU.add))
            c.then(v.tensor_tensor(more[:, :, :], base[:, NT, :].unsqueeze(2).broadcast_to([R, N_EXP, MAX_BLK]),
                                   steps[:R, :].unsqueeze(1).broadcast_to([R, N_EXP, MAX_BLK]), ALU.is_gt))
            c.then(reduce(nblk[:, :], more[:, :, :], ALU.add))
            c.then(v.tensor_tensor_scan(ends[:, :], ones[:R, 0:N_EXP], nblk[:, :], 0.0, ALU.mult, ALU.add))
            c.then(v.tensor_tensor(first[:, :], ends[:, :], nblk[:, :], ALU.subtract))
            for h in range(2):
                th = slice(h * half, (h + 1) * half)
                last = v.tensor_tensor(e1[:, th, :], base[:, th, :],
                                       bank[:R, h, 0:half * N_EXP].rearrange("r (t e) -> r t e", e=N_EXP), ALU.add)
            c.then(last)
            c.then(v.scalar_tensor_tensor(e1[:, :, :], first[:, :].unsqueeze(1).broadcast_to([R, NT, N_EXP]), float(BT), e1[:, :, :],
                                          ALU.mult, ALU.add))
            c.then(v.tensor_tensor(pick[:, :, :, :].rearrange("r j t e -> r j (t e)"), pick[:, :, :, :].rearrange("r j t e -> r j (t e)"),
                                   e1[:, :, :].rearrange("r t e -> r (t e)").unsqueeze(1).broadcast_to([R, 2, NT * N_EXP]), ALU.mult))
            for j in range(2):
                last = reduce(slot_f[:, :, j], pick[:, j, :, :], ALU.add)
            c.then(last)
            v.tensor_copy(slot_i[:, :, :], slot_f[:, :, :]).then_inc(slots_rdy, 1)
            c.then(v.tensor_tensor(done[:, :, :], ends[0:1, :].unsqueeze(1).broadcast_to([1, N_BLK, N_EXP]),
                                   iota[0:1, :].unsqueeze(2).broadcast_to([1, N_BLK, N_EXP]), ALU.is_le))
            c.then(v.tensor_reduce(tab_f[:, 0:N_BLK], done[:, :, :], AX.X, ALU.add))
            c.then(v.tensor_scalar(tab_f[:, 0:N_BLK], tab_f[:, 0:N_BLK], float(N_EXP - 1), None, ALU.min))
            c.then(v.tensor_scalar(done[:, :, 0], iota[0:1, :], ends[0:1, N_EXP - 1:N_EXP], None, ALU.is_lt))
            c.then(v.tensor_reduce(tab_f[:, N_BLK:], done[:, 0:N_BLK:2, 0], AX.X, ALU.add))
            v.tensor_copy(tab_i[:, :], tab_f[:, :]).then_inc(tab_rdy, 1)
            v.wait_ge(ac, 2)
            c.then(reduce(col[:, GSUM, :], g1[:, :, :], ALU.add))
            c.then(v.reciprocal(col[:, PG, :], col[:, GSUM, :]))
            c.then(v.tensor_scalar(col[:, DEN, :], col[:, EX, :], 1.0, None, ALU.add))
            c.then(v.reciprocal(col[:, DEN, :], col[:, DEN, :]))
            c.then(v.tensor_tensor(wt[:, :, 0], col[:, DEN, :], col[:, PG, :], ALU.mult))
            v.tensor_tensor(wt[:, :, 1], wt[:, :, 0], col[:, EX, :], ALU.mult).then_inc(wt_rdy, 1)

        @block.scalar
        def _(a):
            a.sem_inc(hnT_rdy, 2)
            for q in hn_st:
                a.sem_inc(q, 16)
            with a.Fori(0, half) as i:
                for s in range(2):
                    a.wait_ge(x_ld[s], i * 16 + 16)
                    a.activation(junk[:R, :], x_in[:R, s, :], ACT.Square, scale=D ** -0.5, accum_out=ssq[:R, s:s + 1]).then_inc(ssq_rdy, 1)
                    a.wait_ge(hn_rdy, 2 * i + s + 3)
                    a.dma_start(hn_d[ds(i * (2 * R) + s * R, R), :], hn[:R, s, :]).then_inc(hn_st[s], 16)
                    a.wait_ge(tr_done, 2 * i + s + 3)
                    for b in range(2):
                        last = a.activation(hnT[:, s, 4 * b:4 * b + 4, :].rearrange("p k r -> p (k r)"),
                                            bank[:, 2 * s + b, 0:4 * R], ACT.Copy)
                    last.then_inc(hnT_rdy, 1)
            c = Steps(a, ac)
            a.wait_ge(dv, at["shifted"])
            c.then(a.activation(g1[:, :, :], g1[:, :, :], ACT.Exp))
            a.wait_ge(dv, at["gap"])
            c.then(a.activation(col[:, 5, :], col[:, 5, :], ACT.Exp))
            for q in hn_st:
                a.wait_ge(q, 16 * (half + 1))

        @block.tensor
        def _(t):
            t.sem_inc(tr_done, 2)
            t.wait_ge(cst, n_cst)
            with t.Fori(0, half) as i:
                for s in range(2):
                    t.wait_ge(hn_rdy, 2 * i + s + 3)
                    t.wait_ge(hnT_rdy, 2 * i + s + 1)
                    for k in range(KT):
                        last = t.transpose(bank[:, 2 * s + k // 4, (k % 4) * R:(k % 4 + 1) * R], hn[:R, s, k * P:(k + 1) * P], ident[:R, :R])
                    last.then_inc(tr_done, 1)
                    t.wait_ge(hnT_rdy, 2 * i + s + 3)
                    t.wait_ge(lg_rdy, 2 * i + s + 1)
                    for k in range(KT):
                        last = t.matmul(bank[:R, 4 + s, 0:N_LOG], hnT[:, s, k, :], wr[:, k, :], start=(k == 0), stop=(k == KT - 1))
                    last.then_inc(lg_done, 1)
            t.wait_ge(dv, at["picked"])
            t.wait_ge(lg_rdy, NT + 2)
            for n, m in enumerate((before, ones)):
                for h in range(2):
                    last = t.matmul(bank[:R, 2 * n + h, 0:half * N_EXP], m[:R, :R],
                                    both[:, h * half:(h + 1) * half, :].rearrange("r t e -> r (t e)"), start=True, stop=True)
            last.then_inc(pre_done, 1)

        @block.gpsimd
        def _(g):
            g.wait_ge(cst, n_cst)
            with g.Fori(0, half) as i:
                for s in range(2):
                    g.wait_ge(ssq_rdy, 2 * i + s + 1)
                    g.tensor_tensor(ms[:R, s:s + 1], ssq[:R, s:s + 1], rms_cols[:R, 0:1], ALU.add).then_inc(ms_rdy, 1)
                    g.wait_ge(ms_rdy, 2 * i + s + 1)
                    g.tensor_tensor(rstd[:R, s:s + 1], ms[:R, s:s + 1], rms_cols[:R, 1:2], ALU.pow).then_inc(rstd_rdy, 1)
            g.wait_ge(slots_rdy, 1)
            g.wait_ge(vacant, 16)
            for t in range(NT):
                for j in range(2):
                    g.indirect_dma_start(out=slot_asg, out_offset=bass.IndirectOffsetOnAxis(ap=slot_i[:, t, j:j + 1], axis=0),
                                         in_=asg_id[:, t, j:j + 1], in_offset=None).then_inc(scat, 16)
            g.wait_ge(scat, 16 * 2 * NT)


def expert_blocks(nc, hn_d, slot_asg, table_d, wg_d, wu_d, wd_d, ident_d, y_d):
    with ExitStack() as ctx:
        st = Stage(nc, ctx, "ex")
        PAIRS = N_BLK // 2
        M = D_EXP // P
        WS = 3
        ident = st.sb("ident", [P, P])
        table = st.sb("table", [1, N_BLK + 1], I32)
        slots = st.sb("slots", [N_BLK, BT])
        asg = st.sb("asg", [BT, N_BLK + 4], I32)
        tok = st.sb("tok", [BT, N_BLK + 4], I32)
        to_gather = st.sb("to_gather", [BT, 2], I32)
        to_scatter = st.sb("to_scatter", [BT, 2], I32)
        x = st.sb("x", [BT, 2, D])
        xT = st.sb("xT", [P, 2, KT, BT])
        wg = st.sb("w_gate", [P, WS, KT, D_EXP])
        wu = st.sb("w_up", [P, WS, KT, D_EXP])
        wd = st.sb("w_down", [P, WS, M, D])
        sg = st.sb("silu_g", [P, 2, M, BT])
        hT = st.sb("hT", [P, 2, M, BT])
        y = st.sb("y", [BT, 2, D])
        bank = st.ps("bank", [P, 8, 512])

        cst = st.sem("consts_loaded")
        idx_tr = st.sem("idx_transposed")
        idx_rdy = st.sem("idx_ready")
        gather_set = st.sem("gather_index_set")
        scatter_set = st.sem("scatter_index_set")
        asg_rdy = st.sem("asg_ready")
        y_free = st.sem("y_free")
        x_ld = st.sems("x_gathered")
        w_ld = st.sems("w_loaded", WS)
        d_ld = st.sems("w_down_loaded", WS)
        tr_done = st.sem("transposed")
        xT_rdy = st.sem("xT_ready")
        gu_done = st.sem("gate_up_done")
        pool_turn = st.sem("pool_turn")
        zero_rdy = st.sem("x_zeroed")
        sg_rdy = st.sem("silu_ready")
        h_rdy = st.sem("hidden_ready")
        y_done = st.sem("y_done")
        y0_rdy = st.sem("y_first_half_ready")
        y1_rdy = st.sem("y_second_half_ready")
        stored = st.sems("y_stored")
        block = ctx.enter_context(nc.Block())

        def in_use(eng, i, b):
            return eng.If(i * (TURN // 2) + b // 2 < pairs[eng])

        def done(i, b, before=0):
            return i * TURN + (b + 1 + before)

        def loads(i, b, slots=2, n=1):
            return i * (16 * n * (TURN // slots)) + 16 * n * (b // slots + 1)

        pairs = {}

        def load_pairs(eng):
            eng.wait_ge(cst, 48)
            pairs[eng] = eng.value_load(table[0:1, N_BLK:N_BLK + 1], min_val=1, max_val=PAIRS)

        @block.sync
        def _(sp):
            sp.dma_start(ident[:, :], ident_d).then_inc(cst, 16)
            sp.dma_start(table[:, :], table_d).then_inc(cst, 16)
            sp.dma_start(slots[:, :], slot_asg.rearrange("(b p) a -> b (p a)", p=BT)).then_inc(cst, 16)
            load_pairs(sp)

            def load_weights(i, b):
                ws = b % WS
                e = sp.value_load(table[0:1, ds(i * TURN + b, 1)], min_val=0, max_val=N_EXP - 1)
                sp.wait_ge(gu_done, done(i, b))
                sp.dma_start(wg[:, ws, :, :].rearrange("p k f -> p (k f)"),
                             wg_d[ds(e, 1), :, :].rearrange("a (p k) f -> (a p) (k f)", k=KT)).then_inc(w_ld[ws], 16)
                sp.dma_start(wu[:, ws, :, :].rearrange("p k f -> p (k f)"),
                             wu_d[ds(e, 1), :, :].rearrange("a (p k) f -> (a p) (k f)", k=KT)).then_inc(w_ld[ws], 16)
                sp.wait_ge(y_done, done(i, b))
                sp.dma_start(wd[:, ws, :, :].rearrange("p m d -> p (m d)"),
                             wd_d[ds(e, 1), :, :].rearrange("a (p m) d -> (a p) (m d)", m=M)).then_inc(d_ld[ws], 16)

            with sp.Fori(0, N_BLK // TURN) as i:
                for p in range(0, TURN, 2):
                    with in_use(sp, i, p):
                        load_weights(i, p)
                        load_weights(i, p + 1)

        @block.gpsimd
        def _(g):
            g.sem_inc(y_free, 2)
            load_pairs(g)
            g.wait_ge(idx_rdy, 1)
            g.wait_ge(zero_rdy, 1)

            def gather(i, b):
                s = b % 2
                g.wait_ge(tr_done, done(i, b))
                g.tensor_copy(to_gather[:, s:s + 1], tok[:, ds(i * TURN + b, 1)]).then_inc(gather_set, 1)
                g.wait_ge(gather_set, done(i, b))
                g.sem_inc(pool_turn, 1)
                g.indirect_dma_start(out=x[:, s, :], out_offset=None, in_=hn_d,
                                     in_offset=bass.IndirectOffsetOnAxis(ap=to_gather[:, s:s + 1], axis=0),
                                     bounds_check=LEN - 1, oob_is_err=False).then_inc(x_ld[s], 16)

            def scatter(i, b):
                s = b % 2
                g.tensor_copy(to_scatter[:, s:s + 1], asg[:, ds(i * TURN + b, 1)]).then_inc(scatter_set, 1)
                g.wait_ge(y0_rdy, done(i, b, 2))
                g.wait_ge(y1_rdy, done(i, b, 2))
                g.wait_ge(scatter_set, done(i, b))
                g.sem_inc(pool_turn, 1)
                g.indirect_dma_start(out=y_d, out_offset=bass.IndirectOffsetOnAxis(ap=to_scatter[:, s:s + 1], axis=0),
                                     in_=y[:, s, :], in_offset=None,
                                     bounds_check=2 * LEN - 1, oob_is_err=False).then_inc(stored[s], 16)

            def free_y(i, b):
                g.wait_ge(stored[b % 2], loads(i, b))
                g.sem_inc(y_free, 1)

            for b in range(4):
                gather(0, b)
            with g.Fori(0, N_BLK // TURN) as i:
                for p in range(0, TURN, 2):
                    with in_use(g, i, p):
                        for b in (p, p + 1):
                            gather(i, b + 4)
                            scatter(i, b)
                        for b in (p, p + 1):
                            free_y(i, b)
            for q in x_ld:
                g.wait_ge(q, 16 * pairs[g] + 32)

        @block.tensor
        def _(t):
            t.sem_inc(tr_done, 2)
            t.sem_inc(gu_done, WS)
            t.sem_inc(y_done, WS)
            load_pairs(t)
            t.transpose(bank[:BT, 6, 0:N_BLK], slots[:, :], ident[:N_BLK, :N_BLK]).then_inc(idx_tr, 1)
            t.wait_ge(idx_rdy, 1)

            def transpose_x(i, b):
                s = b % 2
                t.wait_ge(x_ld[s], loads(i, b))
                t.wait_ge(xT_rdy, done(i, b))
                for k in range(KT):
                    last = t.transpose(bank[:, 2 * s + k // 4, (k % 4) * BT:(k % 4 + 1) * BT], x[:, s, k::KT], ident[:BT, :BT])
                last.then_inc(tr_done, 1)

            def gate_up(i, b):
                s, ws = b % 2, b % WS
                t.wait_ge(xT_rdy, done(i, b, 2))
                t.wait_ge(w_ld[ws], loads(i, b, WS, 2))
                t.wait_ge(h_rdy, done(i, b))
                for n, w in enumerate((wg, wu)):
                    for m in range(M):
                        for k in range(KT):
                            last = t.matmul(bank[:, 4 + s, (n * M + m) * BT:(n * M + m + 1) * BT], w[:, ws, k, m::M], xT[:, s, k, :],
                                            start=(k == 0), stop=(k == KT - 1))
                last.then_inc(gu_done, 1)

            def down(i, b):
                s, ws = b % 2, b % WS
                t.wait_ge(h_rdy, done(i, b, 2))
                t.wait_ge(d_ld[ws], loads(i, b, WS))
                t.wait_ge(y0_rdy, done(i, b, 1))
                t.wait_ge(y1_rdy, done(i, b, 1))
                for c in range(2):
                    for m in range(M):
                        last = t.matmul(bank[:BT, 6 + c, :], hT[:, s, m, :], wd[:, ws, m, c * 512:(c + 1) * 512],
                                        start=(m == 0), stop=(m == M - 1))
                last.then_inc(y_done, 1)

            transpose_x(0, 0)
            transpose_x(0, 1)
            with t.Fori(0, N_BLK // TURN) as i:
                for p in range(0, TURN, 2):
                    with in_use(t, i, p):
                        for b in (p, p + 1):
                            gate_up(i, b)
                        for b in (p, p + 1):
                            transpose_x(i, b + 2)
                            down(i, b)

        @block.scalar
        def _(a):
            a.sem_inc(y0_rdy, 2)
            load_pairs(a)
            with a.Fori(0, N_BLK // TURN) as i:
                for p in range(0, TURN, 2):
                    with in_use(a, i, p):
                        for b in (p, p + 1):
                            s = b % 2
                            a.wait_ge(gu_done, done(i, b, WS))
                            a.wait_ge(h_rdy, done(i, b))
                            a.activation(sg[:, s, :, :].rearrange("p m t -> p (m t)"), bank[:, 4 + s, 0:M * BT], ACT.Silu).then_inc(sg_rdy, 1)
                        for b in (p, p + 1):
                            s = b % 2
                            a.wait_ge(y_done, done(i, b, WS))
                            a.wait_ge(y_free, done(i, b))
                            a.activation(y[:, s, 0:512], bank[:BT, 6, :], ACT.Copy).then_inc(y0_rdy, 1)

        @block.vector
        def _(v):
            v.sem_inc(xT_rdy, 2)
            v.sem_inc(h_rdy, 2)
            v.sem_inc(y1_rdy, 2)
            v.memset(x[:, :, :], 0.0).then_inc(zero_rdy, 1)
            v.memset(asg[:, N_BLK:], VACANT)
            v.wait_ge(idx_tr, 1)
            v.tensor_copy(asg[:, 0:N_BLK], bank[:BT, 6, 0:N_BLK]).then_inc(asg_rdy, 1)
            v.wait_ge(asg_rdy, 1)
            v.tensor_scalar(tok[:, :], asg[:, :], 1, None, ALU.arith_shift_right).then_inc(idx_rdy, 1)
            load_pairs(v)

            def take_x(i, b):
                s = b % 2
                v.wait_ge(tr_done, done(i, b, 2))
                v.wait_ge(gu_done, done(i, b, WS - 2))
                for b in range(2):
                    last = v.tensor_copy(xT[:, s, 4 * b:4 * b + 4, :].rearrange("p k t -> p (k t)"), bank[:, 2 * s + b, 0:4 * BT])
                last.then_inc(xT_rdy, 1)

            def take_h(i, b):
                s = b % 2
                v.wait_ge(sg_rdy, done(i, b))
                v.wait_ge(y_done, done(i, b, WS - 2))
                v.tensor_tensor(hT[:, s, :, :].rearrange("p m t -> p (m t)"), sg[:, s, :, :].rearrange("p m t -> p (m t)"),
                                bank[:, 4 + s, M * BT:2 * M * BT], ALU.mult).then_inc(h_rdy, 1)

            def take_y(i, b):
                s = b % 2
                v.wait_ge(y_done, done(i, b, WS))
                v.wait_ge(y_free, done(i, b))
                v.tensor_copy(y[:, s, 512:], bank[:BT, 7, :]).then_inc(y1_rdy, 1)

            take_x(0, 0)
            take_x(0, 1)
            with v.Fori(0, N_BLK // TURN) as i:
                for p in range(0, TURN, 2):
                    with in_use(v, i, p):
                        for b in (p, p + 1):
                            take_h(i, b)
                        for b in (p, p + 1):
                            take_x(i, b + 2)
                            take_y(i, b)


def combine(nc, resid2, y_d, weight_d, gain_d, neghalf_d, out):
    with ExitStack() as ctx:
        st = Stage(nc, ctx, "out")
        NT = SEQ // P
        gain = st.sb("gain", [P, D])
        neghalf = st.sb("neghalf", [P, 1])
        res = st.sb("res", [P, 2, D])
        wt = st.sb("wt", [P, 2, 2])
        y = st.sb("y", [P, 2, 2, D])
        acc = st.sb("acc", [P, 2, 2, D])
        junk = st.sb("junk", [P, 2, D])
        ssq = st.sb("ssq", [P, 2])
        ms = st.sb("ms", [P, 2])
        rstd = st.sb("rstd", [P, 2])
        o = st.sb("o", [P, 2, D])
        cst = st.sem("consts_loaded")
        ld = st.sems("loaded")
        half = st.sem("first_added")
        acc_rdy = st.sem("sum_ready")
        ssq_rdy = st.sem("ssq_ready")
        ms_rdy = st.sem("ms_ready")
        rstd_rdy = st.sem("rstd_ready")
        o_rdy = st.sem("out_ready")
        stored = st.sems("stored")
        block = ctx.enter_context(nc.Block())

        @block.sync
        def _(sp):
            sp.dma_start(gain[:, :], gain_d.rearrange("(a d) -> a d", a=1).broadcast_to([P, D])).then_inc(cst, 16)
            sp.dma_start(neghalf[:, :], neghalf_d).then_inc(cst, 16)
            with sp.Fori(0, NT // 2) as i:
                for s in range(2):
                    sp.wait_ge(acc_rdy, 2 * i + s + 1)
                    rows = ds(i * (2 * P) + (N_META + s * P), P)
                    sp.dma_start(y[:, s, :, :].rearrange("p j d -> p (j d)"), y_d.rearrange("(t j) d -> t (j d)", j=2)[rows, :]).then_inc(ld[s], 16)
                    sp.dma_start(wt[:, s, :], weight_d[rows, :]).then_inc(ld[s], 16)
                    sp.dma_start(res[:, s, :], resid2[rows, :]).then_inc(ld[s], 16)

        @block.gpsimd
        def _(g):
            g.wait_ge(cst, 32)
            with g.Fori(0, NT // 2) as i:
                for s in range(2):
                    g.wait_ge(ms_rdy, 2 * i + s + 1)
                    g.tensor_tensor(rstd[:, s:s + 1], ms[:, s:s + 1], neghalf[:, :], ALU.pow).then_inc(rstd_rdy, 1)

        @block.vector
        def _(v):
            v.sem_inc(acc_rdy, 2)
            v.wait_ge(cst, 32)
            with v.Fori(0, NT // 2) as i:
                for s in range(2):
                    v.wait_ge(ld[s], i * 48 + 48)
                    v.scalar_tensor_tensor(acc[:, s, 0, :], y[:, s, 0, :], wt[:, s, 0:1], res[:, s, :], ALU.mult, ALU.add).then_inc(half, 1)
                    v.wait_ge(half, 2 * i + s + 1)
                    v.scalar_tensor_tensor(acc[:, s, 1, :], y[:, s, 1, :], wt[:, s, 1:2], acc[:, s, 0, :], ALU.mult, ALU.add).then_inc(acc_rdy, 1)
                for s in range(2):
                    v.wait_ge(ssq_rdy, 2 * i + s + 1)
                    v.tensor_scalar(ms[:, s:s + 1], ssq[:, s:s + 1], 1.0 / D, EPS, ALU.mult, ALU.add).then_inc(ms_rdy, 1)
                for s in range(2):
                    v.wait_ge(rstd_rdy, 2 * i + s + 1)
                    v.wait_ge(stored[s], i * 16 + 16)
                    v.scalar_tensor_tensor(o[:, s, :], acc[:, s, 1, :], rstd[:, s:s + 1], gain[:, :], ALU.mult, ALU.mult).then_inc(o_rdy, 1)

        @block.scalar
        def _(a):
            for q in stored:
                a.sem_inc(q, 16)
            with a.Fori(0, NT // 2) as i:
                for s in range(2):
                    a.wait_ge(acc_rdy, 2 * i + s + 3)
                    a.activation(junk[:, s, :], acc[:, s, 1, :], ACT.Square, accum_out=ssq[:, s:s + 1]).then_inc(ssq_rdy, 1)
                for s in range(2):
                    a.wait_ge(o_rdy, 2 * i + s + 1)
                    a.dma_start(out[ds(i * (2 * P) + s * P, P), :], o[:, s, :]).then_inc(stored[s], 16)
            for q in stored:
                a.wait_ge(q, 16 * (NT // 2 + 1))




def constants():
    t = np.arange(P)
    one = np.ones((P, P))
    same = np.kron(np.eye(2), np.ones((64, 64)))
    up_strict, up, low_strict = (t[:, None] < t[None, :]), (t[:, None] <= t[None, :]), (t[:, None] > t[None, :])
    cnt = np.minimum(np.arange(1, SEQ + 1)[None, :], np.array(POOL_WINDOWS)[:, None])
    r, s = np.arange(ROWS)[:, None], np.arange(ROWS)[None, :]
    ang_c = 2 * np.pi * (np.outer(t, t) % P) / P
    u = np.arange(LEN)
    ang_s = 2 * np.pi * (np.outer(u, u) % LEN) / LEN
    c = {
        "ident": np.eye(P),
        "rms_cols": np.stack([np.full(P, EPS), np.full(P, -0.5)], axis=1),
        "neghalf": np.full((P, 1), -0.5),
        "blockones": same,
        "blockmean": same / 64,
        "chunk_mask": (np.arange(SEQ) % RC != 0)[None, :],
        "masks": np.concatenate([up_strict, up, up_strict, up, low_strict], axis=1),
        "inv_cnt": 1.0 / cnt,
        "ones": one,
        "chunk_mask2": (np.arange(LEN) % ROWS != 0)[None, :],
        "dirs": np.arange(HD)[:, None] // HEADS == np.arange(2)[None, :],
        "dmask": np.where(np.stack([s <= r, s >= r], axis=1), 3e38, -1e4),
        "strict": s != r,
        "chan": np.concatenate([np.cos(ang_c), -np.sin(ang_c)], axis=1),
        "iota": np.arange(N_BLK)[None, :],
        "block_steps": BT * np.arange(MAX_BLK)[None, :],
        "asg_id": np.arange(2 * LEN).reshape(NCH, ROWS, 2).transpose(1, 0, 2),
        "vacant": VACANT + 2 * np.arange(N_SLOT).reshape(BT, N_BLK),
        "seq": np.stack([np.cos(ang_s), np.sin(ang_s)])[:, :, :HALF_W] / np.sqrt(LEN * P),
    }
    return {k: np.ascontiguousarray(v, dtype=np.float32) for k, v in c.items()}


def columns(v):
    return np.ascontiguousarray(v.reshape(-1, P).T)


def laid_out(a):
    mu = a["mu_shift"][0]
    per_channel = [a[k][0].reshape(-1) for k in ("rwkv_w0", "rwkv_a0", "rwkv_k_k", "rwkv_k_a", "rwkv_r_k")]
    return {
        "pre_norm_cols": columns(a["pre_norm_w"][0]),
        "conv_taps_cols": np.ascontiguousarray(a["conv_w"][0].T),
        "pool_scale_cols": columns(a["pool_scale"][0]),
        "gn_w_cols": columns(a["rwkv_gn_w"][0]),
        "gn_b_cols": columns(a["rwkv_gn_b"][0]),
        "rwkv_columns": np.ascontiguousarray(np.stack(per_channel + list(mu[:4 * C_BR].reshape(4, C_BR)), axis=1)),
        "norm1_cols": columns(a["norm1_g_2"][0]),
        "conv2_taps_cols": np.ascontiguousarray(a["conv_w_2"][0].T),
        "a_log_cols": np.concatenate([a["a_log_fwd_2"][0], a["a_log_bwd_2"][0]]).reshape(HD, 1),
        "dt_bias_cols": np.concatenate([a["dt_bias_fwd_2"][0], a["dt_bias_bwd_2"][0]]).reshape(HD, 1),
        "out_norm_cols": columns(a["out_norm_g_2"][0]),
        "mu_lora": np.ascontiguousarray(mu[4 * C_BR:].reshape(P, 1)),
    }


def build(nc, t, c, out):
    def scratch(name, shape, dt=F32):
        return nc.dram_tensor(f"scr_{name}", shape, dt, kind="Internal").ap()

    x = t["x"][0]
    pT = scratch("pT", [N_IN, SEQ])
    ybT = scratch("ybT", [C_BR, SEQ])
    ycT = scratch("ycT", [C_BR, SEQ])
    yaT = scratch("yaT", [C_BR, SEQ])
    ar_d = scratch("ar", [C_BR, RCH, 2 * RC])
    bk_d = scratch("bk", [C_BR, RCH, 2 * RC])
    v_d = scratch("v", [C_BR, SEQ])
    wc_d = scratch("wc", [C_BR, RCH])
    bonus_d = scratch("bonus", [C_BR, SEQ])
    sz_d = scratch("sz", [C_BR, SEQ])
    yT_d = scratch("yT", [C_BR, SEQ])
    resid = scratch("resid", [LEN, D])

    with ExitStack() as kept_ctx:
        kept = [kept_ctx.enter_context(nc.sbuf_tensor(f"in1_{n}_sb", [P, KT, SEQ], F32R)) for n in ("h_hi", "h_lo")]
        w_in = t["w_in"][0]

        def project(column, end):
            return kept, SEQ, w_in, pT, column, (end - column) // (CT * P)

        norm_project(nc, "in1", x, SEQ, P, t["pre_norm_cols"], w_in, 2 * CT, (4 * C_BR, P), (N_RWKV_IN, 0), pT,
                     c["ident"], c["rms_cols"], kept)
        prm = (t["rwkv_columns"], t["mu_lora"], t["rwkv_w_up"][0], t["rwkv_a_up"][0])
        rwkv_prepare(nc, pT, prm, c["blockones"], c["chunk_mask"], ar_d, bk_d, v_d, wc_d, bonus_d, sz_d, project(CONV_AT, GATE_AT))
        gates_at = GATE_AT + 2 * CT * P
        conv_branch(nc, pT, t["conv_taps_cols"], ybT, project(GATE_AT, gates_at))
        rwkv_scan(nc, ar_d, bk_d, v_d, wc_d, c["ident"], c["masks"], yT_d)
        rwkv_finish(nc, yT_d, bonus_d, sz_d, t["gn_w_cols"], t["gn_b_cols"], c["blockmean"], yaT, project(gates_at, N_IN))
    pool_branch(nc, pT, t["pool_w"][0], t["pool_scale_cols"], c["inv_cnt"], ycT)
    gates = [pT[GATE_AT + n * D:GATE_AT + (n + 1) * D, :] for n in range(3)]
    wb = t["w_branch"][0]
    gate_merge_out(nc, "mix1", SEQ, P, [(wb[n], y) for n, y in enumerate((yaT, ybT, ycT))], gates,
                   t["w_out"][0], t["post_norm_w"][0], x, resid[N_META:, :], c["neghalf"],
                   copy=(resid[0:N_META, :], t["meta_tokens_2"]))

    p2T = scratch("p2T", [IN2, LEN])
    qT_d, kT_d, vT_d, ydT = (scratch(n, [HEADS * DK, LEN]) for n in ("qT", "kT", "vT", "ydT"))
    yfT = scratch("yfT", [F_W, LEN])
    gc_d = scratch("gc", [HD, LEN])
    egc_d = scratch("egc", [HD, LEN])
    tot_d = scratch("tot", [HD, NCH])
    etot_d = scratch("etot", [HD, NCH])
    sc_d = scratch("sc", [HD, ROWS, 5 * NCH])
    resid2 = scratch("resid2", [LEN, D])
    norm_project(nc, "in2", resid, LEN, ROWS, t["norm1_cols"], t["w_in_2"][0], AB_AT // (2 * P), (AB_AT, 4 * HEADS),
                 (GF_AT, D // P), p2T, c["ident"], c["rms_cols"])
    qkv_and_fourier(nc, p2T, t["conv2_taps_cols"], c["ones"], c["rms_cols"], qT_d, kT_d, vT_d, c["chan"], c["seq"], yfT)
    delta_decays(nc, p2T, t["a_log_cols"], t["dt_bias_cols"], c["dirs"], c["chunk_mask2"], c["ident"],
                 gc_d, egc_d, tot_d, etot_d, sc_d)
    delta_scan(nc, p2T, qT_d, kT_d, vT_d, gc_d, egc_d, etot_d, sc_d, c["dmask"], c["strict"], c["ident"], c["ones"],
               t["out_norm_cols"], c["rms_cols"], ydT)
    gate_merge_out(nc, "mix2", LEN, ROWS, [(t["w_fourier_2"][0], yfT), (t["w_delta_2"][0], ydT)],
                   [p2T[GF_AT:GF_AT + D, :], p2T[GF_AT + D:, :]], t["w_out_2"][0], None, resid, resid2, c["neghalf"])

    hn_d = scratch("hn", [LEN, D])
    slot_asg = scratch("slot_asg", [N_SLOT, 1])
    weight_d = scratch("weight", [LEN, 2])
    table_d = scratch("table", [1, N_BLK + 1], I32)
    y_d = scratch("y", [2 * LEN, D])
    route(nc, resid2, t["norm2_g_2"][0], t["w_router_group_2"][0], t["b_router_group_2"][0], t["w_router_expert_2"][0],
          t["b_router_expert_2"][0], c, hn_d, slot_asg, weight_d, table_d)
    expert_blocks(nc, hn_d, slot_asg, table_d, t["w_gate_e_2"][0], t["w_up_e_2"][0], t["w_down_e_2"][0], c["ident"], y_d)
    combine(nc, resid2, y_d, weight_d, t["final_norm_g_2"], c["neghalf"], out)


def kernel(**inputs):
    import concourse.bacc as bacc
    from concourse.bass_utils import run_bass_kernel_spmd

    nc = bacc.Bacc("TRN2", target_bir_lowering=False, num_devices=1)
    given = {k: np.ascontiguousarray(v) for k, v in inputs.items()}
    arrays, t, c = {}, {}, {}
    for aps, prefix, values in ((t, "in_", {**given, **laid_out(given)}), (c, "const_", constants())):
        for name, a in values.items():
            if a.size:
                arrays[prefix + name] = a
                aps[name] = nc.dram_tensor(prefix + name, a.shape, mybir.dt.from_np(a.dtype), kind="ExternalInput").ap()
    out = nc.dram_tensor("out", (1, SEQ, D), F32, kind="ExternalOutput").ap()
    build(nc, t, c, out[0])
    r = run_bass_kernel_spmd(nc, [arrays], core_ids=[0])
    return r.results[0]["out"]
```
